# Optimizing a Trainium2 kernel written in Bass

```python
import jax, jax.numpy as jnp
from jax import lax
import numpy as np
import math

D_MODEL = 1024
BATCH = 1
SEQ = 512
DEPTH = 1

D_INNER = 2 * D_MODEL
SSD_HEAD_DIM = 64
SSD_HEADS = D_INNER // SSD_HEAD_DIM
SSD_GROUPS = 4
SSD_HEADS_PER_GROUP = SSD_HEADS // SSD_GROUPS
SSD_STATE = 128
CONV_WIDTH = 4
CHUNK = 128
XBC_WIDTH = D_INNER + 2 * SSD_GROUPS * SSD_STATE
DT_MIN = 0.001
DT_MAX = 0.1
POOL_WINDOWS = (2, 4, 8, 16)
POOL_GROUPS = len(POOL_WINDOWS)
POOL_WIDTH = D_MODEL
POOL_GROUP_WIDTH = POOL_WIDTH // POOL_GROUPS
N_BRANCHES = 2
D_FF = 4 * D_MODEL
N_MOD = 6
NORM_EPS = 1e-5
IN_SPLITS = (D_INNER,
             D_INNER + XBC_WIDTH,
             D_INNER + XBC_WIDTH + SSD_HEADS,
             D_INNER + XBC_WIDTH + SSD_HEADS + POOL_WIDTH)
IN_COLS = IN_SPLITS[-1] + N_BRANCHES * D_MODEL


def rmsnorm(x, w, eps=NORM_EPS):
    x32 = x.astype(jnp.float32)
    y = x32 * lax.rsqrt(jnp.mean(x32 * x32, axis=-1, keepdims=True) + eps)
    return y.astype(x.dtype) * w

def causal_depthwise_conv(u, w, b):
    k_width = w.shape[0]
    seq = u.shape[1]
    up = jnp.pad(u, ((0, 0), (k_width - 1, 0), (0, 0)))
    out = b
    for k in range(k_width):
        out = out + up[:, k:k + seq] * w[k]
    return out

def segsum_decay(a_cs):
    q = a_cs.shape[-1]
    seg = a_cs[..., :, None] - a_cs[..., None, :]
    mask = jnp.tril(jnp.ones((q, q), dtype=bool))
    return jnp.exp(jnp.where(mask, seg, -jnp.inf))

def ssd_chunked_scan(xdt, dtA, bmat, cmat):
    b, seq, _, p = xdt.shape
    g, hg, n, q = SSD_GROUPS, SSD_HEADS_PER_GROUP, SSD_STATE, CHUNK
    nc = seq // q
    x = xdt.astype(jnp.float32).reshape(b, nc, q, g, hg, p)
    a = dtA.astype(jnp.float32).reshape(b, nc, q, g, hg).transpose(0, 3, 4, 1, 2)
    bc = bmat.astype(jnp.float32).reshape(b, nc, q, g, n)
    cc = cmat.astype(jnp.float32).reshape(b, nc, q, g, n)
    a_cs = jnp.cumsum(a, axis=-1)
    scores = jnp.einsum('bclgn,bcsgn->bgcls', cc, bc)
    mmat = scores[:, :, None] * segsum_decay(a_cs)
    y_diag = jnp.einsum('bghcls,bcsghp->bclghp', mmat, x)
    decay_states = jnp.exp(a_cs[..., -1:] - a_cs)
    states = jnp.einsum('bcsgn,bghcs,bcsghp->bcghpn', bc, decay_states, x)
    chunk_decay = jnp.exp(a_cs[..., -1])

    def step(h, inp):
        s_c, d_c = inp
        return h * d_c[..., None, None] + s_c, h

    h0 = jnp.zeros((b, g, hg, p, n), jnp.float32)
    _, prev = lax.scan(step, h0, (jnp.moveaxis(states, 1, 0), jnp.moveaxis(chunk_decay, 3, 0)))
    prev = jnp.moveaxis(prev, 0, 1)
    y_off = jnp.einsum('bclgn,bcghpn,bghcl->bclghp', cc, prev, jnp.exp(a_cs))
    return (y_diag + y_off).reshape(b, seq, SSD_HEADS, p)

def causal_multiscale_pool(u, pool_w, pool_scale):
    b, seq, _ = u.shape
    gw = POOL_GROUP_WIDTH
    u32 = u.astype(jnp.float32)
    cs = jnp.concatenate([jnp.zeros((b, 1, POOL_WIDTH), jnp.float32), jnp.cumsum(u32, axis=1)], axis=1)
    count = jnp.arange(1, seq + 1, dtype=jnp.float32)[:, None]
    outs = []
    for gi, win in enumerate(POOL_WINDOWS):
        csg = cs[:, :, gi * gw:(gi + 1) * gw]
        start = jnp.concatenate([jnp.zeros((b, win - 1, gw), jnp.float32), csg[:, :seq - win + 1]], axis=1)
        mean = (csg[:, 1:] - start) / jnp.minimum(count, float(win))
        outs.append(mean - u32[..., gi * gw:(gi + 1) * gw])
    pooled = jnp.stack(outs, axis=2).astype(u.dtype)
    y = jnp.einsum('blgc,gcd->blgd', pooled, pool_w).reshape(b, seq, POOL_WIDTH)
    return y * pool_scale

def hybrid_mixer(h, w_in, conv_w, conv_b, dt_bias, a_log, d_skip, ssd_norm_w,
                 w_branch_ssd, pool_w, pool_scale, w_branch_pool, w_out):
    b, seq, _ = h.shape
    proj = h @ w_in
    z, xbc, dt_raw, u_pool, gate_logits = jnp.split(proj, IN_SPLITS, axis=-1)
    xbc = jax.nn.silu(causal_depthwise_conv(xbc, conv_w, conv_b))
    xs, bmat, cmat = jnp.split(xbc, (D_INNER, D_INNER + SSD_GROUPS * SSD_STATE), axis=-1)
    xs = xs.reshape(b, seq, SSD_HEADS, SSD_HEAD_DIM)
    bmat = bmat.reshape(b, seq, SSD_GROUPS, SSD_STATE)
    cmat = cmat.reshape(b, seq, SSD_GROUPS, SSD_STATE)
    dt = jax.nn.softplus(dt_raw.astype(jnp.float32) + dt_bias.astype(jnp.float32))
    a_cont = -jnp.exp(a_log.astype(jnp.float32))
    x32 = xs.astype(jnp.float32)
    y = ssd_chunked_scan(x32 * dt[..., None], dt * a_cont, bmat, cmat)
    y = y + d_skip.astype(jnp.float32)[:, None] * x32
    y = y.reshape(b, seq, D_INNER).astype(h.dtype) * jax.nn.silu(z)
    y = rmsnorm(y.reshape(b, seq, SSD_GROUPS, D_INNER // SSD_GROUPS),
                ssd_norm_w.reshape(SSD_GROUPS, D_INNER // SSD_GROUPS))
    y_ssd = y.reshape(b, seq, D_INNER) @ w_branch_ssd
    y_pool = causal_multiscale_pool(u_pool, pool_w, pool_scale) @ w_branch_pool
    g_ssd, g_pool = jnp.split(jax.nn.sigmoid(gate_logits), N_BRANCHES, axis=-1)
    return (g_ssd * y_ssd + g_pool * y_pool) @ w_out

def first_inputs(seed: int = 0) -> dict:
    key = jax.random.key(seed)
    ks = jax.random.split(key, 24)
    f32 = jnp.float32
    nrm = lambda k, shape, s: jax.random.normal(k, shape, f32) * s
    dt0 = jnp.exp(jax.random.uniform(ks[6], (DEPTH, SSD_HEADS), f32)
                  * (np.log(DT_MAX) - np.log(DT_MIN)) + np.log(DT_MIN))
    return {
        "x": nrm(ks[0], (BATCH, SEQ, D_MODEL), 1.0),
        "c": nrm(ks[1], (BATCH, D_MODEL), 1.0),
        "w_ada": nrm(ks[2], (DEPTH, D_MODEL, N_MOD * D_MODEL), D_MODEL ** -0.5),
        "b_ada": nrm(ks[3], (DEPTH, N_MOD * D_MODEL), 0.01),
        "norm_mix_w": 1.0 + nrm(ks[4], (DEPTH, D_MODEL), 0.05),
        "w_in": nrm(ks[5], (DEPTH, D_MODEL, IN_COLS), D_MODEL ** -0.5),
        "conv_w": nrm(ks[7], (DEPTH, CONV_WIDTH, XBC_WIDTH), CONV_WIDTH ** -0.5),
        "conv_b": nrm(ks[8], (DEPTH, XBC_WIDTH), 0.01),
        "dt_bias": dt0 + jnp.log(-jnp.expm1(-dt0)),
        "a_log": jnp.log(jax.random.uniform(ks[9], (DEPTH, SSD_HEADS), f32, 1.0, 16.0)),
        "d_skip": 1.0 + nrm(ks[10], (DEPTH, SSD_HEADS), 0.1),
        "ssd_norm_w": 1.0 + nrm(ks[11], (DEPTH, D_INNER), 0.05),
        "w_branch_ssd": nrm(ks[12], (DEPTH, D_INNER, D_MODEL), D_INNER ** -0.5),
        "pool_w": nrm(ks[13], (DEPTH, POOL_GROUPS, POOL_GROUP_WIDTH, POOL_GROUP_WIDTH), POOL_GROUP_WIDTH ** -0.5),
        "pool_scale": 1.0 + nrm(ks[14], (DEPTH, POOL_WIDTH), 0.1),
        "w_branch_pool": nrm(ks[15], (DEPTH, POOL_WIDTH, D_MODEL), POOL_WIDTH ** -0.5),
        "w_out": nrm(ks[16], (DEPTH, D_MODEL, D_MODEL), D_MODEL ** -0.5),
        "norm_mlp_w": 1.0 + nrm(ks[17], (DEPTH, D_MODEL), 0.05),
        "w_up": nrm(ks[18], (DEPTH, D_MODEL, D_FF), D_MODEL ** -0.5),
        "w_down": nrm(ks[19], (DEPTH, D_FF, D_MODEL), D_FF ** -0.5),
        "norm_final_w": 1.0 + nrm(ks[20], (D_MODEL,), 0.05),
    }

def first_block(x, c, w_ada, b_ada, norm_mix_w, w_in, conv_w, conv_b, dt_bias, a_log, d_skip,
              ssd_norm_w, w_branch_ssd, pool_w, pool_scale, w_branch_pool, w_out,
              norm_mlp_w, w_up, w_down, norm_final_w):
    for i in range(DEPTH):
        mod = (jax.nn.silu(c) @ w_ada[i] + b_ada[i])[:, None, :]
        shift_m, scale_m, gate_m, shift_f, scale_f, gate_f = jnp.split(mod, N_MOD, axis=-1)
        h = rmsnorm(x, norm_mix_w[i]) * (1.0 + scale_m) + shift_m
        x = x + gate_m * hybrid_mixer(h, w_in[i], conv_w[i], conv_b[i], dt_bias[i], a_log[i],
                                      d_skip[i], ssd_norm_w[i], w_branch_ssd[i], pool_w[i],
                                      pool_scale[i], w_branch_pool[i], w_out[i])
        h = rmsnorm(x, norm_mlp_w[i]) * (1.0 + scale_f) + shift_f
        x = x + gate_f * (jnp.square(jax.nn.relu(h @ w_up[i])) @ w_down[i])
    return rmsnorm(x, norm_final_w)


ML_H = 4
ML_HD = D_MODEL // 8
ML_W = ML_H * ML_HD
ML_CONV = 4
ML_CHUNK = 64
ATT_H = 8
ATT_KV = 2
ATT_HD = 64
ATT_W = ATT_H * ATT_HD
WINDOW = 128
ATT_BLOCK = WINDOW
ROPE_THETA = 10000.0
MIX_W = ML_W + ATT_W
IN_COLS_2 = 4 * ML_W + 2 * ML_H + ATT_W + 2 * ATT_KV * ATT_HD
D_FF_2 = 2816
FFN_CONV = 3
RMS_EPS = 1e-6


def rms_norm(x, g):
    xf = x.astype(jnp.float32)
    y = xf * lax.rsqrt(jnp.mean(xf * xf, axis=-1, keepdims=True) + RMS_EPS)
    return (y * g.astype(jnp.float32)).astype(x.dtype)

def causal_dwconv(x, w, b):
    k_len, ch = w.shape
    y = lax.conv_general_dilated(
        x, w[:, None, :].astype(x.dtype), window_strides=(1,),
        padding=((k_len - 1, 0),), dimension_numbers=("NWC", "WIO", "NWC"),
        feature_group_count=ch)
    return y + b.astype(x.dtype)

def rope(x, pos):
    half = x.shape[-1] // 2
    inv = ROPE_THETA ** (-jnp.arange(half, dtype=jnp.float32) / half)
    ang = pos.astype(jnp.float32)[:, None] * inv[None, :]
    cos = jnp.cos(ang)[None, :, None, :]
    sin = jnp.sin(ang)[None, :, None, :]
    xf = x.astype(jnp.float32)
    x1, x2 = xf[..., :half], xf[..., half:]
    return jnp.concatenate([x1 * cos - x2 * sin, x2 * cos + x1 * sin], axis=-1)

def sliding_window_attention(q, k, v, sinks):
    B, S, H, D = q.shape
    G = k.shape[2]
    R = H // G
    nb = S // ATT_BLOCK
    qb = q.reshape(B, nb, ATT_BLOCK, G, R, D)
    kb = k.reshape(B, nb, ATT_BLOCK, G, D)
    vb = v.reshape(B, nb, ATT_BLOCK, G, D)
    pad = ((0, 0), (1, 0), (0, 0), (0, 0), (0, 0))
    kband = jnp.concatenate([jnp.pad(kb, pad)[:, :-1], kb], axis=2)
    vband = jnp.concatenate([jnp.pad(vb, pad)[:, :-1], vb], axis=2)
    s = jnp.einsum('bnqgrd,bnkgd->bngrqk', qb, kband) * (1.0 / math.sqrt(D))
    qi = jnp.arange(ATT_BLOCK)[:, None] + ATT_BLOCK
    kj = jnp.arange(2 * ATT_BLOCK)[None, :]
    rel = qi - kj
    band = (rel >= 0) & (rel < WINDOW)
    kpos = jnp.arange(nb)[:, None, None] * ATT_BLOCK + kj[None] - ATT_BLOCK
    valid = band[None] & (kpos >= 0)
    s = jnp.where(valid[None, :, None, None], s, -jnp.inf)
    sk = sinks.astype(jnp.float32).reshape(G, R)[None, None, :, :, None, None]
    m = jnp.maximum(jnp.max(s, axis=-1, keepdims=True), sk)
    p = jnp.exp(s - m)
    denom = jnp.sum(p, axis=-1, keepdims=True) + jnp.exp(sk - m)
    p = p / denom
    o = jnp.einsum('bngrqk,bnkgd->bnqgrd', p, vband)
    return o.reshape(B, S, H, D)

def mlstm_chunkwise(q, k, v, i_pre, logf):
    B, S, H, D = q.shape
    L = ML_CHUNK
    nc = S // L
    to_c = lambda t: t.reshape(B, nc, L, H, D).transpose(1, 0, 3, 2, 4)
    to_cg = lambda t: t.reshape(B, nc, L, H).transpose(1, 0, 3, 2)
    causal = jnp.tril(jnp.ones((L, L), dtype=bool))

    def step(carry, xs):
        C, n, m = carry
        qc, kc, vc, ic, fc = xs
        b = jnp.cumsum(fc, axis=-1)
        dmat = jnp.where(causal, b[..., :, None] - b[..., None, :] + ic[..., None, :], -jnp.inf)
        m_inter = b + m[..., None]
        m_t = jnp.maximum(m_inter, jnp.max(dmat, axis=-1))
        w_inter = jnp.exp(m_inter - m_t)
        sqk = jnp.einsum('bhtd,bhsd->bhts', qc, kc) * jnp.exp(dmat - m_t[..., None])
        num = jnp.einsum('bhts,bhsd->bhtd', sqk, vc) + \
            w_inter[..., None] * jnp.einsum('bhvk,bhtk->bhtv', C, qc)
        den = jnp.sum(sqk, axis=-1) + w_inter * jnp.einsum('bhk,bhtk->bht', n, qc)
        h = num / jnp.maximum(jnp.abs(den), jnp.exp(-m_t))[..., None]
        b_last = b[..., -1]
        g = b_last[..., None] - b + ic
        m_new = jnp.maximum(b_last + m, jnp.max(g, axis=-1))
        decay = jnp.exp(b_last + m - m_new)
        ws = jnp.exp(g - m_new[..., None])
        C_new = decay[..., None, None] * C + jnp.einsum('bhsv,bhsk->bhvk', vc * ws[..., None], kc)
        n_new = decay[..., None] * n + jnp.einsum('bhs,bhsk->bhk', ws, kc)
        return (C_new, n_new, m_new), h

    init = (jnp.zeros((B, H, D, D), jnp.float32), jnp.zeros((B, H, D), jnp.float32),
            jnp.zeros((B, H), jnp.float32))
    _, hs = lax.scan(step, init, (to_c(q), to_c(k), to_c(v), to_cg(i_pre), to_cg(logf)))
    return hs.transpose(1, 0, 3, 2, 4).reshape(B, S, H, D)

def token_mixer(h, w_in, ml_conv_w, ml_conv_b, ml_i_b, ml_f_b, ml_norm_g,
                attn_sinks, attn_norm_g, w_out):
    B, S, _ = h.shape
    proj = h @ w_in
    cuts = [2 * ML_W, 3 * ML_W, 4 * ML_W, 4 * ML_W + 2 * ML_H, 4 * ML_W + 2 * ML_H + ATT_W]
    qk_ml, v_ml, o_ml, gates, q_at, kv_at = jnp.split(proj, cuts, axis=-1)
    qk_ml = jax.nn.silu(causal_dwconv(qk_ml, ml_conv_w, ml_conv_b)).astype(jnp.float32)
    q_ml = qk_ml[..., :ML_W].reshape(B, S, ML_H, ML_HD)
    k_ml = qk_ml[..., ML_W:].reshape(B, S, ML_H, ML_HD) * (1.0 / math.sqrt(ML_HD))
    v_ml = v_ml.astype(jnp.float32).reshape(B, S, ML_H, ML_HD)
    gates = gates.astype(jnp.float32)
    i_pre = gates[..., :ML_H] + ml_i_b.astype(jnp.float32)
    logf = jax.nn.log_sigmoid(gates[..., ML_H:] + ml_f_b.astype(jnp.float32))
    h_ml = mlstm_chunkwise(q_ml, k_ml, v_ml, i_pre, logf)
    h_ml = rms_norm(h_ml, ml_norm_g)
    h_ml = h_ml * jax.nn.sigmoid(o_ml.astype(jnp.float32).reshape(B, S, ML_H, ML_HD))
    h_ml = h_ml.reshape(B, S, ML_W).astype(h.dtype)
    pos = jnp.arange(S)
    q_at = rope(q_at.reshape(B, S, ATT_H, ATT_HD), pos)
    k_at = rope(kv_at[..., :ATT_KV * ATT_HD].reshape(B, S, ATT_KV, ATT_HD), pos)
    v_at = kv_at[..., ATT_KV * ATT_HD:].astype(jnp.float32).reshape(B, S, ATT_KV, ATT_HD)
    o_at = sliding_window_attention(q_at, k_at, v_at, attn_sinks).reshape(B, S, ATT_W)
    o_at = rms_norm(o_at, attn_norm_g).astype(h.dtype)
    return jnp.concatenate([h_ml, o_at], axis=-1) @ w_out

def conv_ffn(h, w_up, conv_w, conv_b, w_down):
    u = causal_dwconv(h @ w_up, conv_w, conv_b)
    g, val = u[..., :D_FF_2], u[..., D_FF_2:]
    return (jax.nn.gelu(g, approximate=True) * val) @ w_down

def second_inputs(seed: int = 0) -> dict:
    key = jax.random.key(seed)
    ks = jax.random.split(key, 24)
    f32 = jnp.float32
    nrm = lambda k, shp, s: jax.random.normal(k, shp, f32) * s
    gain = lambda k, shp: 1.0 + 0.05 * jax.random.normal(k, shp, f32)
    L = DEPTH
    f_bias = jnp.linspace(3.0, 6.0, ML_H, dtype=f32)[None, :] + nrm(ks[7], (L, ML_H), 0.1)
    return {
        "x": nrm(ks[0], (BATCH, SEQ, D_MODEL), 1.0),
        "c": nrm(ks[1], (BATCH, D_MODEL), 1.0),
        "w_ada": nrm(ks[2], (L, D_MODEL, N_MOD * D_MODEL), 0.5 * D_MODEL ** -0.5),
        "b_ada": nrm(ks[3], (L, N_MOD * D_MODEL), 0.02),
        "pre_mix_g": gain(ks[4], (L, D_MODEL)),
        "w_in": nrm(ks[5], (L, D_MODEL, IN_COLS_2), D_MODEL ** -0.5),
        "ml_conv_w": nrm(ks[6], (L, ML_CONV, 2 * ML_W), ML_CONV ** -0.5),
        "ml_conv_b": nrm(ks[8], (L, 2 * ML_W), 0.02),
        "ml_i_b": nrm(ks[9], (L, ML_H), 0.1),
        "ml_f_b": f_bias,
        "ml_norm_g": gain(ks[10], (L, ML_H, ML_HD)),
        "attn_sinks": nrm(ks[11], (L, ATT_H), 1.0),
        "attn_norm_g": gain(ks[12], (L, ATT_W)),
        "w_out": nrm(ks[13], (L, MIX_W, D_MODEL), MIX_W ** -0.5),
        "post_mix_g": gain(ks[14], (L, D_MODEL)),
        "pre_ffn_g": gain(ks[15], (L, D_MODEL)),
        "w_up": nrm(ks[16], (L, D_MODEL, 2 * D_FF_2), D_MODEL ** -0.5),
        "ffn_conv_w": nrm(ks[17], (L, FFN_CONV, 2 * D_FF_2), FFN_CONV ** -0.5),
        "ffn_conv_b": nrm(ks[18], (L, 2 * D_FF_2), 0.02),
        "w_down": nrm(ks[19], (L, D_FF_2, D_MODEL), D_FF_2 ** -0.5),
        "post_ffn_g": gain(ks[20], (L, D_MODEL)),
    }

def second_block(x, c, w_ada, b_ada, pre_mix_g, w_in, ml_conv_w, ml_conv_b, ml_i_b,
              ml_f_b, ml_norm_g, attn_sinks, attn_norm_g, w_out, post_mix_g,
              pre_ffn_g, w_up, ffn_conv_w, ffn_conv_b, w_down, post_ffn_g):
    c_act = jax.nn.silu(c)
    for l in range(DEPTH):
        mod = c_act @ w_ada[l] + b_ada[l]
        sh1, sc1, g1, sh2, sc2, g2 = [t[:, None, :] for t in jnp.split(mod, N_MOD, axis=-1)]
        h = rms_norm(x, pre_mix_g[l]) * (1.0 + sc1) + sh1
        y = token_mixer(h, w_in[l], ml_conv_w[l], ml_conv_b[l], ml_i_b[l], ml_f_b[l],
                        ml_norm_g[l], attn_sinks[l], attn_norm_g[l], w_out[l])
        x = x + g1 * rms_norm(y, post_mix_g[l])
        h = rms_norm(x, pre_ffn_g[l]) * (1.0 + sc2) + sh2
        y = conv_ffn(h, w_up[l], ffn_conv_w[l], ffn_conv_b[l], w_down[l])
        x = x + g2 * rms_norm(y, post_ffn_g[l])
    return x


def setup_inputs(seed=0):
    out = dict(first_inputs(seed))
    for name, value in second_inputs(seed + 1).items():
        if name != "x":
            out[name + "_2"] = value
    return out


def reference(
    x, c, w_ada, b_ada, norm_mix_w, w_in, conv_w, conv_b, dt_bias, a_log, d_skip, ssd_norm_w,
    w_branch_ssd, pool_w, pool_scale, w_branch_pool, w_out, norm_mlp_w, w_up, w_down,
    norm_final_w, c_2, w_ada_2, b_ada_2, pre_mix_g_2, w_in_2, ml_conv_w_2, ml_conv_b_2,
    ml_i_b_2, ml_f_b_2, ml_norm_g_2, attn_sinks_2, attn_norm_g_2, w_out_2, post_mix_g_2,
    pre_ffn_g_2, w_up_2, ffn_conv_w_2, ffn_conv_b_2, w_down_2, post_ffn_g_2,
):
    x = first_block(
        x, c, w_ada, b_ada, norm_mix_w, w_in, conv_w, conv_b, dt_bias, a_log, d_skip,
        ssd_norm_w, w_branch_ssd, pool_w, pool_scale, w_branch_pool, w_out, norm_mlp_w, w_up,
        w_down, norm_final_w,
    )
    return second_block(
        x, c_2, w_ada_2, b_ada_2, pre_mix_g_2, w_in_2, ml_conv_w_2, ml_conv_b_2, ml_i_b_2,
        ml_f_b_2, ml_norm_g_2, attn_sinks_2, attn_norm_g_2, w_out_2, post_mix_g_2, pre_ffn_g_2,
        w_up_2, ffn_conv_w_2, ffn_conv_b_2, w_down_2, post_ffn_g_2,
    )


_drawn_inputs = setup_inputs


def setup_inputs(seed=0):
    import zlib

    import numpy as np

    out = dict(_drawn_inputs(seed))
    spreads = {}
    factors = {'b_ada': 2.996,
     'conv_b': 8.0,
     'd_skip': 3.982,
     'ssd_norm_w': 3.702,
     'pre_mix_g_2': 4.133,
     'ml_conv_b_2': 64.0,
     'ml_i_b_2': 200.0,
     'ml_norm_g_2': 7.549,
     'attn_sinks_2': 4.611,
     'attn_norm_g_2': 4.135,
     'post_mix_g_2': 3.939,
     'pre_ffn_g_2': 2.952,
     'ffn_conv_b_2': 7.444,
     'post_ffn_g_2': 3.82}
    for name, (base, spread) in spreads.items():
        noise = np.random.default_rng([zlib.crc32(name.encode()), seed]).standard_normal(out[name].shape)
        drawn = base * np.exp(spread * noise) if base else spread * noise
        out[name] = __import__('jax').numpy.asarray(drawn.astype(out[name].dtype))
    for name, factor in factors.items():
        out[name] = (out[name] * factor).astype(out[name].dtype)
    return out
```

```python
from contextlib import ExitStack

import numpy as np

import concourse.bass as bass
from concourse import mybir

F32 = mybir.dt.float32
F32R = mybir.dt.float32r
ALU = mybir.AluOpType
ACT = mybir.ActivationFunctionType
AX_X = mybir.AxisListType.X

P = 128
D_MODEL = 1024
SEQ = 512
KD = D_MODEL // P
TC = SEQ // P
D_INNER = 2 * D_MODEL
HEADS = 32
GROUPS = 4
HG = HEADS // GROUPS
HD = D_INNER // HEADS
GW = D_INNER // GROUPS
STATE = 128
CONV_W = 4
POOL_WINDOWS = (2, 4, 8, 16)
XBC0 = D_INNER
B0 = XBC0 + D_INNER
C0 = B0 + GROUPS * STATE
DT0 = C0 + GROUPS * STATE
U0 = DT0 + HEADS
GATE0 = U0 + D_MODEL
D_FF = 4 * D_MODEL
FF_HALF = D_FF // P // 2
MH = 4
MD = 128
MW = MH * MD
AH = 8
AD = 64
AKV = 2
D_FF_2 = 2816
G2_TILES = D_FF_2 // P
G2_HALF = G2_TILES // 2
FF2_CONV = 3
GATES2 = 4 * MW
QA2 = GATES2 + 2 * MH
KV2 = QA2 + AH * AD
NORM_EPS = 1e-5
RMS_EPS = 1e-6
MASKED = -1.0e30

SLOT = 2048
ADA_COLS = D_MODEL


class Unit:

    def __init__(self, name, weight, k0, kn, segs, act, ak0=0, token_major=False, first=True, last=True, tag=None):
        self.name, self.weight, self.k0, self.kn, self.segs = name, weight, k0, kn, segs
        self.act, self.ak0, self.token_major, self.first, self.last = act, ak0, token_major, first, last
        self.cols = sum(w + pad for _, w, pad in segs)
        self.tag = tag
        self.n_jobs = TC if token_major else (8 if act == "pool" else self.cols // P)
        assert kn * self.cols <= SLOT


def plan_units():
    u = [Unit("DT", "w_in", 0, KD, [(DT0, HEADS, 0)], "h", token_major=True)]

    def branch(g):
        return [Unit(f"Y{i}", "w_branch_ssd", 4 * g, 4, [(512 * i, 512, 0)], "yT", tag=(g, i)) for i in range(2)]

    for g in range(GROUPS):
        x0 = XBC0 + GW * g
        u += [Unit(f"X{i}", "w_in", 0, KD, [(x0 + 256 * i, 256, 0)], "h", tag=(g, i)) for i in range(2)]
        u += [Unit("BC", "w_in", 0, KD, [(B0 + STATE * g, STATE, 0), (C0 + STATE * g, STATE, 0)], "h", tag=(g, 0))]
        u += [Unit(f"Z{i}", "w_in", 4 * i, 4, [(GW * g, GW, 0)], "h", ak0=4 * i, token_major=True,
                   first=(i == 0), last=(i == 1), tag=(g, i)) for i in range(2)]
        if g:
            u += branch(g - 1)
    u += [Unit("U", "w_in", 0, KD, [(U0 + 256 * i, 256, 0)], "h", tag=i) for i in range(4)]
    u += branch(GROUPS - 1)
    u += [Unit("GS", "w_in", 0, KD, [(GATE0 + 256 * i, 256, 0)], "h", tag=i) for i in range(4)]
    u += [Unit("PW", "pool_w", 0, KD, [(0, 256, 0)], "pool")]
    u += [Unit("GP", "w_in", 0, KD, [(GATE0 + D_MODEL + 256 * i, 256, 0)], "h", tag=i) for i in range(4)]
    u += [Unit("BP", "w_branch_pool", 0, KD, [(256 * i, 256, 0)], "pv", tag=i) for i in range(4)]
    u += [Unit("OUT", "w_out", 0, KD, [(256 * i, 256, 0)], "mixed", tag=i) for i in range(4)]
    for half in range(2):
        u += [Unit("UP", "w_up", 0, KD, [(256 * (8 * half + i), 256, 0)], "h", tag=(half, i)) for i in range(8)]
        u += [Unit("DN", "w_down", FF_HALF * half + 8 * j, 8, [(256 * i, 256, 0)], "hidden", ak0=8 * j,
                   first=(j == 0), last=(j == 1), tag=(half, i)) for i in range(4) for j in range(2)]
    u += [Unit("KV", "w_in_2", 0, KD, [(KV2, 256, 0)], "h", token_major=True)]
    u += [Unit(f"QA{i}", "w_in_2", 4 * i, 4, [(QA2, 512, 0)], "h", ak0=4 * i, token_major=True,
               first=(i == 0), last=(i == 1)) for i in range(2)]
    u += [Unit("GA", "w_in_2", 0, KD, [(GATES2, MH, P - MH), (GATES2 + MH, MH, P - MH)], "h")]
    u += [Unit("QK", "w_in_2", 0, KD, [(256 * i, 256, 0)], "h", tag=i) for i in range(4)]
    u += [Unit(f"V{i}", "w_in_2", 4 * i, 4, [(2 * MW, MW, 0)], "h", ak0=4 * i, token_major=True,
               first=(i == 0), last=(i == 1)) for i in range(2)]
    u += [Unit(f"O{i}", "w_in_2", 4 * i, 4, [(3 * MW, MW, 0)], "h", ak0=4 * i, token_major=True,
               first=(i == 0), last=(i == 1)) for i in range(2)]
    u += [Unit("WO", "w_out_2", 0, KD, [(256 * i, 256, 0)], "h", tag=i) for i in range(4)]
    for half in range(2):
        u += [Unit("FU", "w_up_2", 0, KD, [(P * (G2_HALF * half + i), P, 0), (D_FF_2 + P * (G2_HALF * half + i), P, 0)],
                   "h", tag=(half, i)) for i in range(G2_HALF)]
        u += [Unit("FD", "w_down_2", G2_HALF * half + 8 * j, (8, G2_HALF - 8)[j], [(256 * i, 256, 0)], "hidden2",
                   ak0=8 * j, first=(j == 0), last=(j == 1), tag=(half, i)) for i in range(4) for j in range(2)]
    job = 0
    for n, x in enumerate(u):
        if not x.first:
            job -= x.n_jobs
        x.n, x.job0 = n, job
        job += x.n_jobs
    return u


PARAMS = [("c", KD), ("c2", KD), ("b_ada", 48), ("b_ada2", 48), ("norm_mix", KD), ("norm_mlp", KD), ("norm_final", KD),
          ("conv_w", 24 * CONV_W), ("conv_b", 24), ("ssd_norm", 16), ("pool_scale", KD),
          ("dt_bias", HEADS), ("a_log", HEADS), ("d_skip", HEADS),
          ("pre_mix", KD), ("post_mix", KD), ("pre_ffn", KD), ("post_ffn", KD),
          ("ml_conv_w", 8 * CONV_W), ("ml_conv_b", 8), ("ml_norm", MH), ("attn_norm", 4), ("sinks", AH),
          ("ff_conv_w", 2 * G2_TILES * FF2_CONV), ("ff_conv_b", 2 * G2_TILES), ("gate_b", 2),
          ("eps1", 1), ("eps2", 1)]
CONSTS = [("ident", P), ("tri", P), ("ones", P), ("band", 2 * P), ("cos", TC * 32), ("sin", TC * 32),
          ("pool_count", 4 * 16)]


def offsets(blocks):
    at, out = 0, {}
    for name, n in blocks:
        out[name] = (at, n)
        at += n
    return out, at


PARAM_AT, N_PARAM = offsets(PARAMS)
CONST_AT, N_CONST = offsets(CONSTS)


def constants():
    out = np.zeros((P, N_CONST), np.float32)

    def put(name, value):
        at, n = CONST_AT[name]
        out[:, at:at + n] = np.asarray(value, np.float32).reshape(P, n)

    p, f = np.arange(P)[:, None], np.arange(P)[None, :]
    put("ident", p == f)
    put("tri", p <= f)
    put("ones", np.ones((P, P)))
    key = np.arange(2 * P)[None, :]
    rel = p + P - key
    put("band", np.where((rel >= 0) & (rel < P), 0.0, MASKED))
    half = AD // 2
    inv = np.float32(10000.0) ** (-np.arange(half, dtype=np.float32) / np.float32(half))
    ang = np.arange(SEQ, dtype=np.float32)[:, None] * inv.astype(np.float32)[None, :]
    put("cos", np.cos(ang).reshape(TC, P, half).transpose(1, 0, 2))
    put("sin", np.sin(ang).reshape(TC, P, half).transpose(1, 0, 2))
    t = np.arange(1, 17)
    put("pool_count", np.broadcast_to(np.stack([1.0 / np.minimum(t, w) for w in POOL_WINDOWS])[None], (P, 4, 16)))
    return out


def plan_steps(units):
    before, mid, end = ({u.n: [] for u in units} for _ in range(3))
    at = {}
    for u in units:
        at.setdefault(u.name, []).append(u.n)

    def find(name, g=0):
        return at[name][g]

    before[0] += [("norm", 0)]
    end[0] += [("dt_gates", 0)]
    mid[find("X0")] += [("dt_sums", 0)]
    for g in range(GROUPS):
        mid[find("X1", g)] += [("xs_turn", (g, 0))]
        end[find("X1", g)] += [("xs_turn", (g, 1))]
        mid[find("BC", g)] += [("xs_turn", (g, 2))]
        end[find("BC", g)] += [("xs_turn", (g, 3))]
        mid[find("Z0", g)] += [("b_turn", g)]
    for g in range(GROUPS):
        n = find("Z1", g)
        for i in range(TC):
            end[n + i].append(("ssd_scores", (g, i)))
            mid[n + i + 1].append(("ssd_out", (g, i)))
            turned = mid[n + i + 2]
            turned.insert(sum(name == "xs_turn" for name, _ in turned), ("ssd_turn", (g, i)))
    for i in range(4):
        mid[at["GS"][i]] += [("window", 2 * i)]
        end[at["GS"][i]] += [("window", 2 * i + 1)]
    before[at["UP"][0]] += [("norm", 1)]
    before[at["KV"][0]] += [("norm", 2), ("norm", 3)]
    mid[at["QA0"][0]] += [("rope_k", 0)]
    mid[at["GA"][0]] += [("rope_q", 0), ("rope_q", 1)]
    end[at["GA"][0]] += [("rope_q", 2), ("rope_q", 3), ("ml_gates", 0)]
    mid[at["QK"][1]] += [("ml_columns", 0)]
    mid[at["QK"][3]] += [("k_turn", 0)]
    end[at["QK"][3]] += [("k_turn", 1)]
    mid[at["V0"][0]] += [("k_turn", 2)]
    end[at["V0"][0]] += [("k_turn", 3)]
    n = at["GA"][0]
    for q in range(2 * TC):
        end[n + q] += [("att_scores", q)]
        mid[n + q + 1] += [("att_turn", q)]
        end[n + q + 1] += [("att_out", q)]
    end[at["V1"][0]] += [("ml_scores", 0)]
    mid[at["O0"][0]] += [("ml_out", 0)]
    end[at["O0"][0]] += [("ml_scores", 1)]
    mid[at["O1"][0]] += [("ml_out", 1)]
    end[at["O1"][0]] += [("ml_scores", 2)]
    before[at["WO"][0]] += [("ml_out", 2), ("ml_scores", 3), ("ml_out", 3)] + [("join", c) for c in range(TC)]
    before[at["FU"][0]] += [("norm", 4), ("norm", 5)]
    last = [("norm", 6)]
    for p in range(80):
        mid[1 + p].append(("ada_piece", p))
        if p % 8 == 7:
            end[1 + p].append(("ada_sum", p // 8 + 2))
    order = [s for u in units for s in before[u.n] + mid[u.n] + end[u.n]] + last
    return before, mid, end, last, order


BANKS_OF = {"norm": "D", "ada_sum": "D", "dt_sums": "A", "xs_turn": "A", "b_turn": "A", "ssd_scores": "ABC",
            "ssd_out": "DBC", "ssd_turn": "A", "rope_k": "A", "rope_q": "A", "ml_columns": "AD", "k_turn": "A",
            "att_scores": "BC", "att_turn": "BC", "att_out": "D", "ml_scores": "BC", "ml_out": "DBACAC",
            "join": "AB"}


def build(nc, stream, w_ada, w_ada2, x_in, params_in, consts_in, out):
    units = plan_units()
    before, mid, end, last, order = plan_steps(units)
    bank_use, used = {}, {b: 0 for b in "ABCD"}
    for stage in [("ada_sum", 0), ("ada_sum", 1)] + order:
        bank_use[stage] = []
        for b in BANKS_OF.get(stage[0], ""):
            bank_use[stage].append((b, used[b]))
            used[b] += 1
    conv_units = [u for u in units if u.name in ("X0", "X1", "BC", "QK")]
    conv_at = {(u.n, t): 2 * i + t for i, u in enumerate(conv_units) for t in range(2)}
    unit_at = {}
    for u in units:
        unit_at.setdefault(u.name, []).append(u.n)

    with ExitStack() as ctx:
        def alloc(stack, name, shape, dt=F32):
            return stack.enter_context(nc.sbuf_tensor(name, [P] + list(shape), dt))

        x = alloc(ctx, "x", [KD, SEQ])
        h_hi, h_lo = (alloc(ctx, f"h_{s}", [KD, SEQ], F32R) for s in ("hi", "lo"))
        raw = alloc(ctx, "raw", [2, SLOT])
        w_hi, w_lo = (alloc(ctx, f"w_{s}", [2, SLOT], F32R) for s in ("hi", "lo"))
        par = alloc(ctx, "par", [N_PARAM])
        con = alloc(ctx, "con", [N_CONST])
        mod = alloc(ctx, "mod", [12 * KD])
        mul = alloc(ctx, "mul", [8, KD])
        half = alloc(ctx, "half", [24 * CONV_W + 24 + 8 * CONV_W + 8 + MH])
        cs = alloc(ctx, "cs", [2, KD])
        cst = alloc(ctx, "cst", [2, KD])
        ada_raw = alloc(ctx, "ada_raw", [2, ADA_COLS])
        ada_acc = alloc(ctx, "ada_acc", [ADA_COLS])
        tmp = alloc(ctx, "tmp", [4, SEQ])
        small = alloc(ctx, "small", [64])

        rstd = alloc(ctx, "rstd", [SEQ])
        with ExitStack() as s0:
            ada_first = alloc(s0, "ada_first", [2 * KD, ADA_COLS])
        with ExitStack() as s1:
            xs_tok = alloc(s1, "xs_tok", [2, TC, GW])
            with ExitStack() as s2:
                z = alloc(s2, "z", [TC, GW])
                bc = alloc(s2, "bc", [2, 2, SEQ])
                b_tok = alloc(s2, "b_tok", [2, TC, STATE])
                y_part = alloc(s2, "y_part", [GW])
                y_turned = alloc(s2, "y_turned", [4, P])
                yt_hi, yt_lo = (alloc(s2, f"yt_{s}", [4, SEQ], F32R) for s in ("hi", "lo"))
                xdt = alloc(s2, "xdt", [3, GW])
                decay = alloc(s2, "decay", [HG, P])
                sc = alloc(s2, "sc", [P])
                state = alloc(s2, "state", [GW])
                dt, dta, acs, eacs, edec, cdec, dtt = (alloc(s2, n, [TC, HEADS]) for n in
                                                       ("dt", "dta", "acs", "eacs", "edec", "cdec", "dtt"))
                ss = alloc(s2, "ss", [4])
                sq_out = alloc(s2, "sq_out", [GW])
            with ExitStack() as s3:
                p_hi, p_lo, v_hi, v_lo = (alloc(s3, n, [KD, SEQ], F32R) for n in ("p_hi", "p_lo", "v_hi", "v_lo"))
        with ExitStack() as s4:
            f_hi, f_lo = (alloc(s4, n, [FF_HALF, SEQ], F32R) for n in ("f_hi", "f_lo"))
        with ExitStack() as s5:
            qk = alloc(s5, "qk", [8, SEQ])
            v1 = alloc(s5, "v1", [TC, MH, MD + 1])
            k_tok = alloc(s5, "k_tok", [TC, MH, MD])
            og = alloc(s5, "og", [TC, MW])
            hm = alloc(s5, "hm", [TC, MW])
            qa = alloc(s5, "qa", [TC + 1, 4, P])
            ka = alloc(s5, "ka", [SEQ])
            k_rot = alloc(s5, "k_rot", [TC, P])
            va = alloc(s5, "va", [TC, P])
            prob = alloc(s5, "prob", [4, 2 * P])
            prob_t = alloc(s5, "prob_t", [4, 2, P])
            cell = alloc(s5, "cell", [MH, MD + 1])
            quant = alloc(s5, "quant", [SEQ])
            qcol = alloc(s5, "qcol", [TC, P])
            urow = alloc(s5, "urow", [SEQ])
            dec = alloc(s5, "dec", [MH * TC])
            att = alloc(s5, "att", [32])
            decb = alloc(s5, "decb", [MH * TC])
        with ExitStack() as s6:
            g_hi, g_lo = (alloc(s6, n, [G2_HALF, SEQ], F32R) for n in ("g_hi", "g_lo"))
            gel = alloc(s6, "gel", [SEQ])
        with ExitStack() as s7:
            s7.enter_context(nc.sbuf_tensor("skip7", [P, 2 * G2_HALF * SEQ + SEQ], F32))
            ysum = alloc(s7, "ysum", [KD, SEQ])

        main = [ctx.enter_context(nc.psum_tensor(f"main{i}", [P, SEQ], F32)) for i in range(4)]
        aux = {b: ctx.enter_context(nc.psum_tensor(f"aux{b}", [P, SEQ], F32)) for b in "ABCD"}

        def sem(name):
            return ctx.enter_context(nc.semaphore(name))

        main_full = [sem(f"main_full{i}") for i in range(4)]
        main_free = [sem(f"main_free{i}") for i in range(4)]
        aux_full = {b: sem(f"aux_full{b}") for b in "ABCD"}
        aux_free = {b: sem(f"aux_free{b}") for b in "ABCD"}
        raw_in = [sem(f"raw_in{i}") for i in range(2)]
        ada_in = [sem(f"ada_in{i}") for i in range(2)]
        first_in = [sem(f"first_in{i}") for i in range(2)]
        (par_in, x_in_sem, hi_done, lo_done, unit_done, dve_chain, act_chain, pool_chain, ada_used, conv_a,
         conv_d, conv_t, conv_s, turned, x_ready, ysum_ready, norm_sq, norm_use, norm_rt, norm_tmp, norm_hi,
         norm_lo, cs_t, dt_x, dt_e, dt_s, dt_acs, dt_last, seg, seg_e, mix, pre_x, y_ready, y_sq, y_rs,
         y_norm, yt_h, yt_t, yt_l, z_t, xs_ready, b_ready, st_ready, ssd_read, gate_t, gate_used, win_ready,
         pl_hi, pl_lo, pv_hi, pv_lo, mx_t, mx_hi, mx_lo, x_back, hid_t, hid_hi, hid_lo, gel_a, gel_d, gel_g,
         hid2_t, hid2_hi, hid2_lo, kv_ready, rot_ready, qa_ready, ka_ready, sm_max, sm_exp, pt_ready, at_rs,
         at_sq, at_out, mg_x, mg_e, mg_s, col_ready, dec_ready, kt_ready, v_ready, ml_u, ml_e, ml_p, ml_vw,
         ml_cell, ml_out, ml_sq, ml_rs, og_t, jn_t, jn_hi, jn_lo, out_done, ada_ready, mod_ready, at_raw) = [
            sem(n) for n in (
                "par_in x_in_sem hi_done lo_done unit_done dve_chain act_chain pool_chain ada_used conv_a conv_d "
                "conv_t conv_s turned x_ready ysum_ready norm_sq norm_use norm_rt norm_tmp norm_hi norm_lo cs_t dt_x "
                "dt_e dt_s dt_acs dt_last seg seg_e mix pre_x y_ready y_sq y_rs y_norm yt_h yt_t yt_l z_t xs_ready "
                "b_ready st_ready ssd_read gate_t gate_used win_ready pl_hi pl_lo pv_hi pv_lo mx_t mx_hi mx_lo x_back "
                "hid_t hid_hi hid_lo gel_a gel_d gel_g hid2_t hid2_hi hid2_lo kv_ready rot_ready qa_ready ka_ready "
                "sm_max sm_exp pt_ready at_rs at_sq at_out mg_x mg_e mg_s col_ready dec_ready kt_ready v_ready ml_u "
                "ml_e ml_p ml_vw ml_cell ml_out ml_sq ml_rs og_t jn_t jn_hi jn_lo out_done ada_ready mod_ready at_raw "
            ).split()]
        block = ctx.enter_context(nc.Block())

        def pc(name, a=0, b=None):
            at, n = PARAM_AT[name]
            return par[:, at + a:at + (n if b is None else b)]

        def cc(name, a=0, b=None):
            at, n = CONST_AT[name]
            return con[:, at + a:at + (n if b is None else b)]

        ident, tri, ones = cc("ident"), cc("tri"), cc("ones")
        cw_half = half[:, 0:96]
        cb_half = half[:, 96:120]
        mw_half = half[:, 120:152]
        mb_half = half[:, 152:160]
        mn_half = half[:, 160:164]

        def over(ap, n):
            return ap.unsqueeze(2).to_broadcast([P, ap.shape[1], n])

        def each(ap, n):
            return ap.unsqueeze(1).to_broadcast([P, n, ap.shape[1]])

        def conv_par(u, t):
            if u.name == "QK":
                c = 2 * u.tag + t
                return mw_half[:, 4 * c:4 * c + 4], mb_half[:, c:c + 1]
            g = u.tag[0]
            c = 4 * g + 2 * u.tag[1] + t if u.name in ("X0", "X1") else 16 + 4 * t + g
            return cw_half[:, 4 * c:4 * c + 4], cb_half[:, c:c + 1]

        def mod_at(s):
            return mod[:, KD * s:KD * (s + 1)]

        acts = {"h": (h_hi, h_lo), "yT": (yt_hi, yt_lo), "pool": (p_hi, p_lo), "pv": (v_hi, v_lo),
                "mixed": (p_hi, p_lo), "hidden": (f_hi, f_lo), "hidden2": (g_hi, g_lo)}
        NORMS = [("x", 0, 0, "h"), ("x", 1, 3, "h"), ("x", None, None, "x"), ("x", 2, 6, "h"),
                 ("ysum", 3, None, "add"), ("x", 4, 9, "h"), ("ysum", 5, None, "add")]
        NORM_EPS_OF = ["eps1", "eps1", "eps1", "eps2", "eps2", "eps2", "eps2"]
        X_AT = [0, 8, 24, 32, None, 40, None]
        Y_AT = {4: 8, 6: 24}
        split_norms = [n for n, v in enumerate(NORMS) if v[3] == "h"]
        first_unit_after = {0: 0, 1: unit_at["UP"][0], 3: unit_at["KV"][0], 5: unit_at["FU"][0]}

        def chunk(c):
            return slice(P * c, P * (c + 1))

        turn_of = {}
        for g in range(GROUPS):
            for t in range(4):
                turn_of[6 * g + t] = ("xs_turn", (g, t))

        def win_slot(t):
            return 2 + (t // 2) % 2

        def units_over(k):
            u = units[k - 1]
            if u.last:
                j = u.job0 + u.n_jobs - 1
                return main_full[j % 4], j // 4 + 1
            return unit_done, sum(1 for v in units[:k] if not v.last)

        flat_k = k_tok[:, :, :, :].rearrange("p c h d -> p (c h d)")
        flat_v = v1[:, :, :, :].rearrange("p c h d -> p (c h d)")
        row_i, row_f, row_m, row_b = (flat_k[0:MH, SEQ * n:SEQ * (n + 1)] for n in range(4))
        row_e, row_t, row_z = (flat_v[0:MH, SEQ * n:SEQ * (n + 1)] for n in range(3))

        @block.sync
        def _(sp):
            def load_unit(u):
                s = u.n % 2
                if u.n >= 2:
                    sp.wait_ge(lo_done, u.n - 1)
                k = u.kn * u.cols
                sp.dma_start(raw[:, s, 0:k], stream[u.n, :, 0:k]).then_inc(raw_in[s], 16)

            sp.dma_start(par[:, :], params_in).then_inc(par_in, 16)
            sp.dma_start(con[:, :], consts_in).then_inc(par_in, 16)
            sp.dma_start(x[:, :, :], x_in).then_inc(x_in_sem, 16)
            for s in (1, 0):
                for k in range(KD):
                    sp.dma_start(ada_first[:, KD * s + k, :],
                                 w_ada[P * k:P * (k + 1), ADA_COLS * s:ADA_COLS * (s + 1)]).then_inc(first_in[s], 16)
            for u in units:
                if u.name == "OUT" and u.tag == 2:
                    sp.wait_ge(mx_lo, KD)
                    sp.dma_start(x[:, :, :], x_in).then_inc(x_back, 16)
                load_unit(u)
            sp.wait_ge(x_ready, 48)
            sp.dma_start(out, x[:, :, :]).then_inc(out_done, 16)
            sp.wait_ge(out_done, 16)

        @block.gpsimd
        def _(pool):
            chain = [0]

            def link(ins):
                chain[0] += 1
                ins.then_inc(pool_chain, 1)
                pool.wait_ge(pool_chain, chain[0])

            def split_lo(u):
                s = u.n % 2
                k = u.kn * u.cols
                pool.wait_ge(hi_done, u.n + 1)
                if u.n >= 2:
                    pool.wait_ge(*units_over(u.n - 1))
                nc.gpsimd.tensor_tensor(w_lo[:, s, 0:k], raw[:, s, 0:k], w_hi[:, s, 0:k], ALU.subtract).then_inc(lo_done, 1)

            def ssd_scores(i, n):
                g, c = i
                xs = xs_tok[:, g % 2, c, :].rearrange("p (h d) -> p h d", d=HD)
                heads = slice(HG * g, HG * (g + 1))
                pool.wait_ge(dt_last, 1)
                pool.wait_ge(xs_ready, 4 * (g + 1))
                if n:
                    pool.wait_ge(ssd_read, n)
                    pool.wait_ge(y_ready, n)

                def times(k, factor):
                    return nc.gpsimd.tensor_tensor(xdt[:, k, :].rearrange("p (h d) -> p h d", d=HD), xs,
                                                   over(factor, HD), ALU.mult)
                times(0, dt[:, c, heads])
                times(1, dtt[:, c, heads])
                times(2, pc("d_skip", HG * g, HG * (g + 1))).then_inc(pre_x, 1)

            def ssd_out(i, n):
                pool.wait_ge(y_sq, n + 1)
                link(nc.gpsimd.tensor_scalar(ss[:, 1:2], ss[:, 0:1], 1.0 / GW, 4.0 * NORM_EPS, ALU.mult, ALU.add))
                if n:
                    pool.wait_ge(y_norm, n)
                nc.gpsimd.tensor_tensor(ss[:, 2:3], ss[:, 1:2], small[:, 63:64], ALU.pow).then_inc(y_rs, 1)

            def att_out(q, n):
                if q % 2 == 0:
                    return
                i = q // 2
                pool.wait_ge(at_sq, i + 1)
                link(nc.gpsimd.tensor_scalar(att[:, 26:27], att[:, 25:26], 1.0 / (AH * AD), RMS_EPS, ALU.mult, ALU.add))
                nc.gpsimd.tensor_tensor(att[:, 27:28], att[:, 26:27], small[:, 63:64], ALU.pow).then_inc(at_rs, 1)

            def ml_out_(c, n):
                pool.wait_ge(ml_sq, c + 1)
                link(nc.gpsimd.tensor_scalar(small[:, 4:8], small[:, 0:4], 1.0 / MD, RMS_EPS, ALU.mult, ALU.add))
                nc.gpsimd.tensor_tensor(small[:, 8:12], small[:, 4:8], small[:, 60:64], ALU.pow).then_inc(ml_rs, 1)

            stages = {"ssd_scores": ssd_scores, "ssd_out": ssd_out, "att_out": att_out, "ml_out": ml_out_}
            count = {}

            def run(steps):
                for name, item in steps:
                    n = count.get(name, 0)
                    count[name] = n + 1
                    if name in stages:
                        stages[name](item, n)

            link(nc.gpsimd.memset(small[:, 60:64], -0.5))
            split_lo(units[0])
            for u in units:
                run(before[u.n])
                if u.n + 1 < len(units):
                    split_lo(units[u.n + 1])
                run(mid[u.n])
                run(end[u.n])

        @block.tensor
        def _(pe):
            def take(stage, k):
                b, use = bank_use[stage][k]
                if use:
                    pe.wait_ge(aux_free[b], use)
                return aux[b], aux_full[b]

            def operands_ready(u):
                if u.act == "h":
                    n = sum(1 for v in split_norms if first_unit_after[v] <= u.n)
                    if u.name == "WO":
                        pe.wait_ge(jn_hi, 2 * TC)
                        pe.wait_ge(jn_lo, 2 * TC)
                    else:
                        pe.wait_ge(norm_hi, KD * n)
                        pe.wait_ge(norm_lo, KD * n)
                elif u.act == "yT":
                    pe.wait_ge(yt_h, TC * (u.tag[0] + 1))
                    pe.wait_ge(yt_l, TC * (u.tag[0] + 1))
                elif u.act == "pool":
                    pe.wait_ge(pl_hi, KD)
                    pe.wait_ge(pl_lo, KD)
                elif u.act == "pv":
                    pe.wait_ge(pv_hi, KD)
                    pe.wait_ge(pv_lo, KD)
                elif u.act == "mixed":
                    pe.wait_ge(mx_hi, KD)
                    pe.wait_ge(mx_lo, KD)
                elif u.act == "hidden":
                    pe.wait_ge(hid_hi, FF_HALF * (u.tag[0] + 1))
                    pe.wait_ge(hid_lo, FF_HALF * (u.tag[0] + 1))
                elif u.act == "hidden2":
                    pe.wait_ge(hid2_hi, G2_HALF * (u.tag[0] + 1))
                    pe.wait_ge(hid2_lo, G2_HALF * (u.tag[0] + 1))

            def project(u, part):
                s = u.n % 2
                if part == 0:
                    pe.wait_ge(lo_done, u.n + 1)
                    operands_ready(u)
                wh = w_hi[:, s, 0:u.kn * u.cols].rearrange("p (k c) -> p k c", k=u.kn)
                wl = w_lo[:, s, 0:u.kn * u.cols].rearrange("p (k c) -> p k c", k=u.kn)
                ah, al = acts[u.act]
                jobs = range(u.n_jobs // 2) if part == 0 else range(u.n_jobs // 2, u.n_jobs)
                for t in jobs:
                    j = u.job0 + t
                    bank = main[j % 4]
                    if u.first and j >= 4:
                        pe.wait_ge(main_free[j % 4], j // 4)
                    ks = range(u.kn)
                    if u.act == "pool":
                        ks = range(2 * (t // 2), 2 * (t // 2) + 2)
                    for k in ks:
                        for a, w in ((ah, wh), (al, wh), (ah, wl)):
                            ka_ = k if u.act == "pool" else u.ak0 + k
                            start = u.first and k == ks[0] and a is ah and w is wh
                            stop = u.last and k == ks[-1] and w is wl
                            if u.token_major:
                                ins = nc.tensor.matmul(bank[:, 0:u.cols], a[:, ka_, chunk(t)], w[:, k, :], start=start, stop=stop)
                            else:
                                col = P * (t % 2) if u.act == "pool" else P * t
                                ins = nc.tensor.matmul(bank[:, :], w[:, k, col:col + P], a[:, ka_, :], start=start, stop=stop)
                    if u.last:
                        ins.then_inc(main_full[j % 4], 1)
                return ins

            def norm(i, n):
                src, _, _, _ = NORMS[i]
                bank, full = take(("norm", i), 0)
                for k in range(KD):
                    pe.wait_ge(norm_sq, KD * i + k + 1)
                    ins = nc.tensor.matmul(bank[:, :], ones, tmp[:, k % 2, :], start=(k == 0), stop=(k == KD - 1))
                    if k < KD - 1:
                        ins.then_inc(norm_use, 1)
                ins.then_inc(full, 1)

            def ada_sum(s, n):
                bank, full = take(("ada_sum", s), 0)
                pe.wait_ge(ada_ready, s + 1)
                for t in range(KD):
                    ins = nc.tensor.matmul(bank[:, t:t + 1], ada_acc[:, chunk(t)], ones[:, 0:1], start=True, stop=True)
                ins.then_inc(full, 1)

            def dt_sums(i, n):
                bank, full = take(("dt_sums", 0), 0)
                pe.wait_ge(dt_s, 1)
                for c in range(TC):
                    nc.tensor.matmul(bank[:, HEADS * c:HEADS * (c + 1)], tri, dta[:, c, :], start=True, stop=True)
                for c in range(TC):
                    ins = nc.tensor.matmul(bank[:, P + HEADS * c:P + HEADS * (c + 1)], ones, dta[:, c, :], start=True, stop=True)
                ins.then_inc(full, 1)

            def xs_turn(i, n):
                g, t = i
                bank, full = take(("xs_turn", i), 0)
                cn = conv_at[[u.n for u in conv_units if u.name == f"X{t // 2}"][g], t % 2]
                pe.wait_ge(conv_s, cn + 1)
                for c in range(TC):
                    ins = nc.tensor.transpose(bank[:, chunk(c)], tmp[:, cn % 2, chunk(c)], ident)
                ins.then_inc(full, 1)

            def b_turn(g, n):
                bank, full = take(("b_turn", g), 0)
                cn = conv_at[[u.n for u in conv_units if u.name == "BC"][g], 1]
                pe.wait_ge(conv_s, cn + 1)
                for c in range(TC):
                    ins = nc.tensor.transpose(bank[:, chunk(c)], bc[:, g % 2, 0, chunk(c)], ident)
                ins.then_inc(full, 1)

            def ssd_scores(i, n):
                g, c = i
                pe.wait_ge(dt_acs, 1)
                bank, full = take(("ssd_scores", i), 0)
                nc.tensor.matmul(bank[:, 0:P], bc[:, g % 2, 0, chunk(c)], bc[:, g % 2, 1, chunk(c)],
                                 start=True, stop=True).then_inc(full, 1)
                for b in range(2):
                    bank, full = take(("ssd_scores", i), 1 + b)
                    for k in range(4):
                        hd = HG * g + 4 * b + k
                        ins = nc.tensor.matmul(bank[:, chunk(k)], dta[:, c, hd:hd + 1].to_broadcast([P, P]), tri,
                                               start=True, stop=True)
                    ins.then_inc(full, 1)

            def ssd_out(i, n):
                g, c = i
                bank, full = take(("ssd_out", i), 0)
                pe.wait_ge(mix, n + 1)
                pe.wait_ge(pre_x, n + 1)
                for k in range(HG):
                    ins = nc.tensor.matmul(bank[:, HD * k:HD * (k + 1)], decay[:, k, :], xdt[:, 0, HD * k:HD * (k + 1)],
                                           start=True, stop=True)
                ins.then_inc(full, 1)
                bank, full = take(("ssd_out", i), 1)
                pe.wait_ge(b_ready, g + 1)
                if c:
                    pe.wait_ge(st_ready, n)
                    nc.tensor.matmul(bank[:, :], bc[:, g % 2, 1, chunk(c)], state[:, :], start=True, stop=True).then_inc(full, 1)
                else:
                    nc.tensor.matmul(bank[:, 0:1], ident, ones[:, 0:1], start=True, stop=True).then_inc(full, 1)
                bank, full = take(("ssd_out", i), 2)
                ins = nc.tensor.matmul(bank[:, :], b_tok[:, g % 2, c, :], xdt[:, 1, :], start=True, stop=True)
                ins.then_inc(full, 1)

            def ssd_turn(i, n):
                g, c = i
                bank, full = take(("ssd_turn", i), 0)
                pe.wait_ge(y_norm, n + 1)
                for t in range(4):
                    ins = nc.tensor.transpose(bank[:, chunk(t)], z[:, c, chunk(t)], ident)
                ins.then_inc(full, 1)

            def rope_k(i, n):
                bank, full = take(("rope_k", 0), 0)
                pe.wait_ge(rot_ready, TC)
                for c in range(TC):
                    ins = nc.tensor.transpose(bank[:, chunk(c)], k_rot[:, c, :], ident)
                ins.then_inc(full, 1)

            def rope_q(c, n):
                bank, full = take(("rope_q", c), 0)
                pe.wait_ge(rot_ready, TC + c + 1)
                for t in range(4):
                    ins = nc.tensor.transpose(bank[:, chunk(t)], hm[:, c, chunk(t)], ident)
                ins.then_inc(full, 1)

            def keys(i):
                return (0, P) if i == 0 else (P * (i - 1), 2 * P)

            def att_scores(q, n):
                i, g = q // 2, q % 2
                k0, kn = keys(i)
                rows = slice(AD * g, AD * (g + 1))
                pe.wait_ge(qa_ready, i + 1)
                pe.wait_ge(ka_ready, 1)
                for b in range(2):
                    bank, full = take(("att_scores", q), b)
                    for j in range(2):
                        ins = nc.tensor.matmul(bank[:, 2 * P * j + 2 * P - kn:2 * P * (j + 1)], qa[rows, i + 1, 2 * b + j, :],
                                               ka[rows, k0:k0 + kn], start=True, stop=True)
                    ins.then_inc(full, 1)

            def att_turn(q, n):
                i = q // 2
                pe.wait_ge(sm_exp, q + 1)
                for b in range(2):
                    bank, full = take(("att_turn", q), b)
                    for j in range(2):
                        for r in range(2):
                            if i == 0 and r == 0:
                                continue
                            ins = nc.tensor.transpose(bank[:, 2 * P * j + P * r:2 * P * j + P * (r + 1)],
                                                      prob[:, 2 * b + j, chunk(r)], ident)
                    ins.then_inc(full, 1)

            def att_out_(q, n):
                i, g = q // 2, q % 2
                bank, full = take(("att_out", q), 0)
                pe.wait_ge(pt_ready, 2 * (q + 1))
                pe.wait_ge(kv_ready, TC)
                for j in range(4):
                    for r in range(2):
                        if i == 0 and r == 0:
                            continue
                        ins = nc.tensor.matmul(bank[:, AD * j:AD * (j + 1)], prob_t[:, j, r, :],
                                               va[:, i - 1 + r, AD * g:AD * (g + 1)], start=(r == 0 or i == 0), stop=(r == 1))
                ins.then_inc(full, 1)

            def ml_columns(i, n):
                pe.wait_ge(mg_s, 1)
                bank, full = take(("ml_columns", 0), 0)
                for c in range(TC):
                    ins = nc.tensor.transpose(bank[:, chunk(c)], quant[:, chunk(c)], ident)
                ins.then_inc(full, 1)
                bank, full = take(("ml_columns", 0), 1)
                for hd in range(MH):
                    ins = nc.tensor.matmul(bank[:, TC * hd:TC * (hd + 1)], ident[0:MH, hd:hd + 1].to_broadcast([MH, P]),
                                           dec[0:MH, 0:TC], start=True, stop=True)
                ins.then_inc(full, 1)

            def k_turn(hd, n):
                bank, full = take(("k_turn", hd), 0)
                pe.wait_ge(conv_s, 24 + 4 + hd + 1)
                pe.wait_ge(kt_ready, hd + 1)
                for c in range(TC):
                    ins = nc.tensor.transpose(bank[:, chunk(c)], qk[:, 4 + hd, chunk(c)], ident)
                ins.then_inc(full, 1)

            def ml_scores(c, n):
                bank, full = take(("ml_scores", c), 0)
                pe.wait_ge(kt_ready, MH)
                for hd in range(MH):
                    ins = nc.tensor.matmul(bank[:, chunk(hd)], qk[:, 4 + hd, chunk(c)], qk[:, hd, chunk(c)], start=True, stop=True)
                ins.then_inc(full, 1)
                bank, full = take(("ml_scores", c), 1)
                for hd in range(MH):
                    ins = nc.tensor.matmul(bank[:, chunk(hd)], ident[0:MH, hd:hd + 1].to_broadcast([MH, P]),
                                           urow[0:MH, chunk(c)], start=True, stop=True)
                ins.then_inc(full, 1)

            def ml_out_(c, n):
                pe.wait_ge(ml_p, c + 1)
                pe.wait_ge(v_ready, TC)
                pe.wait_ge(ml_vw, c + 1)
                pp = tmp[:, 0, :].rearrange("p (h t) -> p h t", h=MH)
                vw = tmp[:, :, :].rearrange("p a b -> p (a b)")[:, SEQ:SEQ + MH * (MD + 1)].rearrange("p (h d) -> p h d", h=MH)
                W = MD + 1
                for b in range(2):
                    bank, full = take(("ml_out", c), b)
                    for j in range(2):
                        ins = nc.tensor.matmul(bank[:, W * j:W * (j + 1)], pp[:, 2 * b + j, :], v1[:, c, 2 * b + j, :], start=True, stop=True)
                    ins.then_inc(full, 1)
                for b in range(2):
                    bank, full = take(("ml_out", c), 2 + b)
                    pe.wait_ge(ml_cell, c + 1)
                    for j in range(2):
                        ins = nc.tensor.matmul(bank[:, W * j:W * (j + 1)], qk[:, 2 * b + j, chunk(c)], cell[:, 2 * b + j, :], start=True, stop=True)
                    ins.then_inc(full, 1)
                for b in range(2):
                    bank, full = take(("ml_out", c), 4 + b)
                    pe.wait_ge(dec_ready, MH)
                    for j in range(2):
                        ins = nc.tensor.matmul(bank[:, W * j:W * (j + 1)], k_tok[:, c, 2 * b + j, :], vw[:, 2 * b + j, :], start=True, stop=True)
                    ins.then_inc(full, 1)

            def join(c, n):
                bank, full = take(("join", c), 0)
                pe.wait_ge(ml_out, c + 1)
                for t in range(MH):
                    ins = nc.tensor.transpose(bank[:, chunk(t)], hm[:, c, chunk(t)], ident)
                ins.then_inc(full, 1)
                bank, full = take(("join", c), 1)
                pe.wait_ge(at_out, c + 1)
                for t in range(4):
                    ins = nc.tensor.transpose(bank[:, chunk(t)], qa[:, c, t, :], ident)
                ins.then_inc(full, 1)

            stages = {"norm": norm, "ada_sum": ada_sum, "dt_sums": dt_sums, "xs_turn": xs_turn, "b_turn": b_turn,
                      "ssd_scores": ssd_scores, "ssd_out": ssd_out, "ssd_turn": ssd_turn, "rope_k": rope_k, "rope_q": rope_q,
                      "att_scores": att_scores, "att_turn": att_turn, "att_out": att_out_, "ml_columns": ml_columns,
                      "k_turn": k_turn, "ml_scores": ml_scores, "ml_out": ml_out_, "join": join}
            count = {}

            def run(steps):
                for name, item in steps:
                    n = count.get(name, 0)
                    count[name] = n + 1
                    if name in stages:
                        stages[name](item, n)

            pe.wait_ge(par_in, 32)
            ada_sum(0, 0)
            ada_sum(1, 1)
            for u in units:
                run(before[u.n])
                project(u, 0)
                run(mid[u.n])
                ins = project(u, 1)
                if not u.last:
                    ins.then_inc(unit_done, 1)
                run(end[u.n])
            run(last)

        @block.scalar
        def _(act):
            chain = [0]

            def link(ins):
                chain[0] += 1
                ins.then_inc(act_chain, 1)
                act.wait_ge(act_chain, chain[0])

            run_act = nc.scalar.activation

            def full(stage, k):
                b, use = bank_use[stage][k]
                act.wait_ge(aux_full[b], use + 1)
                return aux[b], aux_free[b]

            def read_by_pe(stage, k):
                b, use = bank_use[stage][k]
                act.wait_ge(aux_full[b], use + 1)

            def tile(j):
                act.wait_ge(main_full[j % 4], j // 4 + 1)
                return main[j % 4], main_free[j % 4]

            def split_hi(u):
                s = u.n % 2
                k = u.kn * u.cols
                act.wait_ge(raw_in[s], 16 * (u.n // 2 + 1))
                if u.n >= 2:
                    act.wait_ge(*units_over(u.n - 1))
                run_act(w_hi[:, s, 0:k], raw[:, s, 0:k], ACT.Copy).then_inc(hi_done, 1)

            def convolve(u, t):
                cn = conv_at[u.n, t]
                w, b = conv_par(u, t)
                if cn >= 2:
                    act.wait_ge(conv_s, cn - 1)
                    if cn - 2 in turn_of:
                        read_by_pe(turn_of[cn - 2], 0)
                bank, free = tile(u.job0 + t)
                run_act(tmp[:, cn % 2, :], bank[:, :], ACT.Identity, bias=b, scale=w[:, 3:4]).then_inc(conv_a, 1)
                act.wait_ge(conv_d, cn + 1)
                run_act(tmp[:, 2 + cn % 2, :], tmp[:, cn % 2, :], ACT.Tanh).then_inc(conv_t, 1)

            def evict(u, t):
                j = u.job0 + t
                if u.name in ("X0", "X1", "BC", "QK"):
                    convolve(u, t)
                elif u.name == "Z1":
                    g = u.tag[0]
                    bank, free = tile(j)
                    if g:
                        read_by_pe(("ssd_turn", (g - 1, t)), 0)
                    run_act(z[:, t, :], bank[:, :], ACT.Tanh, scale=0.5).then_inc(z_t, 1)
                elif u.name == "U":
                    k = 2 * u.tag + t
                    bank, free = tile(j)
                    act.wait_ge(pre_x, 12 if k < 4 else 16)
                    run_act(xs_tok[:, k // 4, k % 4, :], bank[:, :], ACT.Copy).then_inc(free, 1)
                elif u.name == "GS":
                    k = 2 * u.tag + t
                    bank, free = tile(j)
                    if k >= 2:
                        act.wait_ge(gate_used, k - 1)
                    link(run_act(tmp[:, k % 2, :], bank[:, :], ACT.Tanh, scale=0.5))
                    act.sem_inc(gate_t, 1)
                elif u.name == "PW":
                    bank, free = tile(j)
                    run_act(v_hi[:, t, :], bank[:, :], ACT.Copy, scale=pc("pool_scale", t, t + 1)).then_inc(pv_hi, 1)
                elif u.name == "GP":
                    k = 2 * u.tag + t
                    bank, free = tile(j)
                    act.wait_ge(pl_lo, KD)
                    run_act(xs_tok[:, k // 4, k % 4, :], bank[:, :], ACT.Tanh, scale=0.5).then_inc(free, 1)
                elif u.name == "BP":
                    k = 2 * u.tag + t
                    act.wait_ge(mx_t, k + 1)
                    if k == 0:
                        act.wait_ge(*units_over(unit_at["PW"][0] + 1))
                    run_act(p_hi[:, k, :], x[:, k, :], ACT.Copy).then_inc(mx_hi, 1)
                elif u.name == "UP":
                    half_, i = u.tag
                    n = FF_HALF * half_ + 2 * i + t
                    k = 2 * i + t
                    bank, free = tile(j)
                    if n >= 2:
                        act.wait_ge(hid_t, n - 1)
                    link(run_act(tmp[:, n % 2, :], bank[:, :], ACT.Relu))
                    act.sem_inc(free, 1)
                    if half_ and k == 0:
                        act.wait_ge(*units_over(unit_at["DN"][7] + 1))
                    run_act(f_hi[:, k, :], tmp[:, n % 2, :], ACT.Square).then_inc(hid_hi, 1)
                elif u.name == "KV":
                    bank, free = tile(j)
                    run_act(va[:, t, :], bank[:, P:2 * P], ACT.Copy).then_inc(kv_ready, 1)
                elif u.name == "V1":
                    bank, free = tile(j)
                    act.wait_ge(col_ready, 1)
                    link(run_act(v1[:, t, :, 0:MD], bank[:, :].rearrange("p (h d) -> p h d", h=MH), ACT.Copy))
                    act.sem_inc(free, 1)
                    act.sem_inc(v_ready, 1)
                elif u.name == "O1":
                    bank, free = tile(j)
                    link(run_act(og[:, t, :], bank[:, :], ACT.Tanh, scale=0.5))
                    act.sem_inc(free, 1)
                    act.sem_inc(og_t, 1)
                elif u.name == "WO":
                    k = 2 * u.tag + t
                    bank, free = tile(j)
                    link(run_act(ysum[:, k, :], bank[:, :], ACT.Copy))
                    act.sem_inc(free, 1)
                    act.sem_inc(ysum_ready, 1)
                elif u.name == "FU":
                    half_, i = u.tag
                    m = G2_HALF * half_ + i
                    col = m + (G2_TILES if t else 0)
                    bank, free = tile(j)
                    if m >= 1:
                        act.wait_ge(hid2_t, m)
                    run_act(tmp[:, t, :], bank[:, :], ACT.Identity, bias=pc("ff_conv_b", col, col + 1),
                            scale=pc("ff_conv_w", 3 * col + 2, 3 * col + 3)).then_inc(gel_a, 1)
                    if t == 0:
                        act.wait_ge(gel_d, 2 * m + 1)
                        run_act(gel[:, :], tmp[:, 0, :], ACT.Gelu_apprx_tanh).then_inc(gel_g, 1)
                    else:
                        act.wait_ge(hid2_t, m + 1)
                        if half_ and i == 0:
                            act.wait_ge(*units_over(unit_at["FD"][7] + 1))
                        run_act(g_hi[:, i, :], tmp[:, 2 + m % 2, :], ACT.Copy).then_inc(hid2_hi, 1)
                elif u.name == "FD" and u.last and u.tag[0] == 0:
                    k = 2 * u.tag[1] + t
                    bank, free = tile(j)
                    link(run_act(ysum[:, k, :], bank[:, :], ACT.Copy))
                    act.sem_inc(free, 1)
                    act.sem_inc(ysum_ready, 1)

            def load_piece(p):
                s, k = p // 8 + 2, p % 8
                src = w_ada if s < 6 else w_ada2
                if p >= 2:
                    act.wait_ge(ada_used, p - 1)
                c0 = ADA_COLS * (s % 6)
                act.dma_start(ada_raw[:, p % 2, :], src[P * k:P * (k + 1), c0:c0 + ADA_COLS]).then_inc(ada_in[p % 2], 16)

            def ada_piece(p, n):
                if p + 1 < 80:
                    load_piece(p + 1)

            def norm(i, n):
                src, _, _, kind = NORMS[i]
                a = x if src == "x" else ysum
                if i == 0:
                    act.wait_ge(x_in_sem, 16)
                elif src == "x":
                    act.wait_ge(x_ready, X_AT[i])
                else:
                    act.wait_ge(ysum_ready, Y_AT[i])
                for k in range(KD):
                    if k >= 2:
                        act.wait_ge(norm_use, (KD - 1) * i + k - 1)
                    run_act(tmp[:, k % 2, :], a[:, k, :], ACT.Square).then_inc(norm_sq, 1)
                bank, free = full(("norm", i), 0)
                run_act(rstd[:, :], bank[:, :], ACT.Sqrt, bias=pc(NORM_EPS_OF[i]), scale=1.0 / D_MODEL).then_inc(norm_rt, 1)
                if kind == "h":
                    m = split_norms.index(i)
                    shift = mod_at(NORMS[i][2])
                    if i:
                        act.wait_ge(*units_over(first_unit_after[i]))
                    for k in range(KD):
                        act.wait_ge(norm_tmp, KD * m + k + 1)
                        run_act(h_hi[:, k, :], tmp[:, 2 + k % 2, :], ACT.Identity, bias=shift[:, k:k + 1]).then_inc(norm_hi, 1)

            def dt_gates(i, n):
                act.wait_ge(dt_x, TC)
                link(run_act(cdec[:, 0, :], pc("a_log"), ACT.Exp))
                link(run_act(edec[:, :, :], dt[:, :, :], ACT.Abs))
                link(run_act(edec[:, :, :], edec[:, :, :], ACT.Exp, scale=-1.0))
                run_act(edec[:, :, :], edec[:, :, :], ACT.Ln, bias=ones[:, 0:1]).then_inc(dt_e, 1)

            def dt_sums(i, n):
                bank, free = full(("dt_sums", 0), 0)
                run_act(cdec[:, :, :].rearrange("p c h -> p (c h)"), bank[:, P:2 * P], ACT.Exp).then_inc(dt_e, 1)
                act.wait_ge(dt_acs, 1)
                run_act(eacs[:, :, :], acs[:, :, :], ACT.Exp)
                run_act(edec[:, :, :], edec[:, :, :], ACT.Exp).then_inc(dt_e, 1)

            def xs_turn(i, n):
                g, t = i
                bank, free = full(("xs_turn", i), 0)
                if g >= 2:
                    act.wait_ge(pre_x, TC * (g - 1))
                link(run_act(xs_tok[:, g % 2, :, P * t:P * (t + 1)], bank[:, :].rearrange("p (c d) -> p c d", c=TC),
                        ACT.Copy))
                act.sem_inc(free, 1)
                act.sem_inc(xs_ready, 1)

            def b_turn(g, n):
                bank, free = full(("b_turn", g), 0)
                if g >= 2:
                    read_by_pe(("ssd_out", (g - 2, TC - 1)), 2)
                link(run_act(b_tok[:, g % 2, :, :], bank[:, :].rearrange("p (c d) -> p c d", c=TC), ACT.Copy))
                act.sem_inc(free, 1)
                act.sem_inc(b_ready, 1)

            def ssd_scores(i, n):
                act.wait_ge(seg, n + 1)
                run_act(decay[:, :, :], decay[:, :, :], ACT.Exp).then_inc(seg_e, 1)

            def ssd_out(i, n):
                g, c = i
                act.wait_ge(y_ready, n + 1)
                if n:
                    act.wait_ge(y_rs, n)
                run_act(sq_out[:, :], z[:, c, :], ACT.Square, accum_out=ss[:, 0:1]).then_inc(y_sq, 1)

            def ssd_turn(i, n):
                g, c = i
                act.wait_ge(yt_t, n + 1)
                if c == 0 and g:
                    act.wait_ge(*units_over(unit_at["Y1"][g - 1] + 1))
                run_act(yt_hi[:, :, chunk(c)], y_turned[:, :, :], ACT.Copy).then_inc(yt_h, 1)

            def window(t, n):
                act.wait_ge(win_ready, t + 1)
                run_act(p_hi[:, t, :], tmp[:, win_slot(t), :], ACT.Copy).then_inc(pl_hi, 1)

            def rope_k(i, n):
                bank, free = full(("rope_k", 0), 0)
                link(run_act(ka[:, :], bank[:, :], ACT.Copy))
                act.sem_inc(free, 1)
                act.sem_inc(ka_ready, 1)

            def rope_q(c, n):
                bank, free = full(("rope_q", c), 0)
                link(run_act(qa[:, c + 1, :, :].rearrange("p t d -> p (t d)"), bank[:, :], ACT.Copy))
                act.sem_inc(free, 1)
                act.sem_inc(qa_ready, 1)

            def att_scores(q, n):
                ks = slice(P, 2 * P) if q < 2 else slice(0, 2 * P)
                act.wait_ge(sm_max, q + 1)
                for j in range(4):
                    run_act(prob[:, j, ks], prob[:, j, ks], ACT.Exp, bias=att[:, 8 + j:9 + j], accum_out=att[:, 12 + j:13 + j])
                run_act(att[:, 16:20], att[:, 16:20], ACT.Exp).then_inc(sm_exp, 1)

            def att_turn(q, n):
                rs_ = 1 if q < 2 else 0
                if q:
                    read_by_pe(("att_out", q - 1), 0)
                for b in range(2):
                    bank, free = full(("att_turn", q), b)
                    link(run_act(prob_t[:, 2 * b:2 * b + 2, rs_:2, :],
                            bank[:, :].rearrange("p (j r t) -> p j r t", j=2, r=2)[:, :, rs_:2, :], ACT.Copy))
                    act.sem_inc(free, 1)
                    act.sem_inc(pt_ready, 1)

            def att_out(q, n):
                if q % 2:
                    i = q // 2
                    act.wait_ge(at_raw, q + 1)
                    read_by_pe(("ml_columns", 0), 0)
                    if i:
                        act.wait_ge(at_rs, i)
                    run_act(quant[:, :], qa[:, i, :, :].rearrange("p t d -> p (t d)"), ACT.Square,
                            accum_out=att[:, 25:26]).then_inc(at_sq, 1)

            def ml_gates(i, n):
                act.wait_ge(mg_x, 1)
                link(run_act(row_e, row_f, ACT.Abs))
                link(run_act(row_e, row_e, ACT.Exp, scale=-1.0))
                run_act(row_e, row_e, ACT.Ln, bias=ones[0:MH, 0:1]).then_inc(mg_e, 1)
                act.wait_ge(mg_x, 2)
                run_act(quant[32:32 + MH, :], row_t, ACT.Exp)
                run_act(dec[0:MH, 0:TC], row_t.rearrange("p (c t) -> p c t", c=TC)[:, :, P - 1], ACT.Exp)
                run_act(quant[64:64 + MH, :], row_z, ACT.Exp)
                run_act(quant[96:96 + MH, :], row_m, ACT.Exp, scale=-1.0).then_inc(mg_s, 1)

            def k_turn(hd, n):
                act.wait_ge(conv_s, 24 + 4 + hd + 1)
                link(run_act(qk[:, 4 + hd, :], qk[:, 4 + hd, :], ACT.Copy, scale=float(MD) ** -0.5))
                act.sem_inc(kt_ready, 1)
                act.wait_ge(col_ready, 1)
                bank, free = full(("k_turn", hd), 0)
                link(run_act(k_tok[:, :, hd, :], bank[:, :].rearrange("p (c d) -> p c d", c=TC), ACT.Copy))
                act.sem_inc(free, 1)
                act.sem_inc(dec_ready, 1)

            def ml_scores(c, n):
                act.wait_ge(ml_u, c + 1)
                run_act(tmp[:, 0, :], tmp[:, 0, :], ACT.Exp).then_inc(ml_e, 1)

            def join(c, n):
                for b in range(2):
                    act.wait_ge(jn_t, 2 * c + b + 1)
                    if c == 0 and b == 0:
                        act.wait_ge(*units_over(unit_at["WO"][0]))
                    run_act(h_hi[:, 4 * b:4 * b + 4, chunk(c)], tmp[:, b, :].rearrange("p (t d) -> p t d", t=4),
                            ACT.Copy).then_inc(jn_hi, 1)

            stages = {"norm": norm, "ada_piece": ada_piece, "dt_gates": dt_gates, "dt_sums": dt_sums, "xs_turn": xs_turn,
                      "b_turn": b_turn, "ssd_scores": ssd_scores, "ssd_out": ssd_out, "ssd_turn": ssd_turn, "window": window,
                      "rope_k": rope_k, "rope_q": rope_q, "att_scores": att_scores, "att_turn": att_turn, "att_out": att_out,
                      "ml_gates": ml_gates, "k_turn": k_turn, "ml_scores": ml_scores, "join": join}
            count = {}

            def run(steps):
                for name, item in steps:
                    n = count.get(name, 0)
                    count[name] = n + 1
                    if name in stages:
                        stages[name](item, n)

            act.wait_ge(par_in, 32)
            run_act(cst[:, :, :].rearrange("p a k -> p (a k)"), par[:, 0:2 * KD],
                    ACT.Tanh, scale=0.5).then_inc(cs_t, 1)
            load_piece(0)
            split_hi(units[0])
            for u in units:
                run(before[u.n])
                if u.n + 1 < len(units):
                    split_hi(units[u.n + 1])
                if u.last:
                    for t in range(u.n_jobs // 2):
                        evict(u, t)
                run(mid[u.n])
                if u.last:
                    for t in range(u.n_jobs // 2, u.n_jobs):
                        evict(u, t)
                run(end[u.n])
            run(last)

        @block.vector
        def _(dve):
            chain = [0]

            def link(ins):
                chain[0] += 1
                ins.then_inc(dve_chain, 1)
                dve.wait_ge(dve_chain, chain[0])

            stt, tt, ts = nc.vector.scalar_tensor_tensor, nc.vector.tensor_tensor, nc.vector.tensor_scalar

            def full(stage, k):
                b, use = bank_use[stage][k]
                dve.wait_ge(aux_full[b], use + 1)
                return aux[b], aux_free[b]

            def tile(j):
                dve.wait_ge(main_full[j % 4], j // 4 + 1)
                return main[j % 4], main_free[j % 4]

            def convolve(u, t):
                cn = conv_at[u.n, t]
                w, _ = conv_par(u, t)
                bank, free = tile(u.job0 + t)
                dve.wait_ge(conv_a, cn + 1)
                acc = tmp[:, cn % 2, :]
                for d in range(1, CONV_W):
                    ins = stt(acc[:, d:SEQ], bank[:, 0:SEQ - d], w[:, 3 - d:4 - d], acc[:, d:SEQ], ALU.mult, ALU.add)
                    if d < CONV_W - 1:
                        link(ins)
                link(ins)
                dve.sem_inc(conv_d, 1)
                dve.sem_inc(free, 1)
                dve.wait_ge(conv_t, cn + 1)
                if u.name == "BC":
                    g = u.tag[0]
                    if g >= 2:
                        full(("ssd_out", (g - 2, TC - 1)), 2)
                    dst = bc[:, g % 2, t, :]
                elif u.name == "QK":
                    dst = qk[:, 2 * u.tag + t, :]
                else:
                    dst = acc
                stt(dst, tmp[:, 2 + cn % 2, :], 1.0, acc, ALU.add, ALU.mult).then_inc(conv_s, 1)

            def rope(src, heads, c, a, b):
                cos = cc("cos", 32 * c, 32 * (c + 1))
                sin = cc("sin", 32 * c, 32 * (c + 1))
                v = src.rearrange("p (n d) -> p n d", d=32)
                tt(a.rearrange("p (n d) -> p n d", d=32), v, each(cos, 2 * heads), ALU.mult)
                return tt(b.rearrange("p (n d) -> p n d", d=32), v, each(sin, 2 * heads), ALU.mult)

            def evict(u, t):
                j = u.job0 + t
                if u.name in ("X0", "X1", "BC", "QK"):
                    convolve(u, t)
                elif u.name == "DT":
                    bank, free = tile(j)
                    link(tt(dt[:, t, :], bank[:, 0:HEADS], pc("dt_bias"), ALU.add))
                    dve.sem_inc(free, 1)
                    dve.sem_inc(dt_x, 1)
                elif u.name == "Z1":
                    bank, free = tile(j)
                    dve.wait_ge(z_t, TC * u.tag[0] + t + 1)
                    link(stt(z[:, t, :], z[:, t, :], 1.0, bank[:, :], ALU.add, ALU.mult))
                    dve.sem_inc(free, 1)
                elif u.name in ("Y0", "Y1"):
                    k = 4 * u.tag[1] + t
                    bank, free = tile(j)
                    if u.tag[0] == 0:
                        nc.vector.tensor_copy(x[:, k, :], bank[:, :]).then_inc(free, 1)
                    else:
                        tt(x[:, k, :], x[:, k, :], bank[:, :], ALU.add).then_inc(free, 1)
                elif u.name == "GS":
                    k = 2 * u.tag + t
                    bank, free = tile(j)
                    dve.wait_ge(gate_t, k + 1)
                    link(stt(x[:, k, :], tmp[:, k % 2, :], 1.0, x[:, k, :], ALU.add, ALU.mult))
                    dve.sem_inc(free, 1)
                    dve.sem_inc(gate_used, 1)
                elif u.name == "PW":
                    bank, free = tile(j)
                    dve.wait_ge(pv_hi, t + 1)
                    link(stt(v_lo[:, t, :], bank[:, :], pc("pool_scale", t, t + 1), v_hi[:, t, :], ALU.mult, ALU.subtract))
                    dve.sem_inc(free, 1)
                    dve.sem_inc(pv_lo, 1)
                elif u.name == "BP":
                    k = 2 * u.tag + t
                    gate = xs_tok[:, k // 4, k % 4, :]
                    bank, free = tile(j)
                    jg = units[unit_at["GP"][0]].job0 + k
                    dve.wait_ge(main_free[jg % 4], jg // 4 + 1)
                    link(stt(gate, gate, 1.0, bank[:, :], ALU.add, ALU.mult))
                    dve.sem_inc(free, 1)
                    link(tt(x[:, k, :], x[:, k, :], gate, ALU.add))
                    dve.sem_inc(mx_t, 1)
                    dve.wait_ge(mx_hi, k + 1)
                    tt(p_lo[:, k, :], x[:, k, :], p_hi[:, k, :], ALU.subtract).then_inc(mx_lo, 1)
                elif u.name == "OUT":
                    k = 2 * u.tag + t
                    bank, free = tile(j)
                    dve.wait_ge(x_back, 16)
                    link(stt(x[:, k, :], bank[:, :], mul[:, 6, k:k + 1], x[:, k, :], ALU.mult, ALU.add))
                    dve.sem_inc(free, 1)
                    dve.sem_inc(x_ready, 1)
                elif u.name == "UP":
                    half_, i = u.tag
                    n = FF_HALF * half_ + 2 * i + t
                    k = 2 * i + t
                    dve.wait_ge(hid_hi, n + 1)
                    link(tt(tmp[:, 2 + n % 2, :], tmp[:, n % 2, :], tmp[:, n % 2, :], ALU.mult))
                    dve.sem_inc(hid_t, 1)
                    tt(f_lo[:, k, :], tmp[:, 2 + n % 2, :], f_hi[:, k, :], ALU.subtract).then_inc(hid_lo, 1)
                elif u.name == "DN":
                    k = 2 * u.tag[1] + t
                    bank, free = tile(j)
                    link(stt(x[:, k, :], bank[:, :], mod_at(5)[:, k:k + 1], x[:, k, :], ALU.mult, ALU.add))
                    dve.sem_inc(free, 1)
                    dve.sem_inc(x_ready, 1)
                elif u.name == "KV":
                    bank, free = tile(j)
                    a, b = tmp[:, 0, 0:P], tmp[:, 1, 0:P]
                    dve.wait_ge(kv_ready, t + 1)
                    link(rope(bank[:, 0:P], AKV, t, a, b))
                    dve.sem_inc(free, 1)
                    v = k_rot[:, t, :].rearrange("p (h s d) -> p h s d", h=AKV, s=2)
                    a, b = (y.rearrange("p (h s d) -> p h s d", h=AKV, s=2) for y in (a, b))
                    tt(v[:, :, 0, :], a[:, :, 0, :], b[:, :, 1, :], ALU.subtract)
                    link(tt(v[:, :, 1, :], a[:, :, 1, :], b[:, :, 0, :], ALU.add))
                    dve.sem_inc(rot_ready, 1)
                elif u.name == "QA1":
                    bank, free = tile(j)
                    a, b = tmp[:, 0, :], tmp[:, 1, :]
                    link(rope(bank[:, :], AH, t, a, b))
                    dve.sem_inc(free, 1)
                    v = hm[:, t, :].rearrange("p (j g s d) -> p g j s d", j=4, g=2, s=2)
                    a, b = (y.rearrange("p (g j s d) -> p g j s d", g=2, j=4, s=2) for y in (a, b))
                    for g in range(2):
                        tt(v[:, g, :, 0, :], a[:, g, :, 0, :], b[:, g, :, 1, :], ALU.subtract)
                        ins = tt(v[:, g, :, 1, :], a[:, g, :, 1, :], b[:, g, :, 0, :], ALU.add)
                    link(ins)
                    dve.sem_inc(rot_ready, 1)
                elif u.name == "GA":
                    bank, free = tile(j)
                    link(ts((row_i, row_f)[t], bank[0:MH, :], pc("gate_b", t, t + 1)[0:MH, :], None, ALU.add))
                    dve.sem_inc(free, 1)
                elif u.name == "FU":
                    half_, i = u.tag
                    m = G2_HALF * half_ + i
                    col = m + (G2_TILES if t else 0)
                    bank, free = tile(j)
                    dve.wait_ge(gel_a, 2 * m + t + 1)
                    acc = tmp[:, t, :]
                    for d in range(1, FF2_CONV):
                        wt = pc("ff_conv_w", 3 * col + 2 - d, 3 * col + 3 - d)
                        link(stt(acc[:, d:SEQ], bank[:, 0:SEQ - d], wt, acc[:, d:SEQ], ALU.mult, ALU.add))
                    dve.sem_inc(free, 1)
                    if t == 0:
                        dve.sem_inc(gel_d, 2)
                    else:
                        dve.wait_ge(gel_g, m + 1)
                        link(tt(tmp[:, 2 + m % 2, :], gel[:, :], acc, ALU.mult))
                        dve.sem_inc(hid2_t, 1)
                        dve.wait_ge(hid2_hi, m + 1)
                        tt(g_lo[:, i, :], tmp[:, 2 + m % 2, :], g_hi[:, i, :], ALU.subtract).then_inc(hid2_lo, 1)
                elif u.name == "FD" and u.tag[0] == 1:
                    k = 2 * u.tag[1] + t
                    bank, free = tile(j)
                    dve.wait_ge(ysum_ready, 16)
                    link(tt(ysum[:, k, :], ysum[:, k, :], bank[:, :], ALU.add))
                    dve.sem_inc(free, 1)
                    dve.sem_inc(ysum_ready, 1)

            def add_piece(s, k, src):
                c = cs[:, s // 6, k:k + 1]
                if k == 0:
                    link(ts(ada_acc[:, :], src, c, None, ALU.mult))
                else:
                    link(stt(ada_acc[:, :], src, c, ada_acc[:, :], ALU.mult, ALU.add))

            def ada_piece(p, n):
                s, k = p // 8 + 2, p % 8
                dve.wait_ge(ada_in[p % 2], 16 * (p // 2 + 1))
                add_piece(s, k, ada_raw[:, p % 2, :])
                dve.sem_inc(ada_used, 1)
                if k == 7:
                    dve.sem_inc(ada_ready, 1)

            MULS = {1: (0, "norm_mix"), 4: (1, "norm_mlp"), 7: (2, "pre_mix"), 8: (3, "post_mix"), 10: (4, "pre_ffn"), 11: (5, "post_ffn")}

            def ada_sum(s, n):
                bank, free = full(("ada_sum", s), 0)
                b = pc("b_ada" if s < 6 else "b_ada2", KD * (s % 6), KD * (s % 6 + 1))
                link(tt(mod_at(s), bank[:, 0:KD], b, ALU.add))
                dve.sem_inc(free, 1)
                if s in (1, 4, 7, 10):
                    link(stt(mul[:, MULS[s][0], :], mod_at(s), 1.0, pc(MULS[s][1]), ALU.add, ALU.mult))
                elif s in (8, 11):
                    link(tt(mul[:, MULS[s][0], :], mod_at(s), pc(MULS[s][1]), ALU.mult))
                elif s == 2:
                    link(ts(mul[:, 6, :], mod_at(s), 0.5, None, ALU.mult))
                dve.sem_inc(mod_ready, 1)

            def norm(i, n):
                src, m_, _, kind = NORMS[i]
                a = x if src == "x" else ysum
                scale = pc("norm_final") if m_ is None else mul[:, m_, :]
                dve.wait_ge(norm_rt, i + 1)
                link(nc.vector.reciprocal(rstd[:, :], rstd[:, :]))
                dve.sem_inc(aux_free["D"], 1)
                if kind == "x":
                    for k in range(KD):
                        stt(x[:, k, :], x[:, k, :], scale[:, k:k + 1], rstd[:, :], ALU.mult, ALU.mult).then_inc(x_ready, 1)
                elif kind == "add":
                    for k in range(KD):
                        link(stt(ysum[:, k, :], ysum[:, k, :], scale[:, k:k + 1], rstd[:, :], ALU.mult, ALU.mult))
                        tt(x[:, k, :], x[:, k, :], ysum[:, k, :], ALU.add).then_inc(x_ready, 1)
                else:
                    m = split_norms.index(i)
                    shift = mod_at(NORMS[i][2])
                    if i:
                        dve.wait_ge(*units_over(first_unit_after[i]))
                    for k in range(KD + 1):
                        if k < KD:
                            if k >= 2:
                                dve.wait_ge(norm_lo, KD * m + k - 1)
                            stt(tmp[:, 2 + k % 2, :], x[:, k, :], scale[:, k:k + 1], rstd[:, :], ALU.mult,
                                ALU.mult).then_inc(norm_tmp, 1)
                        if k:
                            dve.wait_ge(norm_hi, KD * m + k)
                            dve.wait_ge(norm_tmp, KD * m + k)
                            stt(h_lo[:, k - 1, :], tmp[:, 2 + (k - 1) % 2, :], shift[:, k - 1:k], h_hi[:, k - 1, :],
                                ALU.add, ALU.subtract).then_inc(norm_lo, 1)

            def dt_gates(i, n):
                dve.wait_ge(dt_e, 1)
                link(stt(dt[:, :, :], dt[:, :, :], 0.0, edec[:, :, :], ALU.max, ALU.add))
                stt(dta[:, :, :], dt[:, :, :], -1.0, each(cdec[:, 0, :], TC), ALU.mult, ALU.mult).then_inc(dt_s, 1)

            def dt_sums(i, n):
                bank, free = full(("dt_sums", 0), 0)
                dve.wait_ge(dt_e, 2)
                link(nc.vector.tensor_copy(acs[:, :, :].rearrange("p c h -> p (c h)"), bank[:, 0:P]))
                tt(edec[:, :, :].rearrange("p c h -> p (c h)"), bank[:, P:2 * P], acs[:, :, :].rearrange("p c h -> p (c h)"),
                   ALU.subtract).then_inc(dt_acs, 1)
                dve.wait_ge(dt_e, 3)
                link(tt(dtt[:, :, :], dt[:, :, :], edec[:, :, :], ALU.mult))
                dve.sem_inc(free, 1)
                dve.sem_inc(dt_last, 1)

            def ssd_scores(i, n):
                g, c = i
                if n:
                    full(("ssd_out", (g, c - 1) if c else (g - 1, TC - 1)), 0)
                for b in range(2):
                    bank, free = full(("ssd_scores", i), 1 + b)
                    for k in range(4):
                        hd = HG * g + 4 * b + k
                        ins = ts(decay[:, 4 * b + k, :], bank[:, chunk(k)], acs[:, c, hd:hd + 1], 0.0, ALU.subtract, ALU.min)
                    link(ins)
                    dve.sem_inc(free, 1)
                dve.sem_inc(seg, 1)
                bank, free = full(("ssd_scores", i), 0)
                link(tt(sc[:, :], bank[:, 0:P], tri, ALU.mult))
                dve.sem_inc(free, 1)
                dve.wait_ge(seg_e, n + 1)
                tt(decay[:, :, :], decay[:, :, :], each(sc[:, :], HG), ALU.mult).then_inc(mix, 1)

            def ssd_out(i, n):
                g, c = i
                heads = slice(HG * g, HG * (g + 1))

                def by_head(ap):
                    return ap.rearrange("p (h d) -> p h d", h=HG)
                bank_d, free_d = full(("ssd_out", i), 0)
                bank_o, free_o = full(("ssd_out", i), 1)
                bank_s, free_s = full(("ssd_out", i), 2)
                dve.wait_ge(pre_x, n + 1)
                if c:
                    link(tt(by_head(y_part[:, :]), by_head(bank_o[:, :]), over(eacs[:, c, heads], HD), ALU.mult))
                    dve.sem_inc(free_o, 1)
                    if c < TC - 1:
                        link(tt(by_head(state[:, :]), by_head(state[:, :]), over(cdec[:, c, heads], HD), ALU.mult))
                        link(tt(state[:, :], state[:, :], bank_s[:, :], ALU.add))
                    dve.sem_inc(free_s, 1)
                    dve.sem_inc(st_ready, 1)
                    link(tt(y_part[:, :], y_part[:, :], bank_d[:, :], ALU.add))
                    dve.sem_inc(free_d, 1)
                    link(tt(y_part[:, :], y_part[:, :], xdt[:, 2, :], ALU.add))
                else:
                    dve.sem_inc(free_o, 1)
                    link(nc.vector.tensor_copy(state[:, :], bank_s[:, :]))
                    dve.sem_inc(free_s, 1)
                    dve.sem_inc(st_ready, 1)
                    link(tt(y_part[:, :], bank_d[:, :], xdt[:, 2, :], ALU.add))
                    dve.sem_inc(free_d, 1)
                dve.sem_inc(ssd_read, 1)
                link(tt(z[:, c, :], z[:, c, :], y_part[:, :], ALU.mult))
                dve.sem_inc(y_ready, 1)
                dve.wait_ge(y_rs, n + 1)
                link(ts(z[:, c, :], z[:, c, :], ss[:, 2:3], None, ALU.mult))
                dve.sem_inc(y_norm, 1)

            def ssd_turn(i, n):
                g, c = i
                bank, free = full(("ssd_turn", i), 0)
                if n:
                    dve.wait_ge(yt_h, n)
                link(tt(y_turned[:, :, :], bank[:, :].rearrange("p (t d) -> p t d", t=4), over(pc("ssd_norm", 4 * g, 4 * g + 4), P), ALU.mult))
                dve.sem_inc(free, 1)
                dve.sem_inc(yt_t, 1)
                dve.wait_ge(yt_h, n + 1)
                if c == 0 and g:
                    dve.wait_ge(*units_over(unit_at["Y1"][g - 1] + 1))
                link(tt(yt_lo[:, :, chunk(c)], y_turned[:, :, :], yt_hi[:, :, chunk(c)], ALU.subtract))
                dve.sem_inc(yt_l, 1)

            def window(t, n):
                w = POOL_WINDOWS[t // 2]
                if t == 0:
                    j = units[unit_at["U"][3]].job0 + 1
                    for b in range(4):
                        dve.wait_ge(main_free[(j - b) % 4], (j - b) // 4 + 1)
                else:
                    dve.wait_ge(pl_hi, t)
                u = xs_tok[:, t // 4, t % 4, :]
                src, d, slot = u, 1, 0
                while d < w:
                    dst = tmp[:, 2 + slot, :]
                    nc.vector.tensor_copy(dst[:, 0:d], src[:, 0:d])
                    link(tt(dst[:, d:SEQ], src[:, d:SEQ], src[:, 0:SEQ - d], ALU.add))
                    src, d, slot = dst, 2 * d, 1 - slot
                assert 2 + 1 - slot == win_slot(t)
                link(tt(src[:, 0:16], src[:, 0:16], cc("pool_count", 16 * (t // 2), 16 * (t // 2 + 1)), ALU.mult))
                tt(src[:, 0:16], src[:, 0:16], u[:, 0:16], ALU.subtract)
                link(stt(src[:, 16:SEQ], src[:, 16:SEQ], 1.0 / w, u[:, 16:SEQ], ALU.mult, ALU.subtract))
                dve.sem_inc(win_ready, 1)
                dve.wait_ge(pl_hi, t + 1)
                tt(p_lo[:, t, :], src, p_hi[:, t, :], ALU.subtract).then_inc(pl_lo, 1)

            def att_scores(q, n):
                g = q % 2
                ks = slice(P, 2 * P) if q < 2 else slice(0, 2 * P)
                kn = ks.stop - ks.start
                for b in range(2):
                    bank, free = full(("att_scores", q), b)
                    ins = stt(prob[:, 2 * b:2 * b + 2, ks], bank[:, :].rearrange("p (j k) -> p j k", j=2)[:, :, ks],
                              float(AD) ** -0.5, each(cc("band", ks.start, ks.stop), 2), ALU.mult, ALU.add)
                    link(ins)
                    dve.sem_inc(free, 1)
                link(nc.vector.tensor_reduce(att[:, 0:4], prob[:, :, ks], AX_X, ALU.max))
                link(tt(att[:, 4:8], att[:, 0:4], pc("sinks", 4 * g, 4 * g + 4), ALU.max))
                ts(att[:, 8:12], att[:, 4:8], -1.0, None, ALU.mult)
                tt(att[:, 16:20], pc("sinks", 4 * g, 4 * g + 4), att[:, 4:8], ALU.subtract).then_inc(sm_max, 1)

            def att_out(q, n):
                i, g = q // 2, q % 2
                dve.wait_ge(sm_exp, q + 1)
                link(tt(att[:, 20:24], att[:, 12:16], att[:, 16:20], ALU.add))
                link(nc.vector.reciprocal(att[:, 28:32], att[:, 20:24]))
                bank, free = full(("att_out", q), 0)
                o = qa[:, i, :, :].rearrange("p t d -> p (t d)")[:, 2 * P * g:2 * P * (g + 1)]
                link(tt(o.rearrange("p (j d) -> p j d", j=4), bank[:, 0:2 * P].rearrange("p (j d) -> p j d", j=4),
                        over(att[:, 28:32], AD), ALU.mult))
                dve.sem_inc(free, 1)
                dve.sem_inc(at_raw, 1)
                if g:
                    dve.wait_ge(at_rs, i + 1)
                    o = qa[:, i, :, :].rearrange("p t d -> p (t d)")
                    link(ts(o, o, att[:, 27:28], None, ALU.mult))
                    dve.sem_inc(at_out, 1)

            def ml_gates(i, n):
                scan = nc.vector.tensor_tensor_scan
                nc.vector.memset(quant[:, :], 0.0)
                nc.vector.memset(cell[:, :, :], 0.0)
                link(nc.vector.memset(row_z, 0.0))
                dve.sem_inc(mg_x, 1)
                dve.wait_ge(mg_e, 1)
                link(stt(row_f, row_f, 0.0, row_e, ALU.min, ALU.subtract))
                for c in range(TC):
                    scan(row_b[:, chunk(c)], row_f[:, chunk(c)], row_z[:, chunk(c)], 0.0, ALU.add, ALU.add)
                link(scan(row_m, row_f, row_i, 0.0, ALU.add, ALU.max))
                tt(urow[0:MH, :], row_b, row_m, ALU.subtract)
                link(tt(quant[0:MH, :], row_i, row_b, ALU.subtract))
                for c in range(TC):
                    m_prev = 0.0 if c == 0 else row_m[:, P * c - 1:P * c]
                    ts(row_t[:, chunk(c)], urow[0:MH, chunk(c)], m_prev, None, ALU.add)
                    ins = ts(row_z[:, chunk(c)], quant[0:MH, chunk(c)], urow[0:MH, P * (c + 1) - 1:P * (c + 1)], None, ALU.add)
                ins.then_inc(mg_x, 1)

            def ml_columns(i, n):
                bank, free = full(("ml_columns", 0), 0)
                link(nc.vector.tensor_copy(qcol[:, :, :].rearrange("p c t -> p (c t)"), bank[:, :]))
                dve.sem_inc(free, 1)
                bank, free = full(("ml_columns", 0), 1)
                link(nc.vector.tensor_copy(decb[:, :], bank[:, 0:MH * TC]))
                dve.sem_inc(free, 1)
                nc.vector.memset(v1[:, :, :, MD:MD + 1], 1.0).then_inc(col_ready, 1)
                dve.sem_inc(ml_cell, 1)

            def flat_tmp(a, n):
                return tmp[:, :, :].rearrange("p a b -> p (a b)")[:, a:a + n]

            W = MD + 1

            def ml_scores(c, n):
                bank_s, free_s = full(("ml_scores", c), 0)
                bank_u, free_u = full(("ml_scores", c), 1)
                for hd in range(MH):
                    ins = ts(tmp[:, 0, chunk(hd)], bank_u[:, chunk(hd)], qcol[:, c, hd:hd + 1], 0.0, ALU.add, ALU.min)
                link(ins)
                dve.sem_inc(free_u, 1)
                dve.sem_inc(ml_u, 1)
                dve.wait_ge(ml_e, c + 1)
                pp = tmp[:, 0, :].rearrange("p (h t) -> p h t", h=MH)
                link(tt(pp, pp, each(tri, MH), ALU.mult))
                link(tt(tmp[:, 0, :], tmp[:, 0, :], bank_s[:, :], ALU.mult))
                dve.sem_inc(free_s, 1)
                dve.sem_inc(ml_p, 1)
                dve.wait_ge(v_ready, TC)
                vw = flat_tmp(SEQ, MH * W).rearrange("p (h d) -> p h d", h=MH)
                tt(vw, v1[:, c, :, :], over(qcol[:, c, 64:64 + MH], W), ALU.mult).then_inc(ml_vw, 1)

            def ml_out_(c, n):
                part = flat_tmp(SEQ + MH * W, 2 * W).rearrange("p (h d) -> p h d", h=2)
                tot = flat_tmp(SEQ + MH * W + 2 * W, MH * W).rearrange("p (h d) -> p h d", h=MH)
                for b in range(2):
                    bank, free = full(("ml_out", c), b)
                    bank2, free2 = full(("ml_out", c), 2 + b)
                    link(tt(part, bank2[:, 0:2 * W].rearrange("p (h d) -> p h d", h=2),
                            over(qcol[:, c, 32 + 2 * b:34 + 2 * b], W), ALU.mult))
                    dve.sem_inc(free2, 1)
                    link(tt(tot[:, 2 * b:2 * b + 2, :], part, bank[:, 0:2 * W].rearrange("p (h d) -> p h d", h=2), ALU.add))
                    dve.sem_inc(free, 1)
                dec_c = decb[:, :].rearrange("p (h c) -> p h c", h=MH)[:, :, c]
                for b in range(2):
                    full(("ml_out", c), 4 + b)
                link(tt(cell[:, :, :], cell[:, :, :], over(dec_c, W), ALU.mult))
                for b in range(2):
                    bank, free = full(("ml_out", c), 4 + b)
                    v = cell[:, 2 * b:2 * b + 2, :]
                    link(tt(v, v, bank[:, 0:2 * W].rearrange("p (h d) -> p h d", h=2), ALU.add))
                    dve.sem_inc(free, 1)
                dve.sem_inc(ml_cell, 1)
                den = tot[:, :, MD]
                link(ts(small[:, 12:16], den, -1.0, None, ALU.mult))
                link(tt(small[:, 12:16], small[:, 12:16], den, ALU.max))
                link(tt(small[:, 12:16], small[:, 12:16], qcol[:, c, 96:96 + MH], ALU.max))
                link(nc.vector.reciprocal(small[:, 16:20], small[:, 12:16]))
                hv = hm[:, c, :].rearrange("p (h d) -> p h d", h=MH)
                link(tt(hv, tot[:, :, 0:MD], over(small[:, 16:20], MD), ALU.mult))
                link(tt(tmp[:, 0, :], hm[:, c, :], hm[:, c, :], ALU.mult))
                nc.vector.tensor_reduce(small[:, 0:4], tmp[:, 0, :].rearrange("p (h d) -> p h d", h=MH), AX_X, ALU.add).then_inc(ml_sq, 1)
                dve.wait_ge(ml_rs, c + 1)
                link(tt(hv, hv, over(small[:, 8:12], MD), ALU.mult))

            def join(c, n):
                dve.wait_ge(og_t, TC)
                stt(hm[:, c, :], og[:, c, :], 1.0, hm[:, c, :], ALU.add, ALU.mult).then_inc(ml_out, 1)
                for b in range(2):
                    bank, free = full(("join", c), b)
                    if c:
                        dve.wait_ge(jn_hi, 2 * c - 1 + b)
                    col = mn_half if b == 0 else pc("attn_norm")
                    v = tmp[:, b, :].rearrange("p (t d) -> p t d", t=4)
                    link(tt(v, bank[:, :].rearrange("p (t d) -> p t d", t=4), over(col, P), ALU.mult))
                    dve.sem_inc(free, 1)
                    dve.sem_inc(jn_t, 1)
                    dve.wait_ge(jn_hi, 2 * c + b + 1)
                    tt(h_lo[:, 4 * b:4 * b + 4, chunk(c)], v, h_hi[:, 4 * b:4 * b + 4, chunk(c)], ALU.subtract).then_inc(jn_lo, 1)

            stages = {"norm": norm, "ada_piece": ada_piece, "ada_sum": ada_sum, "dt_gates": dt_gates, "dt_sums": dt_sums,
                      "ssd_scores": ssd_scores, "ssd_out": ssd_out, "ssd_turn": ssd_turn, "window": window,
                      "att_scores": att_scores, "att_out": att_out, "ml_gates": ml_gates, "ml_columns": ml_columns,
                      "ml_scores": ml_scores, "ml_out": ml_out_, "join": join}
            count = {}

            def run(steps):
                for name, item in steps:
                    n = count.get(name, 0)
                    count[name] = n + 1
                    if name in stages:
                        stages[name](item, n)

            dve.wait_ge(par_in, 32)
            ts(cw_half, pc("conv_w"), 0.5, None, ALU.mult)
            ts(cb_half, pc("conv_b"), 0.5, None, ALU.mult)
            ts(mw_half, pc("ml_conv_w"), 0.5, None, ALU.mult)
            ts(mb_half, pc("ml_conv_b"), 0.5, None, ALU.mult)
            ts(mn_half, pc("ml_norm"), 0.5, None, ALU.mult)
            dve.wait_ge(cs_t, 1)
            csf = cs[:, :, :].rearrange("p a k -> p (a k)")
            link(stt(csf, cst[:, :, :].rearrange("p a k -> p (a k)"), 1.0, par[:, 0:2 * KD], ALU.add, ALU.mult))
            link(ts(csf, csf, 0.5, None, ALU.mult))
            for n, s in enumerate((0, 1)):
                dve.wait_ge(first_in[s], 16 * KD)
                for k in range(KD):
                    add_piece(s, k, ada_first[:, KD * s + k, :])
                dve.sem_inc(ada_ready, 1)
                ada_sum(s, n)
            for u in units:
                run(before[u.n])
                if u.last:
                    for t in range(u.n_jobs // 2):
                        evict(u, t)
                run(mid[u.n])
                if u.last:
                    for t in range(u.n_jobs // 2, u.n_jobs):
                        evict(u, t)
                run(end[u.n])
            run(last)


def pack_weights(inputs):
    units = plan_units()
    out = np.zeros((len(units), P, SLOT), np.float32)
    for u in units:
        w = np.asarray(inputs[u.weight])[0]
        w = w.reshape(-1, w.shape[-1])
        at = 0
        view = out[u.n, :, :u.kn * u.cols].reshape(P, u.kn, u.cols)
        rows = w[P * u.k0:P * (u.k0 + u.kn)].reshape(u.kn, P, -1).transpose(1, 0, 2)
        for c0, n, pad in u.segs:
            view[:, :, at:at + n] = rows[:, :, c0:c0 + n]
            at += n + pad
    return out


def columns(v):
    return np.asarray(v).reshape(-1, P).T


def pack_params(inputs):
    out = np.zeros((P, N_PARAM), np.float32)

    def put(name, value):
        at, n = PARAM_AT[name]
        out[:, at:at + n] = value

    for name, source in (("c", "c"), ("c2", "c_2"), ("b_ada", "b_ada"), ("b_ada2", "b_ada_2"), ("norm_mix", "norm_mix_w"),
                         ("norm_mlp", "norm_mlp_w"), ("norm_final", "norm_final_w"), ("conv_b", "conv_b"),
                         ("ssd_norm", "ssd_norm_w"), ("pool_scale", "pool_scale"), ("pre_mix", "pre_mix_g_2"),
                         ("post_mix", "post_mix_g_2"), ("pre_ffn", "pre_ffn_g_2"), ("post_ffn", "post_ffn_g_2"),
                         ("ml_conv_b", "ml_conv_b_2"), ("ml_norm", "ml_norm_g_2"), ("attn_norm", "attn_norm_g_2"),
                         ("ff_conv_b", "ffn_conv_b_2")):
        put(name, columns(inputs[source]))
    for name, source in (("conv_w", "conv_w"), ("ml_conv_w", "ml_conv_w_2"), ("ff_conv_w", "ffn_conv_w_2")):
        w = np.asarray(inputs[source])[0]
        put(name, w.reshape(w.shape[0], -1, P).transpose(2, 1, 0).reshape(P, -1))
    for name, source in (("dt_bias", "dt_bias"), ("a_log", "a_log"), ("d_skip", "d_skip"), ("sinks", "attn_sinks_2")):
        put(name, np.broadcast_to(np.asarray(inputs[source]).reshape(1, -1), (P, PARAM_AT[name][1])))
    at, _ = PARAM_AT["gate_b"]
    out[0:MH, at] = np.asarray(inputs["ml_i_b_2"])[0]
    out[0:MH, at + 1] = np.asarray(inputs["ml_f_b_2"])[0]
    put("eps1", NORM_EPS)
    put("eps2", RMS_EPS)
    return out


def kernel(**inputs):
    import concourse.bacc as bacc
    from concourse.bass_utils import run_bass_kernel_spmd

    nc = bacc.Bacc("TRN2", target_bir_lowering=False, num_devices=1)
    x = np.asarray(inputs["x"])[0]
    arrays = {
        "stream": pack_weights(inputs),
        "w_ada": np.ascontiguousarray(np.asarray(inputs["w_ada"])[0]),
        "w_ada2": np.ascontiguousarray(np.asarray(inputs["w_ada_2"])[0]),
        "x_in": np.ascontiguousarray(x.T.reshape(KD, P, SEQ).transpose(1, 0, 2)),
        "params": pack_params(inputs),
        "consts": constants(),
    }
    args = [nc.dram_tensor(name, a.shape, F32, kind="ExternalInput").ap() for name, a in arrays.items()]
    out = nc.dram_tensor("out", (P, KD, SEQ), F32, kind="ExternalOutput").ap()
    build(nc, *args, out)
    r = run_bass_kernel_spmd(nc, [arrays], core_ids=[0])
    y = np.asarray(r.results[0]["out"])
    return np.ascontiguousarray(y.transpose(1, 0, 2).reshape(D_MODEL, SEQ).T)[None]
```

```python
from contextlib import ExitStack

import numpy as np

import concourse.bass as bass
from concourse import mybir

F32 = mybir.dt.float32
F32R = mybir.dt.float32r
ALU = mybir.AluOpType
ACT = mybir.ActivationFunctionType
AX_X = mybir.AxisListType.X

P = 128
D_MODEL = 1024
SEQ = 512
KD = D_MODEL // P
TC = SEQ // P
D_INNER = 2 * D_MODEL
HEADS = 32
GROUPS = 4
HG = HEADS // GROUPS
HD = D_INNER // HEADS
GW = D_INNER // GROUPS
STATE = 128
CONV_W = 4
POOL_WINDOWS = (2, 4, 8, 16)
XBC0 = D_INNER
B0 = XBC0 + D_INNER
C0 = B0 + GROUPS * STATE
DT0 = C0 + GROUPS * STATE
U0 = DT0 + HEADS
GATE0 = U0 + D_MODEL
D_FF = 4 * D_MODEL
FF_HALF = D_FF // P // 2
MH = 4
MD = 128
MW = MH * MD
AH = 8
AD = 64
AKV = 2
D_FF_2 = 2816
G2_TILES = D_FF_2 // P
G2_HALF = G2_TILES // 2
FF2_CONV = 3
GATES2 = 4 * MW
QA2 = GATES2 + 2 * MH
KV2 = QA2 + AH * AD
NORM_EPS = 1e-5
RMS_EPS = 1e-6
MASKED = -1.0e30

SLOT = 2048
ADA_COLS = D_MODEL


class Unit:

    def __init__(self, name, weight, k0, kn, segs, act, ak0=0, token_major=False, first=True, last=True, tag=None):
        self.name, self.weight, self.k0, self.kn, self.segs = name, weight, k0, kn, segs
        self.act, self.ak0, self.token_major, self.first, self.last = act, ak0, token_major, first, last
        self.cols = sum(w + pad for _, w, pad in segs)
        self.tag = tag
        self.n_jobs = TC if token_major else (8 if act == "pool" else -(-self.cols // P))
        assert kn * self.cols <= SLOT


def plan_units():
    u = [Unit("DT", "w_in", 0, KD, [(DT0, HEADS, 0)], "h")]

    def branch(g):
        return [Unit(f"Y{i}", "w_branch_ssd", 4 * g, 4, [(512 * i, 512, 0)], "yT", tag=(g, i)) for i in range(2)]

    for g in range(GROUPS):
        x0 = XBC0 + GW * g
        u += [Unit(f"X{i}", "w_in", 0, KD, [(x0 + 256 * i, 256, 0)], "h", tag=(g, i)) for i in range(2)]
        u += [Unit("BC", "w_in", 0, KD, [(B0 + STATE * g, STATE, 0), (C0 + STATE * g, STATE, 0)], "h", tag=(g, 0))]
        u += [Unit(f"Z{i}", "w_in", 4 * i, 4, [(GW * g, GW, 0)], "h", ak0=4 * i, token_major=True,
                   first=(i == 0), last=(i == 1), tag=(g, i)) for i in range(2)]
        if g:
            u += branch(g - 1)
    u += [Unit("U", "w_in", 0, KD, [(U0 + 256 * i, 256, 0)], "h", tag=i) for i in range(4)]
    u += branch(GROUPS - 1)
    u += [Unit("GS", "w_in", 0, KD, [(GATE0 + 256 * i, 256, 0)], "h", tag=i) for i in range(4)]
    u += [Unit("PW", "pool_w", 0, KD, [(0, 256, 0)], "pool")]
    u += [Unit("GP", "w_in", 0, KD, [(GATE0 + D_MODEL + 256 * i, 256, 0)], "h", tag=i) for i in range(4)]
    u += [Unit("BP", "w_branch_pool", 0, KD, [(256 * i, 256, 0)], "pv", tag=i) for i in range(4)]
    u += [Unit("OUT", "w_out", 0, KD, [(256 * i, 256, 0)], "mixed", tag=i) for i in range(4)]
    for half in range(2):
        u += [Unit("UP", "w_up", 0, KD, [(256 * (8 * half + i), 256, 0)], "h", tag=(half, i)) for i in range(8)]
        u += [Unit("DN", "w_down", FF_HALF * half + 8 * j, 8, [(256 * i, 256, 0)], "hidden", ak0=8 * j,
                   first=(j == 0), last=(j == 1), tag=(half, i)) for i in range(4) for j in range(2)]
    u += [Unit("KV", "w_in_2", 0, KD, [(KV2, 256, 0)], "h", token_major=True)]
    u += [Unit(f"QA{i}", "w_in_2", 4 * i, 4, [(QA2, 512, 0)], "h", ak0=4 * i, token_major=True,
               first=(i == 0), last=(i == 1)) for i in range(2)]
    u += [Unit("GA", "w_in_2", 0, KD, [(GATES2, MH, P - MH), (GATES2 + MH, MH, P - MH)], "h")]
    u += [Unit("QK", "w_in_2", 0, KD, [(256 * i, 256, 0)], "h", tag=i) for i in range(4)]
    u += [Unit(f"V{i}", "w_in_2", 4 * i, 4, [(2 * MW, MW, 0)], "h", ak0=4 * i, token_major=True,
               first=(i == 0), last=(i == 1)) for i in range(2)]
    u += [Unit(f"O{i}", "w_in_2", 4 * i, 4, [(3 * MW, MW, 0)], "h", ak0=4 * i, token_major=True,
               first=(i == 0), last=(i == 1)) for i in range(2)]
    u += [Unit("WO", "w_out_2", 0, KD, [(256 * i, 256, 0)], "h", tag=i) for i in range(4)]
    for half in range(2):
        u += [Unit("FU", "w_up_2", 0, KD, [(P * (G2_HALF * half + i), P, 0), (D_FF_2 + P * (G2_HALF * half + i), P, 0)],
                   "h", tag=(half, i)) for i in range(G2_HALF)]
        u += [Unit("FD", "w_down_2", G2_HALF * half + 6 * j, (6, G2_HALF - 6)[j], [(256 * i, 256, 0)], "hidden2",
                   ak0=6 * j, first=(j == 0), last=(j == 1), tag=(half, i)) for i in range(4) for j in range(2)]
    job = 0
    for n, x in enumerate(u):
        if not x.first:
            job -= x.n_jobs
        x.n, x.job0 = n, job
        job += x.n_jobs
    return u


PARAMS = [("c", KD), ("c2", KD), ("b_ada", 48), ("b_ada2", 48), ("norm_mix", KD), ("norm_mlp", KD), ("norm_final", KD),
          ("conv_w", 24 * CONV_W), ("conv_b", 24), ("ssd_norm", 16), ("pool_scale", KD),
          ("dt_bias", HEADS), ("a_log", HEADS), ("d_skip", HEADS),
          ("pre_mix", KD), ("post_mix", KD), ("pre_ffn", KD), ("post_ffn", KD),
          ("ml_conv_w", 8 * CONV_W), ("ml_conv_b", 8), ("ml_norm", MH), ("attn_norm", 4), ("sinks", AH),
          ("ff_conv_w", 2 * G2_TILES * FF2_CONV), ("ff_conv_b", 2 * G2_TILES), ("gate_b", 2),
          ("eps1", 1), ("eps2", 1)]
CONSTS = [("ident", P), ("tri", P), ("ones", P), ("band", 2 * P), ("cos", TC * 32), ("sin", TC * 32),
          ("pool_count", 4 * 16)]


def offsets(blocks):
    at, out = 0, {}
    for name, n in blocks:
        out[name] = (at, n)
        at += n
    return out, at


PARAM_AT, N_PARAM = offsets(PARAMS)
CONST_AT, N_CONST = offsets(CONSTS)


def constants():
    out = np.zeros((P, N_CONST), np.float32)

    def put(name, value):
        at, n = CONST_AT[name]
        out[:, at:at + n] = np.asarray(value, np.float32).reshape(P, n)

    p, f = np.arange(P)[:, None], np.arange(P)[None, :]
    put("ident", p == f)
    put("tri", p <= f)
    put("ones", np.ones((P, P)))
    key = np.arange(2 * P)[None, :]
    rel = p + P - key
    put("band", np.where((rel >= 0) & (rel < P), 0.0, MASKED))
    half = AD // 2
    inv = np.float32(10000.0) ** (-np.arange(half, dtype=np.float32) / np.float32(half))
    ang = np.arange(SEQ, dtype=np.float32)[:, None] * inv.astype(np.float32)[None, :]
    put("cos", np.cos(ang).reshape(TC, P, half).transpose(1, 0, 2))
    put("sin", np.sin(ang).reshape(TC, P, half).transpose(1, 0, 2))
    t = np.arange(1, 17)
    put("pool_count", np.broadcast_to(np.stack([1.0 / np.minimum(t, w) for w in POOL_WINDOWS])[None], (P, 4, 16)))
    return out


def plan_steps(units):
    before, mid, end = ({u.n: [] for u in units} for _ in range(3))
    at = {}
    for u in units:
        at.setdefault(u.name, []).append(u.n)

    def find(name, g=0):
        return at[name][g]

    def square_sums(norm, units_of):
        for pair, n in enumerate(units_of[:-1]):
            mid[n + 1].append(("sumsq", (norm, pair)))
        return [("sumsq", (norm, KD // 2 - 1))]

    def all_sums(norm):
        return [("sumsq", (norm, pair)) for pair in range(KD // 2)]

    before[0] += all_sums(0) + [("norm", 0)]
    mid[find("X0")] += [("dt_turn", 0), ("dt_gates", 0)]
    mid[find("X1")] += [("dt_sums", 0)]
    for g in range(GROUPS):
        for t in range(4):
            (end, mid)[t % 2][find("X0", g) + (t + 1) // 2].append(("xs_turn", (g, t)))
        end[find("BC", g)] += [("silu", g)]
        end[find("Z0", g)] += [("b_turn", g)]
    for g in range(GROUPS):
        n = find("Z1", g)
        for i in range(TC):
            end[n + i].append(("ssd_scores", (g, i)))
            end[n + i + 1].append(("ssd_out", (g, i)))
            mid[n + i + 2].append(("ssd_turn", (g, i)))
    n = at["U"][3]
    for t in range(KD):
        (end, mid)[t % 2][n + (t + 1) // 2].append(("window", t))
    before[at["UP"][0]] += square_sums(1, at["OUT"]) + [("norm", 1)]
    before[at["KV"][0]] += square_sums(2, at["DN"][9::2]) + [("norm", 2)] + all_sums(3) + [("norm", 3)]
    mid[at["QA0"][0]] += [("rope_k", 0)]
    mid[at["GA"][0]] += [("rope_q", 0), ("rope_q", 1)]
    end[at["GA"][0]] += [("rope_q", 2), ("rope_q", 3), ("ml_gates", 0)]
    mid[at["QK"][1]] += [("ml_columns", 0)]
    for hd in range(MH):
        (end, mid)[hd % 2][at["QK"][3] + (hd + 1) // 2].append(("k_turn", hd))
    n = at["GA"][0]
    for q in range(2 * TC):
        end[n + q + 1].append(("att_out", q))
    for q in range(2 * TC):
        mid[n + q + 1].append(("att_turn", q))
        end[n + q].append(("att_scores", q))
    end[at["V1"][0]] += [("ml_scores", 0)]
    mid[at["O0"][0]] += [("ml_out", 0), ("ml_scores", 1)]
    end[at["O0"][0]] += [("ml_out", 1), ("ml_scores", 2)]
    mid[at["O1"][0]] += [("ml_out", 2), ("ml_scores", 3)]
    before[at["WO"][0]] += [("ml_out", 3)] + [("join", c) for c in range(TC)]
    before[at["FU"][0]] += square_sums(4, at["WO"]) + [("norm", 4)] + all_sums(5) + [("norm", 5)]
    last = square_sums(6, at["FD"][9::2]) + [("norm", 6)]
    for p in range(80):
        mid[1 + p].append(("ada_piece", p))
        if p % 8 == 7:
            end[1 + p].append(("ada_sum", p // 8 + 2))
    rank = ["silu", "b_turn", "ssd_out", "ssd_scores", "xs_turn", "ssd_turn"]
    for steps in (*mid.values(), *end.values()):
        steps.sort(key=lambda s: rank.index(s[0]) if s[0] in rank else len(rank))
    order = [s for u in units for s in before[u.n] + mid[u.n] + end[u.n]] + last
    return before, mid, end, last, order


BANKS_OF = {"ada_sum": "B", "dt_turn": "A", "dt_sums": "A", "b_turn": "A", "ssd_scores": "ABC",
            "ssd_out": "DBC", "ssd_turn": "A", "rope_k": "A", "rope_q": "A", "ml_columns": "AD", "k_turn": "A",
            "att_scores": "BC", "att_turn": "BC", "att_out": "D", "ml_scores": "BC", "ml_out": "DBACAC",
            "join": "AB"}


SPREAD = (1, 2, 4, 6)


def sum_stage(i):
    return i, KD // 2 - 1 if i in SPREAD else 0


def build(nc, stream, w_ada, w_ada2, x_in, params_in, consts_in, out):
    units = plan_units()
    before, mid, end, last, order = plan_steps(units)
    bank_use, used = {}, {b: 0 for b in "ABCD"}
    for stage in before[0][:4] + [("ada_sum", 1), ("ada_sum", 0)] + [s for s in order if s not in before[0][:4]]:
        bank_use[stage] = []
        name, item = stage
        if name == "xs_turn":
            banks = "DB"[item[1] % 2]
        elif name == "sumsq":
            banks = "D" if item == sum_stage(item[0]) else ""
        else:
            banks = BANKS_OF.get(name, "")
        for b in banks:
            bank_use[stage].append((b, used[b]))
            used[b] += 1
    conv_units = [u for u in units if u.name in ("X0", "X1", "BC", "QK")]
    conv_at = {(u.n, t): 2 * i + t for i, u in enumerate(conv_units) for t in range(2)}
    unit_at = {}
    for u in units:
        unit_at.setdefault(u.name, []).append(u.n)

    with ExitStack() as ctx:
        def alloc(stack, name, shape, dt=F32):
            return stack.enter_context(nc.sbuf_tensor(name, [P] + list(shape), dt))

        x = alloc(ctx, "x", [KD, SEQ])
        h_hi, h_lo = (alloc(ctx, f"h_{s}", [KD, SEQ], F32R) for s in ("hi", "lo"))
        raw = alloc(ctx, "raw", [2, SLOT])
        w_hi, w_lo = (alloc(ctx, f"w_{s}", [2, SLOT], F32R) for s in ("hi", "lo"))
        par = alloc(ctx, "par", [N_PARAM])
        con = alloc(ctx, "con", [N_CONST])
        mod = alloc(ctx, "mod", [12 * KD])
        mul = alloc(ctx, "mul", [8, KD])
        half = alloc(ctx, "half", [24 * CONV_W + 24 + 8 * CONV_W + 8 + MH])
        cs = alloc(ctx, "cs", [2, KD])
        cst = alloc(ctx, "cst", [2, KD])
        ada_raw = alloc(ctx, "ada_raw", [2, ADA_COLS])
        ada_acc = alloc(ctx, "ada_acc", [ADA_COLS])
        tmp = alloc(ctx, "tmp", [4, SEQ])
        small = alloc(ctx, "small", [64])

        rstd = alloc(ctx, "rstd", [SEQ])
        with ExitStack() as s0:
            ada_first = alloc(s0, "ada_first", [2 * KD, ADA_COLS])
        with ExitStack() as s1:
            xs_tok = alloc(s1, "xs_tok", [2, TC, GW])
            with ExitStack() as s2:
                z = alloc(s2, "z", [TC, GW])
                bc = alloc(s2, "bc", [2, 2, SEQ])
                b_tok = alloc(s2, "b_tok", [2, TC, STATE])
                y_part = alloc(s2, "y_part", [GW])
                y_turned = alloc(s2, "y_turned", [4, P])
                xdt = alloc(s2, "xdt", [3, GW])
                decay = alloc(s2, "decay", [HG, P])
                sc = alloc(s2, "sc", [P])
                state = alloc(s2, "state", [GW])
                dt, dta, acs, eacs, edec, cdec, dtt = (alloc(s2, n, [TC, HEADS]) for n in
                                                       ("dt", "dta", "acs", "eacs", "edec", "cdec", "dtt"))
                ss = alloc(s2, "ss", [4])
                sq_out = alloc(s2, "sq_out", [GW])
                yt_hi, yt_lo = (alloc(s2, f"yt_{s}", [4, SEQ], F32R) for s in ("hi", "lo"))
            with ExitStack() as s3:
                p_hi, p_lo, v_hi, v_lo = (alloc(s3, n, [KD, SEQ], F32R) for n in ("p_hi", "p_lo", "v_hi", "v_lo"))
        with ExitStack() as s4:
            f_hi, f_lo = (alloc(s4, n, [FF_HALF, SEQ], F32R) for n in ("f_hi", "f_lo"))
        with ExitStack() as s5:
            qk = alloc(s5, "qk", [8, SEQ])
            v1 = alloc(s5, "v1", [TC, MH, MD + 1])
            k_tok = alloc(s5, "k_tok", [TC, MH, MD])
            og = alloc(s5, "og", [TC, MW])
            hm = alloc(s5, "hm", [TC, MW])
            qa = alloc(s5, "qa", [TC + 1, 4, P])
            ka = alloc(s5, "ka", [SEQ])
            k_rot = alloc(s5, "k_rot", [TC, P])
            va = alloc(s5, "va", [TC, P])
            prob = alloc(s5, "prob", [4, 2 * P])
            prob_t = alloc(s5, "prob_t", [4, 2, P])
            cell = alloc(s5, "cell", [MH, MD + 1])
            quant = alloc(s5, "quant", [SEQ])
            qcol = alloc(s5, "qcol", [TC, P])
            urow = alloc(s5, "urow", [SEQ])
            dec = alloc(s5, "dec", [MH * TC])
            att = alloc(s5, "att", [32])
            decb = alloc(s5, "decb", [MH * TC])
        with ExitStack() as s6:
            g_hi, g_lo = (alloc(s6, n, [G2_HALF, SEQ], F32R) for n in ("g_hi", "g_lo"))
            gel = alloc(s6, "gel", [SEQ])
        with ExitStack() as s7:
            s7.enter_context(nc.sbuf_tensor("skip7", [P, 2 * G2_HALF * SEQ + SEQ], F32))
            ysum = alloc(s7, "ysum", [KD, SEQ])

        main = [ctx.enter_context(nc.psum_tensor(f"main{i}", [P, SEQ], F32)) for i in range(4)]
        aux = {b: ctx.enter_context(nc.psum_tensor(f"aux{b}", [P, SEQ], F32)) for b in "ABCD"}

        def sem(name):
            return ctx.enter_context(nc.semaphore(name))

        main_full = [sem(f"main_full{i}") for i in range(4)]
        main_free = [sem(f"main_free{i}") for i in range(4)]
        aux_full = {b: sem(f"aux_full{b}") for b in "ABCD"}
        aux_free = {b: sem(f"aux_free{b}") for b in "ABCD"}
        raw_in = [sem(f"raw_in{i}") for i in range(2)]
        ada_in = [sem(f"ada_in{i}") for i in range(2)]
        first_in = [sem(f"first_in{i}") for i in range(KD)]
        (par_in, x_in_sem, hi_done, lo_done, unit_done, dve_chain, act_chain, pool_chain, ada_used, conv_a,
         conv_d, conv_t, conv_s, turned, x_ready, ysum_ready, norm_sq, norm_use, norm_add, norm_rt, norm_tmp,
         norm_hi, norm_lo, cs_t, dt_f, dt_x, dt_e, dt_s, dt_acs, dt_last, seg, seg_e, mix, pre_x, y_ready,
         y_sq, y_rs, y_norm, yt_h, yt_t, yt_l, z_t, xs_ready, b_ready, st_ready, ssd_read, gate_t, gate_used,
         win_ready, pl_hi, pl_lo, pv_hi, pv_lo, mx_t, mx_hi, mx_lo, x_back, hid_t, hid_hi, hid_lo, gel_a,
         gel_d, gel_g, hid2_t, hid2_hi, hid2_lo, kv_ready, rot_ready, qa_ready, ka_ready, sm_max, sm_exp,
         pt_ready, at_rs, at_sq, at_out, mg_x, mg_e, mg_s, col_ready, dec_ready, kt_ready, v_ready, ml_u,
         ml_e, ml_p, ml_vw, ml_cell, ml_out, ml_sq, ml_rs, og_t, jn_t, jn_hi, jn_lo, out_done, ada_ready,
         mod_ready, at_raw) = [
            sem(n) for n in (
                "par_in x_in_sem hi_done lo_done unit_done dve_chain act_chain pool_chain ada_used conv_a conv_d "
                "conv_t conv_s turned x_ready ysum_ready norm_sq norm_use norm_add norm_rt norm_tmp norm_hi norm_lo "
                "cs_t dt_f dt_x dt_e dt_s dt_acs dt_last seg seg_e mix pre_x y_ready y_sq y_rs y_norm yt_h yt_t yt_l "
                "z_t xs_ready b_ready st_ready ssd_read gate_t gate_used win_ready pl_hi pl_lo pv_hi pv_lo mx_t mx_hi "
                "mx_lo x_back hid_t hid_hi hid_lo gel_a gel_d gel_g hid2_t hid2_hi hid2_lo kv_ready rot_ready "
                "qa_ready ka_ready sm_max sm_exp pt_ready at_rs at_sq at_out mg_x mg_e mg_s col_ready dec_ready "
                "kt_ready v_ready ml_u ml_e ml_p ml_vw ml_cell ml_out ml_sq ml_rs og_t jn_t jn_hi jn_lo out_done "
                "ada_ready mod_ready at_raw "
            ).split()]
        block = ctx.enter_context(nc.Block())

        def pc(name, a=0, b=None):
            at, n = PARAM_AT[name]
            return par[:, at + a:at + (n if b is None else b)]

        def cc(name, a=0, b=None):
            at, n = CONST_AT[name]
            return con[:, at + a:at + (n if b is None else b)]

        ident, tri, ones = cc("ident"), cc("tri"), cc("ones")
        cw_half = half[:, 0:96]
        cb_half = half[:, 96:120]
        mw_half = half[:, 120:152]
        mb_half = half[:, 152:160]
        mn_half = half[:, 160:164]

        def over(ap, n):
            return ap.unsqueeze(2).to_broadcast([P, ap.shape[1], n])

        def each(ap, n):
            return ap.unsqueeze(1).to_broadcast([P, n, ap.shape[1]])

        def conv_par(u, t):
            if u.name == "QK":
                c = 2 * u.tag + t
                return mw_half[:, 4 * c:4 * c + 4], mb_half[:, c:c + 1]
            g = u.tag[0]
            c = 4 * g + 2 * u.tag[1] + t if u.name in ("X0", "X1") else 16 + 4 * t + g
            return cw_half[:, 4 * c:4 * c + 4], cb_half[:, c:c + 1]

        def mod_at(s):
            return mod[:, KD * s:KD * (s + 1)]

        acts = {"h": (h_hi, h_lo), "yT": (yt_hi, yt_lo), "pool": (p_hi, p_lo), "pv": (v_hi, v_lo),
                "mixed": (p_hi, p_lo), "hidden": (f_hi, f_lo), "hidden2": (g_hi, g_lo)}
        NORMS = [("x", 0, 0, "h"), ("x", 1, 3, "h"), ("x", None, None, "x"), ("x", 2, 6, "h"),
                 ("ysum", 3, None, "add"), ("x", 4, 9, "h"), ("ysum", 5, None, "add")]
        NORM_EPS_OF = ["eps1", "eps1", "eps1", "eps2", "eps2", "eps2", "eps2"]
        X_AT = [0, 8, 24, 32, None, 40, None]
        Y_AT = {4: 8, 6: 24}
        split_norms = [n for n, v in enumerate(NORMS) if v[3] == "h"]
        first_unit_after = {0: 0, 1: unit_at["UP"][0], 3: unit_at["KV"][0], 5: unit_at["FU"][0]}

        def chunk(c):
            return slice(P * c, P * (c + 1))

        turn_of = {}
        for g in range(GROUPS):
            for t in range(4):
                turn_of[6 * g + t] = ("xs_turn", (g, t))

        def win_slot(t):
            return 2 + (t // 2) % 2

        def units_over(k):
            u = units[k - 1]
            if u.last:
                j = u.job0 + u.n_jobs - 1
                return main_full[j % 4], j // 4 + 1
            return unit_done, sum(1 for v in units[:k] if not v.last)

        flat_k = k_tok[:, :, :, :].rearrange("p c h d -> p (c h d)")
        flat_v = v1[:, :, :, :].rearrange("p c h d -> p (c h d)")
        row_i, row_f, row_m, row_b = (flat_k[0:MH, SEQ * n:SEQ * (n + 1)] for n in range(4))
        row_e, row_t, row_z = (flat_v[0:MH, SEQ * n:SEQ * (n + 1)] for n in range(3))

        @block.sync
        def _(sp):
            def load_unit(u):
                s = u.n % 2
                if u.n >= 2:
                    sp.wait_ge(lo_done, u.n - 1)
                k = u.kn * u.cols
                sp.dma_start(raw[:, s, 0:k], stream[u.n, :, 0:k]).then_inc(raw_in[s], 16)

            sp.dma_start(par[:, :], params_in).then_inc(par_in, 16)
            sp.dma_start(con[:, :], consts_in).then_inc(par_in, 16)
            sp.dma_start(x[:, :, :], x_in).then_inc(x_in_sem, 16)
            AHEAD = 4
            for s in (1, 0):
                load_unit(units[1 - s])
                for k in range(KD):
                    i = KD * (1 - s) + k - AHEAD
                    if i >= 0:
                        sp.wait_ge(first_in[i % KD], 16 * (i // KD + 1))
                    sp.dma_start(ada_first[:, KD * s + k, :],
                                 w_ada[P * k:P * (k + 1), ADA_COLS * s:ADA_COLS * (s + 1)]).then_inc(first_in[k], 16)
            for u in units:
                if u.name == "OUT" and u.tag == 2:
                    sp.wait_ge(mx_lo, KD)
                    sp.dma_start(x[:, :, :], x_in).then_inc(x_back, 16)
                if u.n >= 2:
                    load_unit(u)
            for k in range(KD):
                sp.wait_ge(x_ready, 5 * KD + k + 1)
                sp.dma_start(out[:, k, :], x[:, k, :]).then_inc(out_done, 16)
            sp.wait_ge(out_done, 16 * KD)

        @block.gpsimd
        def _(pool):
            chain = [0]

            def link(ins):
                chain[0] += 1
                ins.then_inc(pool_chain, 1)
                pool.wait_ge(pool_chain, chain[0])

            def split_lo(u):
                s = u.n % 2
                k = u.kn * u.cols
                pool.wait_ge(hi_done, u.n + 1)
                if u.n >= 2:
                    pool.wait_ge(*units_over(u.n - 1))
                nc.gpsimd.tensor_tensor(w_lo[:, s, 0:k], raw[:, s, 0:k], w_hi[:, s, 0:k], ALU.subtract).then_inc(lo_done, 1)

            def ssd_scores(i, n):
                g, c = i
                xs = xs_tok[:, g % 2, c, :].rearrange("p (h d) -> p h d", d=HD)
                heads = slice(HG * g, HG * (g + 1))
                pool.wait_ge(dt_last, 1)
                pool.wait_ge(xs_ready, 4 * (g + 1))
                if n:
                    pool.wait_ge(ssd_read, n)
                    pool.wait_ge(y_ready, n)

                def times(k, factor):
                    return nc.gpsimd.tensor_tensor(xdt[:, k, :].rearrange("p (h d) -> p h d", d=HD), xs,
                                                   over(factor, HD), ALU.mult)
                times(0, dt[:, c, heads])
                times(1, dtt[:, c, heads])
                times(2, pc("d_skip", HG * g, HG * (g + 1))).then_inc(pre_x, 1)

            def ssd_out(i, n):
                pool.wait_ge(y_sq, n + 1)
                link(nc.gpsimd.tensor_scalar(ss[:, 1:2], ss[:, 0:1], 1.0 / GW, 4.0 * NORM_EPS, ALU.mult, ALU.add))
                if n:
                    pool.wait_ge(y_norm, n)
                nc.gpsimd.tensor_tensor(ss[:, 2:3], ss[:, 1:2], small[:, 63:64], ALU.pow).then_inc(y_rs, 1)

            def att_out(q, n):
                if q % 2 == 0:
                    return
                i = q // 2
                pool.wait_ge(at_sq, i + 1)
                link(nc.gpsimd.tensor_scalar(att[:, 26:27], att[:, 25:26], 1.0 / (AH * AD), RMS_EPS, ALU.mult, ALU.add))
                nc.gpsimd.tensor_tensor(att[:, 27:28], att[:, 26:27], small[:, 63:64], ALU.pow).then_inc(at_rs, 1)

            def ml_out_(c, n):
                pool.wait_ge(ml_sq, c + 1)
                link(nc.gpsimd.tensor_scalar(small[:, 4:8], small[:, 0:4], 1.0 / MD, RMS_EPS, ALU.mult, ALU.add))
                nc.gpsimd.tensor_tensor(small[:, 8:12], small[:, 4:8], small[:, 60:64], ALU.pow).then_inc(ml_rs, 1)

            def join(c, n):
                for b in (1, 0):
                    v = tmp[:, 2 * (c % 2) + b, :].rearrange("p (t d) -> p t d", t=4)
                    pool.wait_ge(jn_hi, 2 * c + 2 - b)
                    nc.gpsimd.tensor_tensor(h_lo[:, 4 * b:4 * b + 4, chunk(c)], v, h_hi[:, 4 * b:4 * b + 4, chunk(c)],
                                            ALU.subtract).then_inc(jn_lo, 1)

            stages = {"ssd_scores": ssd_scores, "ssd_out": ssd_out, "att_out": att_out, "ml_out": ml_out_, "join": join}
            count = {}

            def run(steps):
                for name, item in steps:
                    n = count.get(name, 0)
                    count[name] = n + 1
                    if name in stages:
                        stages[name](item, n)

            link(nc.gpsimd.memset(small[:, 60:64], -0.5))
            split_lo(units[0])
            for u in units:
                run(before[u.n])
                if u.n + 1 < len(units):
                    split_lo(units[u.n + 1])
                run(mid[u.n])
                run(end[u.n])

        @block.tensor
        def _(pe):
            def take(stage, k):
                b, use = bank_use[stage][k]
                if use:
                    pe.wait_ge(aux_free[b], use)
                return aux[b], aux_full[b]

            def operands_ready(u):
                if u.act == "h":
                    n = sum(1 for v in split_norms if first_unit_after[v] <= u.n)
                    if u.name == "WO":
                        pe.wait_ge(jn_hi, 2 * TC)
                        pe.wait_ge(jn_lo, 2 * TC)
                    elif u.n not in first_unit_after.values():
                        pe.wait_ge(norm_hi, KD * n)
                        pe.wait_ge(norm_lo, KD * n)
                elif u.act == "yT":
                    pe.wait_ge(yt_h, TC * (u.tag[0] + 1))
                    pe.wait_ge(yt_l, TC * (u.tag[0] + 1))

            split_tiles = {"pv": (pv_hi, pv_lo, 0), "mixed": (mx_hi, mx_lo, 0), "hidden": (hid_hi, hid_lo, FF_HALF),
                           "hidden2": (hid2_hi, hid2_lo, G2_HALF)}

            def project(u, part):
                s = u.n % 2
                if part == 0:
                    pe.wait_ge(lo_done, u.n + 1)
                    operands_ready(u)
                wh = w_hi[:, s, 0:u.kn * u.cols].rearrange("p (k c) -> p k c", k=u.kn)
                wl = w_lo[:, s, 0:u.kn * u.cols].rearrange("p (k c) -> p k c", k=u.kn)
                ah, al = acts[u.act]
                jobs = range(u.n_jobs // 2) if part == 0 else range(u.n_jobs // 2, u.n_jobs)
                ins = None
                for t in jobs:
                    j = u.job0 + t
                    bank = main[j % 4]
                    if u.first and j >= 4:
                        pe.wait_ge(main_free[j % 4], j // 4)
                    ks = range(u.kn)
                    if u.act == "pool":
                        ks = range(2 * (t // 2), 2 * (t // 2) + 2)
                        pe.wait_ge(pl_hi, ks[-1] + 1)
                        pe.wait_ge(pl_lo, ks[-1] + 1)
                    for k in ks:
                        if t == 0 and u.n in first_unit_after.values():
                            m = sum(1 for v in split_norms if first_unit_after[v] < u.n)
                            pe.wait_ge(norm_hi, KD * m + k + 1)
                            pe.wait_ge(norm_lo, KD * m + k + 1)
                        if t == 0 and u.act in split_tiles:
                            tile_hi, tile_lo, of_half = split_tiles[u.act]
                            there = (of_half * u.tag[0] if of_half else 0) + u.ak0 + k + 1
                            pe.wait_ge(tile_hi, there)
                            pe.wait_ge(tile_lo, there)
                        for a, w in ((ah, wh), (al, wh), (ah, wl)):
                            ka_ = k if u.act == "pool" else u.ak0 + k
                            start = u.first and k == ks[0] and a is ah and w is wh
                            stop = u.last and k == ks[-1] and w is wl
                            if u.token_major:
                                ins = nc.tensor.matmul(bank[:, 0:u.cols], a[:, ka_, chunk(t)], w[:, k, :], start=start, stop=stop)
                            else:
                                col = P * (t % 2) if u.act == "pool" else P * t
                                n = min(P, u.cols)
                                ins = nc.tensor.matmul(bank[0:n, :], w[:, k, col:col + n], a[:, ka_, :], start=start, stop=stop)
                    if u.last:
                        ins.then_inc(main_full[j % 4], 1)
                return ins

            def sumsq(item, n):
                i, pair = item
                if item == sum_stage(i):
                    bank, full = take(("sumsq", item), 0)
                    if i in SPREAD:
                        pe.wait_ge(norm_add, (KD - 1) * (SPREAD.index(i) + 1))
                        nc.tensor.matmul(bank[:, :], ones, rstd[:, :], start=True, stop=True).then_inc(full, 1)
                if i in SPREAD:
                    return
                for k in range(2 * pair, 2 * pair + 2):
                    pe.wait_ge(norm_sq, KD * i + k + 1)
                    ins = nc.tensor.matmul(aux["D"][:, :], ones, tmp[:, k % 2, :], start=(k == 0), stop=(k == KD - 1))
                    ins.then_inc(norm_use if k < KD - 1 else aux_full["D"], 1)

            def ada_sum(s, n):
                bank, full = take(("ada_sum", s), 0)
                pe.wait_ge(ada_ready, s + 1 if s > 1 else 2 - s)
                acc = ada_acc if s > 1 else ada_first[:, KD * s, :]
                for t in range(KD):
                    ins = nc.tensor.matmul(bank[:, t:t + 1], acc[:, chunk(t)], ones[:, 0:1], start=True, stop=True)
                ins.then_inc(full, 1)

            def dt_turn(i, n):
                bank, full = take(("dt_turn", 0), 0)
                pe.wait_ge(dt_f, 1)
                for c in range(TC):
                    ins = nc.tensor.transpose(bank[:, HEADS * c:HEADS * (c + 1)], sq_out[0:HEADS, chunk(c)], ident[0:HEADS, 0:HEADS])
                ins.then_inc(full, 1)

            def dt_sums(i, n):
                bank, full = take(("dt_sums", 0), 0)
                pe.wait_ge(dt_s, 1)
                for c in range(TC):
                    nc.tensor.matmul(bank[:, HEADS * c:HEADS * (c + 1)], tri, dta[:, c, :], start=True, stop=True)
                for c in range(TC):
                    ins = nc.tensor.matmul(bank[:, P + HEADS * c:P + HEADS * (c + 1)], ones, dta[:, c, :], start=True, stop=True)
                ins.then_inc(full, 1)

            def xs_turn(i, n):
                g, t = i
                bank, full = take(("xs_turn", i), 0)
                cn = conv_at[[u.n for u in conv_units if u.name == f"X{t // 2}"][g], t % 2]
                pe.wait_ge(conv_s, cn + 1)
                for c in range(TC):
                    ins = nc.tensor.transpose(bank[:, chunk(c)], tmp[:, cn % 2, chunk(c)], ident)
                ins.then_inc(full, 1)

            def b_turn(g, n):
                bank, full = take(("b_turn", g), 0)
                cn = conv_at[[u.n for u in conv_units if u.name == "BC"][g], 1]
                pe.wait_ge(conv_s, cn + 1)
                for c in range(TC):
                    ins = nc.tensor.transpose(bank[:, chunk(c)], bc[:, g % 2, 0, chunk(c)], ident)
                ins.then_inc(full, 1)

            def ssd_scores(i, n):
                g, c = i
                pe.wait_ge(dt_acs, 1)
                bank, full = take(("ssd_scores", i), 0)
                nc.tensor.matmul(bank[:, 0:P], bc[:, g % 2, 0, chunk(c)], bc[:, g % 2, 1, chunk(c)],
                                 start=True, stop=True).then_inc(full, 1)
                for b in range(2):
                    bank, full = take(("ssd_scores", i), 1 + b)
                    for k in range(4):
                        hd = HG * g + 4 * b + k
                        ins = nc.tensor.matmul(bank[:, chunk(k)], dta[:, c, hd:hd + 1].to_broadcast([P, P]), tri,
                                               start=True, stop=True)
                    ins.then_inc(full, 1)

            def ssd_out(i, n):
                g, c = i
                pe.wait_ge(b_ready, g + 1)
                pe.wait_ge(pre_x, n + 1)
                bank, full = take(("ssd_out", i), 1)
                if c:
                    pe.wait_ge(st_ready, n)
                    nc.tensor.matmul(bank[:, :], bc[:, g % 2, 1, chunk(c)], state[:, :], start=True, stop=True).then_inc(full, 1)
                else:
                    nc.tensor.matmul(bank[:, 0:1], ident, ones[:, 0:1], start=True, stop=True).then_inc(full, 1)
                bank, full = take(("ssd_out", i), 2)
                if c < TC - 1:
                    nc.tensor.matmul(bank[:, :], b_tok[:, g % 2, c, :], xdt[:, 1, :], start=True, stop=True).then_inc(full, 1)
                else:
                    nc.tensor.matmul(bank[:, 0:1], ident, ones[:, 0:1], start=True, stop=True).then_inc(full, 1)
                bank, full = take(("ssd_out", i), 0)
                pe.wait_ge(mix, n + 1)
                for k in range(HG):
                    ins = nc.tensor.matmul(bank[:, HD * k:HD * (k + 1)], decay[:, k, :], xdt[:, 0, HD * k:HD * (k + 1)],
                                           start=True, stop=True)
                ins.then_inc(full, 1)

            def ssd_turn(i, n):
                g, c = i
                bank, full = take(("ssd_turn", i), 0)
                pe.wait_ge(y_norm, n + 1)
                for t in range(4):
                    ins = nc.tensor.transpose(bank[:, chunk(t)], z[:, c, chunk(t)], ident)
                ins.then_inc(full, 1)

            def rope_k(i, n):
                bank, full = take(("rope_k", 0), 0)
                pe.wait_ge(rot_ready, TC)
                for c in range(TC):
                    ins = nc.tensor.transpose(bank[:, chunk(c)], k_rot[:, c, :], ident)
                ins.then_inc(full, 1)

            def rope_q(c, n):
                bank, full = take(("rope_q", c), 0)
                pe.wait_ge(rot_ready, TC + c + 1)
                for t in range(4):
                    ins = nc.tensor.transpose(bank[:, chunk(t)], hm[:, c, chunk(t)], ident)
                ins.then_inc(full, 1)

            def keys(i):
                return (0, P) if i == 0 else (P * (i - 1), 2 * P)

            def att_scores(q, n):
                i, g = q // 2, q % 2
                k0, kn = keys(i)
                rows = slice(AD * g, AD * (g + 1))
                pe.wait_ge(qa_ready, i + 1)
                pe.wait_ge(ka_ready, 1)
                for b in range(2):
                    bank, full = take(("att_scores", q), b)
                    for j in range(2):
                        ins = nc.tensor.matmul(bank[:, 2 * P * j + 2 * P - kn:2 * P * (j + 1)], qa[rows, i + 1, 2 * b + j, :],
                                               ka[rows, k0:k0 + kn], start=True, stop=True)
                    ins.then_inc(full, 1)

            def att_turn(q, n):
                i = q // 2
                pe.wait_ge(sm_exp, q + 1)
                for b in range(2):
                    bank, full = take(("att_turn", q), b)
                    for j in range(2):
                        for r in range(2):
                            if i == 0 and r == 0:
                                continue
                            ins = nc.tensor.transpose(bank[:, 2 * P * j + P * r:2 * P * j + P * (r + 1)],
                                                      prob[:, 2 * b + j, chunk(r)], ident)
                    ins.then_inc(full, 1)

            def att_out_(q, n):
                i, g = q // 2, q % 2
                bank, full = take(("att_out", q), 0)
                pe.wait_ge(pt_ready, 2 * (q + 1))
                pe.wait_ge(kv_ready, TC)
                for j in range(4):
                    for r in range(2):
                        if i == 0 and r == 0:
                            continue
                        ins = nc.tensor.matmul(bank[:, AD * j:AD * (j + 1)], prob_t[:, j, r, :],
                                               va[:, i - 1 + r, AD * g:AD * (g + 1)], start=(r == 0 or i == 0), stop=(r == 1))
                ins.then_inc(full, 1)

            def ml_columns(i, n):
                pe.wait_ge(mg_s, 1)
                bank, full = take(("ml_columns", 0), 0)
                for c in range(TC):
                    ins = nc.tensor.transpose(bank[:, chunk(c)], quant[:, chunk(c)], ident)
                ins.then_inc(full, 1)
                bank, full = take(("ml_columns", 0), 1)
                for hd in range(MH):
                    ins = nc.tensor.matmul(bank[:, TC * hd:TC * (hd + 1)], ident[0:MH, hd:hd + 1].to_broadcast([MH, P]),
                                           dec[0:MH, 0:TC], start=True, stop=True)
                ins.then_inc(full, 1)

            def k_turn(hd, n):
                bank, full = take(("k_turn", hd), 0)
                pe.wait_ge(conv_s, 24 + 4 + hd + 1)
                pe.wait_ge(kt_ready, hd + 1)
                for c in range(TC):
                    ins = nc.tensor.transpose(bank[:, chunk(c)], qk[:, 4 + hd, chunk(c)], ident)
                ins.then_inc(full, 1)

            def ml_scores(c, n):
                bank, full = take(("ml_scores", c), 0)
                pe.wait_ge(kt_ready, MH)
                for hd in range(MH):
                    ins = nc.tensor.matmul(bank[:, chunk(hd)], qk[:, 4 + hd, chunk(c)], qk[:, hd, chunk(c)], start=True, stop=True)
                ins.then_inc(full, 1)
                bank, full = take(("ml_scores", c), 1)
                for hd in range(MH):
                    ins = nc.tensor.matmul(bank[:, chunk(hd)], ident[0:MH, hd:hd + 1].to_broadcast([MH, P]),
                                           urow[0:MH, chunk(c)], start=True, stop=True)
                ins.then_inc(full, 1)

            def ml_out_(c, n):
                W = MD + 1
                for b in range(2):
                    bank, full = take(("ml_out", c), 2 + b)
                    pe.wait_ge(ml_cell, c + 1)
                    for j in range(2):
                        ins = nc.tensor.matmul(bank[:, W * j:W * (j + 1)], qk[:, 2 * b + j, chunk(c)], cell[:, 2 * b + j, :], start=True, stop=True)
                    ins.then_inc(full, 1)
                pe.wait_ge(ml_p, c + 1)
                pe.wait_ge(v_ready, TC)
                pe.wait_ge(ml_vw, c + 1)
                pp = tmp[:, 0, :].rearrange("p (h t) -> p h t", h=MH)
                vw = tmp[:, :, :].rearrange("p a b -> p (a b)")[:, SEQ:SEQ + MH * (MD + 1)].rearrange("p (h d) -> p h d", h=MH)
                for b in range(2):
                    bank, full = take(("ml_out", c), b)
                    for j in range(2):
                        ins = nc.tensor.matmul(bank[:, W * j:W * (j + 1)], pp[:, 2 * b + j, :], v1[:, c, 2 * b + j, :], start=True, stop=True)
                    ins.then_inc(full, 1)
                for b in range(2):
                    bank, full = take(("ml_out", c), 4 + b)
                    pe.wait_ge(dec_ready, MH)
                    for j in range(2):
                        ins = nc.tensor.matmul(bank[:, W * j:W * (j + 1)], k_tok[:, c, 2 * b + j, :], vw[:, 2 * b + j, :], start=True, stop=True)
                    ins.then_inc(full, 1)

            def join(c, n):
                bank, full = take(("join", c), 1)
                pe.wait_ge(at_out, c + 1)
                for t in range(4):
                    ins = nc.tensor.transpose(bank[:, chunk(t)], qa[:, c, t, :], ident)
                ins.then_inc(full, 1)
                bank, full = take(("join", c), 0)
                pe.wait_ge(ml_out, c + 1)
                for t in range(MH):
                    ins = nc.tensor.transpose(bank[:, chunk(t)], hm[:, c, chunk(t)], ident)
                ins.then_inc(full, 1)

            stages = {"sumsq": sumsq, "ada_sum": ada_sum, "dt_turn": dt_turn, "dt_sums": dt_sums, "xs_turn": xs_turn, "b_turn": b_turn,
                      "ssd_scores": ssd_scores, "ssd_out": ssd_out, "ssd_turn": ssd_turn, "rope_k": rope_k, "rope_q": rope_q,
                      "att_scores": att_scores, "att_turn": att_turn, "att_out": att_out_, "ml_columns": ml_columns,
                      "k_turn": k_turn, "ml_scores": ml_scores, "ml_out": ml_out_, "join": join}
            count = {}

            def run(steps):
                for name, item in steps:
                    n = count.get(name, 0)
                    count[name] = n + 1
                    if name in stages:
                        stages[name](item, n)

            pe.wait_ge(par_in, 32)
            run(before[0])
            ada_sum(1, 0)
            ada_sum(0, 1)
            for u in units:
                if u.n:
                    run(before[u.n])
                project(u, 0)
                run(mid[u.n])
                ins = project(u, 1)
                if not u.last:
                    ins.then_inc(unit_done, 1)
                run(end[u.n])
            run(last)

        @block.scalar
        def _(act):
            chain = [0]

            def link(ins):
                chain[0] += 1
                ins.then_inc(act_chain, 1)
                act.wait_ge(act_chain, chain[0])

            run_act = nc.scalar.activation

            def full(stage, k):
                b, use = bank_use[stage][k]
                act.wait_ge(aux_full[b], use + 1)
                return aux[b], aux_free[b]

            def read_by_pe(stage, k):
                b, use = bank_use[stage][k]
                act.wait_ge(aux_full[b], use + 1)

            def tile(j):
                act.wait_ge(main_full[j % 4], j // 4 + 1)
                return main[j % 4], main_free[j % 4]

            def split_hi(u):
                s = u.n % 2
                k = u.kn * u.cols
                act.wait_ge(raw_in[s], 16 * (u.n // 2 + 1))
                if u.n >= 2:
                    act.wait_ge(*units_over(u.n - 1))
                run_act(w_hi[:, s, 0:k], raw[:, s, 0:k], ACT.Copy).then_inc(hi_done, 1)

            def convolve(u, t):
                cn = conv_at[u.n, t]
                w, b = conv_par(u, t)
                if cn >= 2:
                    act.wait_ge(conv_s, cn - 1)
                    if cn - 2 in turn_of:
                        read_by_pe(turn_of[cn - 2], 0)
                bank, free = tile(u.job0 + t)
                run_act(tmp[:, cn % 2, :], bank[:, :], ACT.Identity, bias=b, scale=w[:, 3:4]).then_inc(conv_a, 1)
                act.wait_ge(conv_d, cn + 1)
                run_act(tmp[:, 2 + cn % 2, :], tmp[:, cn % 2, :], ACT.Tanh).then_inc(conv_t, 1)

            def evict(u, t):
                j = u.job0 + t
                if u.name in ("X0", "X1", "BC", "QK"):
                    convolve(u, t)
                elif u.name == "Z1":
                    g = u.tag[0]
                    bank, free = tile(j)
                    if g:
                        read_by_pe(("ssd_turn", (g - 1, t)), 0)
                    run_act(z[:, t, :], bank[:, :], ACT.Tanh, scale=0.5).then_inc(z_t, 1)
                elif u.name == "U":
                    k = 2 * u.tag + t
                    bank, free = tile(j)
                    act.wait_ge(pre_x, 12 if k < 4 else 16)
                    run_act(xs_tok[:, k // 4, k % 4, :], bank[:, :], ACT.Copy).then_inc(free, 1)
                elif u.name == "GS":
                    k = 2 * u.tag + t
                    bank, free = tile(j)
                    if k >= 2:
                        act.wait_ge(gate_used, k - 1)
                    link(run_act(tmp[:, k % 2, :], bank[:, :], ACT.Tanh, scale=0.5))
                    act.sem_inc(gate_t, 1)
                elif u.name == "PW":
                    bank, free = tile(j)
                    run_act(v_hi[:, t, :], bank[:, :], ACT.Copy, scale=pc("pool_scale", t, t + 1)).then_inc(pv_hi, 1)
                elif u.name == "GP":
                    k = 2 * u.tag + t
                    bank, free = tile(j)
                    act.wait_ge(pl_lo, KD)
                    run_act(xs_tok[:, k // 4, k % 4, :], bank[:, :], ACT.Tanh, scale=0.5).then_inc(free, 1)
                elif u.name == "BP":
                    k = 2 * u.tag + t
                    act.wait_ge(mx_t, k + 1)
                    if k == 0:
                        act.wait_ge(*units_over(unit_at["PW"][0] + 1))
                    run_act(p_hi[:, k, :], x[:, k, :], ACT.Copy).then_inc(mx_hi, 1)
                elif u.name == "UP":
                    half_, i = u.tag
                    n = FF_HALF * half_ + 2 * i + t
                    k = 2 * i + t
                    bank, free = tile(j)
                    if n >= 2:
                        act.wait_ge(hid_t, n - 1)
                    link(run_act(tmp[:, n % 2, :], bank[:, :], ACT.Relu))
                    act.sem_inc(free, 1)
                    if half_ and k == 0:
                        act.wait_ge(*units_over(unit_at["DN"][7] + 1))
                    run_act(f_hi[:, k, :], tmp[:, n % 2, :], ACT.Square).then_inc(hid_hi, 1)
                elif u.name == "KV":
                    bank, free = tile(j)
                    run_act(va[:, t, :], bank[:, P:2 * P], ACT.Copy).then_inc(kv_ready, 1)
                elif u.name == "V1":
                    bank, free = tile(j)
                    act.wait_ge(col_ready, 1)
                    link(run_act(v1[:, t, :, 0:MD], bank[:, :].rearrange("p (h d) -> p h d", h=MH), ACT.Copy))
                    act.sem_inc(free, 1)
                    act.sem_inc(v_ready, 1)
                elif u.name == "O1":
                    bank, free = tile(j)
                    link(run_act(og[:, t, :], bank[:, :], ACT.Tanh, scale=0.5))
                    act.sem_inc(free, 1)
                    act.sem_inc(og_t, 1)
                elif u.name == "WO":
                    k = 2 * u.tag + t
                    bank, free = tile(j)
                    link(run_act(ysum[:, k, :], bank[:, :], ACT.Copy))
                    act.sem_inc(free, 1)
                    act.sem_inc(ysum_ready, 1)
                elif u.name == "FU":
                    half_, i = u.tag
                    m = G2_HALF * half_ + i
                    col = m + (G2_TILES if t else 0)
                    bank, free = tile(j)
                    if m >= 1:
                        act.wait_ge(hid2_t, m)
                    run_act(tmp[:, t, :], bank[:, :], ACT.Identity, bias=pc("ff_conv_b", col, col + 1),
                            scale=pc("ff_conv_w", 3 * col + 2, 3 * col + 3)).then_inc(gel_a, 1)
                    if t == 0:
                        act.wait_ge(gel_d, 2 * m + 1)
                        run_act(gel[:, :], tmp[:, 0, :], ACT.Gelu_apprx_tanh).then_inc(gel_g, 1)
                    else:
                        act.wait_ge(hid2_t, m + 1)
                        if half_ and i == 0:
                            act.wait_ge(*units_over(unit_at["FD"][7] + 1))
                        run_act(g_hi[:, i, :], tmp[:, 2 + m % 2, :], ACT.Copy).then_inc(hid2_hi, 1)
                elif u.name == "FD" and u.last and u.tag[0] == 0:
                    k = 2 * u.tag[1] + t
                    bank, free = tile(j)
                    link(run_act(ysum[:, k, :], bank[:, :], ACT.Copy))
                    act.sem_inc(free, 1)
                    act.sem_inc(ysum_ready, 1)

            def load_piece(p):
                s, k = p // 8 + 2, p % 8
                src = w_ada if s < 6 else w_ada2
                if p >= 2:
                    act.wait_ge(ada_used, p - 1)
                c0 = ADA_COLS * (s % 6)
                act.dma_start(ada_raw[:, p % 2, :], src[P * k:P * (k + 1), c0:c0 + ADA_COLS]).then_inc(ada_in[p % 2], 16)

            def ada_piece(p, n):
                if p + 1 < 80:
                    load_piece(p + 1)

            def sumsq(item, n):
                i, pair = item
                src = NORMS[i][0]
                for k in range(2 * pair, 2 * pair + 2):
                    if i == 0:
                        act.wait_ge(x_in_sem, 16)
                    elif src == "x":
                        act.wait_ge(x_ready, X_AT[i] - KD + k + 1)
                    else:
                        act.wait_ge(ysum_ready, Y_AT[i] - KD + k + 1)
                    if i in SPREAD:
                        if k >= 3:
                            act.wait_ge(norm_add, (KD - 1) * SPREAD.index(i) + k - 2)
                    elif k >= 2:
                        act.wait_ge(norm_use, (KD - 1) * (0, 3, 5).index(i) + k - 1)
                    a = x if src == "x" else ysum
                    to = rstd[:, :] if i in SPREAD and k == 0 else tmp[:, k % 2, :]
                    run_act(to, a[:, k, :], ACT.Square).then_inc(norm_sq, 1)

            def norm(i, n):
                kind = NORMS[i][3]
                bank, free = full(("sumsq", sum_stage(i)), 0)
                run_act(rstd[:, :], bank[:, :], ACT.Sqrt, bias=pc(NORM_EPS_OF[i]), scale=1.0 / D_MODEL).then_inc(norm_rt, 1)
                if kind == "h":
                    m = split_norms.index(i)
                    shift = mod_at(NORMS[i][2])
                    if i:
                        act.wait_ge(*units_over(first_unit_after[i]))
                    for k in range(KD):
                        act.wait_ge(norm_tmp, KD * m + k + 1)
                        run_act(h_hi[:, k, :], tmp[:, 2 + k % 2, :], ACT.Identity, bias=shift[:, k:k + 1]).then_inc(norm_hi, 1)

            def dt_gates(i, n):
                act.wait_ge(dt_x, 1)
                link(run_act(cdec[:, 0, :], pc("a_log"), ACT.Exp))
                link(run_act(edec[:, :, :], dt[:, :, :], ACT.Abs))
                link(run_act(edec[:, :, :], edec[:, :, :], ACT.Exp, scale=-1.0))
                run_act(edec[:, :, :], edec[:, :, :], ACT.Ln, bias=ones[:, 0:1]).then_inc(dt_e, 1)

            def dt_sums(i, n):
                bank, free = full(("dt_sums", 0), 0)
                run_act(cdec[:, :, :].rearrange("p c h -> p (c h)"), bank[:, P:2 * P], ACT.Exp).then_inc(dt_e, 1)
                act.wait_ge(dt_acs, 1)
                run_act(eacs[:, :, :], acs[:, :, :], ACT.Exp)
                run_act(edec[:, :, :], edec[:, :, :], ACT.Exp).then_inc(dt_e, 1)

            def xs_turn(i, n):
                g, t = i
                bank, free = full(("xs_turn", i), 0)
                if g >= 2:
                    act.wait_ge(pre_x, TC * (g - 1))
                link(run_act(xs_tok[:, g % 2, :, P * t:P * (t + 1)], bank[:, :].rearrange("p (c d) -> p c d", c=TC),
                        ACT.Copy))
                act.sem_inc(free, 1)
                act.sem_inc(xs_ready, 1)

            def b_turn(g, n):
                bank, free = full(("b_turn", g), 0)
                if g >= 2:
                    read_by_pe(("ssd_out", (g - 2, TC - 1)), 2)
                link(run_act(b_tok[:, g % 2, :, :], bank[:, :].rearrange("p (c d) -> p c d", c=TC), ACT.Copy))
                act.sem_inc(free, 1)
                act.sem_inc(b_ready, 1)

            def ssd_scores(i, n):
                act.wait_ge(seg, n + 1)
                run_act(decay[:, :, :], decay[:, :, :], ACT.Exp).then_inc(seg_e, 1)

            def ssd_out(i, n):
                g, c = i
                act.wait_ge(y_ready, n + 1)
                run_act(sq_out[:, :], z[:, c, :], ACT.Square, accum_out=ss[:, 0:1]).then_inc(y_sq, 1)
                act.wait_ge(y_rs, n + 1)
                run_act(z[:, c, :], z[:, c, :], ACT.Copy, scale=ss[:, 2:3]).then_inc(y_norm, 1)

            def ssd_turn(i, n):
                g, c = i
                act.wait_ge(yt_t, n + 1)
                if c == 0 and g:
                    act.wait_ge(*units_over(unit_at["Y1"][g - 1] + 1))
                run_act(yt_hi[:, :, chunk(c)], y_turned[:, :, :], ACT.Copy).then_inc(yt_h, 1)

            def window(t, n):
                act.wait_ge(win_ready, t + 1)
                run_act(p_hi[:, t, :], tmp[:, win_slot(t), :], ACT.Copy).then_inc(pl_hi, 1)

            def rope_k(i, n):
                bank, free = full(("rope_k", 0), 0)
                link(run_act(ka[:, :], bank[:, :], ACT.Copy))
                act.sem_inc(free, 1)
                act.sem_inc(ka_ready, 1)

            def rope_q(c, n):
                bank, free = full(("rope_q", c), 0)
                link(run_act(qa[:, c + 1, :, :].rearrange("p t d -> p (t d)"), bank[:, :], ACT.Copy))
                act.sem_inc(free, 1)
                act.sem_inc(qa_ready, 1)

            def att_scores(q, n):
                ks = slice(P, 2 * P) if q < 2 else slice(0, 2 * P)
                act.wait_ge(sm_max, q + 1)
                for j in range(4):
                    run_act(prob[:, j, ks], prob[:, j, ks], ACT.Exp, bias=att[:, 8 + j:9 + j], accum_out=att[:, 12 + j:13 + j])
                run_act(att[:, 16:20], att[:, 16:20], ACT.Exp).then_inc(sm_exp, 1)

            def att_turn(q, n):
                rs_ = 1 if q < 2 else 0
                if q:
                    read_by_pe(("att_out", q - 1), 0)
                for b in range(2):
                    bank, free = full(("att_turn", q), b)
                    link(run_act(prob_t[:, 2 * b:2 * b + 2, rs_:2, :],
                            bank[:, :].rearrange("p (j r t) -> p j r t", j=2, r=2)[:, :, rs_:2, :], ACT.Copy))
                    act.sem_inc(free, 1)
                    act.sem_inc(pt_ready, 1)

            def att_out(q, n):
                if q % 2:
                    i = q // 2
                    act.wait_ge(at_raw, q + 1)
                    read_by_pe(("ml_columns", 0), 0)
                    if i:
                        act.wait_ge(at_rs, i)
                    run_act(quant[:, :], qa[:, i, :, :].rearrange("p t d -> p (t d)"), ACT.Square,
                            accum_out=att[:, 25:26]).then_inc(at_sq, 1)

            def ml_gates(i, n):
                act.wait_ge(mg_x, 1)
                link(run_act(row_e, row_f, ACT.Abs))
                link(run_act(row_e, row_e, ACT.Exp, scale=-1.0))
                run_act(row_e, row_e, ACT.Ln, bias=ones[0:MH, 0:1]).then_inc(mg_e, 1)
                act.wait_ge(mg_x, 2)
                run_act(quant[32:32 + MH, :], row_t, ACT.Exp)
                run_act(dec[0:MH, 0:TC], row_t.rearrange("p (c t) -> p c t", c=TC)[:, :, P - 1], ACT.Exp)
                run_act(quant[64:64 + MH, :], row_z, ACT.Exp)
                run_act(quant[96:96 + MH, :], row_m, ACT.Exp, scale=-1.0).then_inc(mg_s, 1)

            def k_turn(hd, n):
                act.wait_ge(conv_s, 24 + 4 + hd + 1)
                link(run_act(qk[:, 4 + hd, :], qk[:, 4 + hd, :], ACT.Copy, scale=float(MD) ** -0.5))
                act.sem_inc(kt_ready, 1)
                act.wait_ge(col_ready, 1)
                bank, free = full(("k_turn", hd), 0)
                link(run_act(k_tok[:, :, hd, :], bank[:, :].rearrange("p (c d) -> p c d", c=TC), ACT.Copy))
                act.sem_inc(free, 1)
                act.sem_inc(dec_ready, 1)

            def ml_scores(c, n):
                act.wait_ge(ml_u, c + 1)
                run_act(tmp[:, 0, :], tmp[:, 0, :], ACT.Exp).then_inc(ml_e, 1)

            def join(c, n):
                for b in (1, 0):
                    act.wait_ge(jn_t, 2 * c + 2 - b)
                    if c == 0 and b == 1:
                        act.wait_ge(*units_over(unit_at["WO"][0]))
                    run_act(h_hi[:, 4 * b:4 * b + 4, chunk(c)], tmp[:, 2 * (c % 2) + b, :].rearrange("p (t d) -> p t d", t=4),
                            ACT.Copy).then_inc(jn_hi, 1)

            stages = {"norm": norm, "sumsq": sumsq, "ada_piece": ada_piece, "dt_gates": dt_gates, "dt_sums": dt_sums, "xs_turn": xs_turn,
                      "b_turn": b_turn, "ssd_scores": ssd_scores, "ssd_out": ssd_out, "ssd_turn": ssd_turn, "window": window,
                      "rope_k": rope_k, "rope_q": rope_q, "att_scores": att_scores, "att_turn": att_turn, "att_out": att_out,
                      "ml_gates": ml_gates, "k_turn": k_turn, "ml_scores": ml_scores, "join": join}
            count = {}

            def run(steps):
                for name, item in steps:
                    n = count.get(name, 0)
                    count[name] = n + 1
                    if name in stages:
                        stages[name](item, n)

            act.wait_ge(par_in, 32)
            run_act(cst[:, :, :].rearrange("p a k -> p (a k)"), par[:, 0:2 * KD],
                    ACT.Tanh, scale=0.5).then_inc(cs_t, 1)
            load_piece(0)
            run(before[0][:KD // 2])
            split_hi(units[0])
            split_hi(units[1])
            for u in units:
                run(before[u.n] if u.n else before[0][KD // 2:])
                if 0 < u.n < len(units) - 1:
                    split_hi(units[u.n + 1])
                if u.last:
                    for t in range(u.n_jobs // 2):
                        evict(u, t)
                run(mid[u.n])
                if u.last:
                    for t in range(u.n_jobs // 2, u.n_jobs):
                        evict(u, t)
                run(end[u.n])
            run(last)

        @block.vector
        def _(dve):
            chain = [0]

            def link(ins):
                chain[0] += 1
                ins.then_inc(dve_chain, 1)
                dve.wait_ge(dve_chain, chain[0])

            stt, tt, ts = nc.vector.scalar_tensor_tensor, nc.vector.tensor_tensor, nc.vector.tensor_scalar

            def full(stage, k):
                b, use = bank_use[stage][k]
                dve.wait_ge(aux_full[b], use + 1)
                return aux[b], aux_free[b]

            def tile(j):
                dve.wait_ge(main_full[j % 4], j // 4 + 1)
                return main[j % 4], main_free[j % 4]

            open_silu = []

            def convolve(u, t):
                cn = conv_at[u.n, t]
                w, _ = conv_par(u, t)
                bank, free = tile(u.job0 + t)
                finish_silu()
                dve.wait_ge(conv_a, cn + 1)
                acc = tmp[:, cn % 2, :]
                for d in range(1, CONV_W):
                    ins = stt(acc[:, d:SEQ], bank[:, 0:SEQ - d], w[:, 3 - d:4 - d], acc[:, d:SEQ], ALU.mult, ALU.add)
                    if d < CONV_W - 1:
                        link(ins)
                link(ins)
                dve.sem_inc(conv_d, 1)
                dve.sem_inc(free, 1)
                open_silu.append((u, t))

            def finish_silu():
                if not open_silu:
                    return
                u, t = open_silu.pop()
                cn = conv_at[u.n, t]
                acc = tmp[:, cn % 2, :]
                dve.wait_ge(conv_t, cn + 1)
                if u.name == "BC":
                    g = u.tag[0]
                    if g >= 2:
                        full(("ssd_out", (g - 2, TC - 1)), 2)
                    dst = bc[:, g % 2, t, :]
                elif u.name == "QK":
                    dst = qk[:, 2 * u.tag + t, :]
                else:
                    dst = acc
                stt(dst, tmp[:, 2 + cn % 2, :], 1.0, acc, ALU.add, ALU.mult).then_inc(conv_s, 1)

            def rope(src, heads, c, a, b):
                cos = cc("cos", 32 * c, 32 * (c + 1))
                sin = cc("sin", 32 * c, 32 * (c + 1))
                v = src.rearrange("p (n d) -> p n d", d=32)
                tt(a.rearrange("p (n d) -> p n d", d=32), v, each(cos, 2 * heads), ALU.mult)
                return tt(b.rearrange("p (n d) -> p n d", d=32), v, each(sin, 2 * heads), ALU.mult)

            def evict(u, t):
                j = u.job0 + t
                if u.name in ("X0", "X1", "BC", "QK"):
                    convolve(u, t)
                elif u.name == "DT":
                    bank, free = tile(j)
                    link(nc.vector.tensor_copy(sq_out[0:HEADS, :], bank[0:HEADS, :]))
                    dve.sem_inc(free, 1)
                    dve.sem_inc(dt_f, 1)
                elif u.name == "Z1":
                    bank, free = tile(j)
                    dve.wait_ge(z_t, TC * u.tag[0] + t + 1)
                    link(stt(z[:, t, :], z[:, t, :], 1.0, bank[:, :], ALU.add, ALU.mult))
                    dve.sem_inc(free, 1)
                elif u.name in ("Y0", "Y1"):
                    k = 4 * u.tag[1] + t
                    bank, free = tile(j)
                    if u.tag[0] == 0:
                        nc.vector.tensor_copy(x[:, k, :], bank[:, :]).then_inc(free, 1)
                    else:
                        tt(x[:, k, :], x[:, k, :], bank[:, :], ALU.add).then_inc(free, 1)
                elif u.name == "GS":
                    k = 2 * u.tag + t
                    bank, free = tile(j)
                    dve.wait_ge(gate_t, k + 1)
                    link(stt(x[:, k, :], tmp[:, k % 2, :], 1.0, x[:, k, :], ALU.add, ALU.mult))
                    dve.sem_inc(free, 1)
                    dve.sem_inc(gate_used, 1)
                elif u.name == "PW":
                    bank, free = tile(j)
                    dve.wait_ge(pv_hi, t + 1)
                    link(stt(v_lo[:, t, :], bank[:, :], pc("pool_scale", t, t + 1), v_hi[:, t, :], ALU.mult, ALU.subtract))
                    dve.sem_inc(free, 1)
                    dve.sem_inc(pv_lo, 1)
                elif u.name == "BP":
                    k = 2 * u.tag + t
                    gate = xs_tok[:, k // 4, k % 4, :]
                    bank, free = tile(j)
                    jg = units[unit_at["GP"][0]].job0 + k
                    dve.wait_ge(main_free[jg % 4], jg // 4 + 1)
                    link(stt(gate, gate, 1.0, bank[:, :], ALU.add, ALU.mult))
                    dve.sem_inc(free, 1)
                    link(tt(x[:, k, :], x[:, k, :], gate, ALU.add))
                    dve.sem_inc(mx_t, 1)
                    dve.wait_ge(mx_hi, k + 1)
                    tt(p_lo[:, k, :], x[:, k, :], p_hi[:, k, :], ALU.subtract).then_inc(mx_lo, 1)
                elif u.name == "OUT":
                    k = 2 * u.tag + t
                    bank, free = tile(j)
                    dve.wait_ge(x_back, 16)
                    link(stt(x[:, k, :], bank[:, :], mul[:, 6, k:k + 1], x[:, k, :], ALU.mult, ALU.add))
                    dve.sem_inc(free, 1)
                    dve.sem_inc(x_ready, 1)
                elif u.name == "UP":
                    half_, i = u.tag
                    n = FF_HALF * half_ + 2 * i + t
                    k = 2 * i + t
                    dve.wait_ge(hid_hi, n + 1)
                    link(tt(tmp[:, 2 + n % 2, :], tmp[:, n % 2, :], tmp[:, n % 2, :], ALU.mult))
                    dve.sem_inc(hid_t, 1)
                    tt(f_lo[:, k, :], tmp[:, 2 + n % 2, :], f_hi[:, k, :], ALU.subtract).then_inc(hid_lo, 1)
                elif u.name == "DN":
                    k = 2 * u.tag[1] + t
                    bank, free = tile(j)
                    link(stt(x[:, k, :], bank[:, :], mod_at(5)[:, k:k + 1], x[:, k, :], ALU.mult, ALU.add))
                    dve.sem_inc(free, 1)
                    dve.sem_inc(x_ready, 1)
                elif u.name == "KV":
                    bank, free = tile(j)
                    a, b = tmp[:, 0, 0:P], tmp[:, 1, 0:P]
                    dve.wait_ge(kv_ready, t + 1)
                    link(rope(bank[:, 0:P], AKV, t, a, b))
                    dve.sem_inc(free, 1)
                    v = k_rot[:, t, :].rearrange("p (h s d) -> p h s d", h=AKV, s=2)
                    a, b = (y.rearrange("p (h s d) -> p h s d", h=AKV, s=2) for y in (a, b))
                    tt(v[:, :, 0, :], a[:, :, 0, :], b[:, :, 1, :], ALU.subtract)
                    link(tt(v[:, :, 1, :], a[:, :, 1, :], b[:, :, 0, :], ALU.add))
                    dve.sem_inc(rot_ready, 1)
                elif u.name == "QA1":
                    bank, free = tile(j)
                    a, b = tmp[:, 0, :], tmp[:, 1, :]
                    link(rope(bank[:, :], AH, t, a, b))
                    dve.sem_inc(free, 1)
                    v = hm[:, t, :].rearrange("p (j g s d) -> p g j s d", j=4, g=2, s=2)
                    a, b = (y.rearrange("p (g j s d) -> p g j s d", g=2, j=4, s=2) for y in (a, b))
                    for g in range(2):
                        tt(v[:, g, :, 0, :], a[:, g, :, 0, :], b[:, g, :, 1, :], ALU.subtract)
                        ins = tt(v[:, g, :, 1, :], a[:, g, :, 1, :], b[:, g, :, 0, :], ALU.add)
                    link(ins)
                    dve.sem_inc(rot_ready, 1)
                elif u.name == "GA":
                    bank, free = tile(j)
                    link(ts((row_i, row_f)[t], bank[0:MH, :], pc("gate_b", t, t + 1)[0:MH, :], None, ALU.add))
                    dve.sem_inc(free, 1)
                elif u.name == "FU":
                    half_, i = u.tag
                    m = G2_HALF * half_ + i
                    col = m + (G2_TILES if t else 0)
                    bank, free = tile(j)
                    dve.wait_ge(gel_a, 2 * m + t + 1)
                    acc = tmp[:, t, :]
                    for d in range(1, FF2_CONV):
                        wt = pc("ff_conv_w", 3 * col + 2 - d, 3 * col + 3 - d)
                        link(stt(acc[:, d:SEQ], bank[:, 0:SEQ - d], wt, acc[:, d:SEQ], ALU.mult, ALU.add))
                    dve.sem_inc(free, 1)
                    if t == 0:
                        dve.sem_inc(gel_d, 2)
                    else:
                        dve.wait_ge(gel_g, m + 1)
                        link(tt(tmp[:, 2 + m % 2, :], gel[:, :], acc, ALU.mult))
                        dve.sem_inc(hid2_t, 1)
                        dve.wait_ge(hid2_hi, m + 1)
                        tt(g_lo[:, i, :], tmp[:, 2 + m % 2, :], g_hi[:, i, :], ALU.subtract).then_inc(hid2_lo, 1)
                elif u.name == "FD" and u.tag[0] == 1:
                    k = 2 * u.tag[1] + t
                    bank, free = tile(j)
                    dve.wait_ge(ysum_ready, 16)
                    link(tt(ysum[:, k, :], ysum[:, k, :], bank[:, :], ALU.add))
                    dve.sem_inc(free, 1)
                    dve.sem_inc(ysum_ready, 1)

            def add_piece(s, k, src):
                c = cs[:, s // 6, k:k + 1]
                acc = ada_acc[:, :] if s > 1 else ada_first[:, KD * s, :]
                if k == 0:
                    link(ts(acc, src, c, None, ALU.mult))
                else:
                    link(stt(acc, src, c, acc, ALU.mult, ALU.add))

            def ada_piece(p, n):
                s, k = p // 8 + 2, p % 8
                dve.wait_ge(ada_in[p % 2], 16 * (p // 2 + 1))
                add_piece(s, k, ada_raw[:, p % 2, :])
                dve.sem_inc(ada_used, 1)
                if k == 7:
                    dve.sem_inc(ada_ready, 1)

            MULS = {1: (0, "norm_mix"), 4: (1, "norm_mlp"), 7: (2, "pre_mix"), 8: (3, "post_mix"), 10: (4, "pre_ffn"), 11: (5, "post_ffn")}

            def ada_sum(s, n):
                bank, free = full(("ada_sum", s), 0)
                b = pc("b_ada" if s < 6 else "b_ada2", KD * (s % 6), KD * (s % 6 + 1))
                link(tt(mod_at(s), bank[:, 0:KD], b, ALU.add))
                dve.sem_inc(free, 1)
                if s in (1, 4, 7, 10):
                    link(stt(mul[:, MULS[s][0], :], mod_at(s), 1.0, pc(MULS[s][1]), ALU.add, ALU.mult))
                elif s in (8, 11):
                    link(tt(mul[:, MULS[s][0], :], mod_at(s), pc(MULS[s][1]), ALU.mult))
                elif s == 2:
                    link(ts(mul[:, 6, :], mod_at(s), 0.5, None, ALU.mult))
                dve.sem_inc(mod_ready, 1)

            def sumsq(item, n):
                i, pair = item
                if i in SPREAD:
                    for k in range(max(1, 2 * pair), 2 * pair + 2):
                        dve.wait_ge(norm_sq, KD * i + k + 1)
                        link(tt(rstd[:, :], rstd[:, :], tmp[:, k % 2, :], ALU.add))
                        dve.sem_inc(norm_add, 1)

            def reciprocal_root(i):
                dve.wait_ge(norm_rt, i + 1)
                link(nc.vector.reciprocal(rstd[:, :], rstd[:, :]))
                dve.sem_inc(aux_free["D"], 1)

            def norm(i, n):
                src, m_, _, kind = NORMS[i]
                a = x if src == "x" else ysum
                scale = pc("norm_final") if m_ is None else mul[:, m_, :]
                if i:
                    reciprocal_root(i)
                if kind == "x":
                    for k in range(KD):
                        stt(x[:, k, :], x[:, k, :], scale[:, k:k + 1], rstd[:, :], ALU.mult, ALU.mult).then_inc(x_ready, 1)
                elif kind == "add":
                    for k in range(KD):
                        link(stt(ysum[:, k, :], ysum[:, k, :], scale[:, k:k + 1], rstd[:, :], ALU.mult, ALU.mult))
                        tt(x[:, k, :], x[:, k, :], ysum[:, k, :], ALU.add).then_inc(x_ready, 1)
                else:
                    m = split_norms.index(i)
                    shift = mod_at(NORMS[i][2])
                    if i:
                        dve.wait_ge(*units_over(first_unit_after[i]))
                    for k in range(KD + 1):
                        if k < KD:
                            if k >= 2:
                                dve.wait_ge(norm_lo, KD * m + k - 1)
                            stt(tmp[:, 2 + k % 2, :], x[:, k, :], scale[:, k:k + 1], rstd[:, :], ALU.mult,
                                ALU.mult).then_inc(norm_tmp, 1)
                        if k:
                            dve.wait_ge(norm_hi, KD * m + k)
                            dve.wait_ge(norm_tmp, KD * m + k)
                            stt(h_lo[:, k - 1, :], tmp[:, 2 + (k - 1) % 2, :], shift[:, k - 1:k], h_hi[:, k - 1, :],
                                ALU.add, ALU.subtract).then_inc(norm_lo, 1)

            def dt_turn(i, n):
                bank, free = full(("dt_turn", 0), 0)
                link(tt(dt[:, :, :], bank[:, 0:TC * HEADS].rearrange("p (c h) -> p c h", c=TC), each(pc("dt_bias"), TC), ALU.add))
                dve.sem_inc(free, 1)
                dve.sem_inc(dt_x, 1)

            def dt_gates(i, n):
                dve.wait_ge(dt_e, 1)
                link(stt(dt[:, :, :], dt[:, :, :], 0.0, edec[:, :, :], ALU.max, ALU.add))
                stt(dta[:, :, :], dt[:, :, :], -1.0, each(cdec[:, 0, :], TC), ALU.mult, ALU.mult).then_inc(dt_s, 1)

            def dt_sums(i, n):
                bank, free = full(("dt_sums", 0), 0)
                dve.wait_ge(dt_e, 2)
                link(nc.vector.tensor_copy(acs[:, :, :].rearrange("p c h -> p (c h)"), bank[:, 0:P]))
                tt(edec[:, :, :].rearrange("p c h -> p (c h)"), bank[:, P:2 * P], acs[:, :, :].rearrange("p c h -> p (c h)"),
                   ALU.subtract).then_inc(dt_acs, 1)
                dve.wait_ge(dt_e, 3)
                link(tt(dtt[:, :, :], dt[:, :, :], edec[:, :, :], ALU.mult))
                dve.sem_inc(free, 1)
                dve.sem_inc(dt_last, 1)

            def ssd_scores(i, n):
                g, c = i
                if n:
                    full(("ssd_out", (g, c - 1) if c else (g - 1, TC - 1)), 0)
                for b in range(2):
                    bank, free = full(("ssd_scores", i), 1 + b)
                    for k in range(4):
                        hd = HG * g + 4 * b + k
                        ins = ts(decay[:, 4 * b + k, :], bank[:, chunk(k)], acs[:, c, hd:hd + 1], 0.0, ALU.subtract, ALU.min)
                    link(ins)
                    dve.sem_inc(free, 1)
                dve.sem_inc(seg, 1)
                bank, free = full(("ssd_scores", i), 0)
                link(tt(sc[:, :], bank[:, 0:P], tri, ALU.mult))
                dve.sem_inc(free, 1)
                dve.wait_ge(seg_e, n + 1)
                tt(decay[:, :, :], decay[:, :, :], each(sc[:, :], HG), ALU.mult).then_inc(mix, 1)

            def ssd_out(i, n):
                g, c = i
                heads = slice(HG * g, HG * (g + 1))

                def by_head(ap):
                    return ap.rearrange("p (h d) -> p h d", h=HG)
                bank_o, free_o = full(("ssd_out", i), 1)
                bank_s, free_s = full(("ssd_out", i), 2)
                dve.wait_ge(pre_x, n + 1)
                if c:
                    link(tt(by_head(y_part[:, :]), by_head(bank_o[:, :]), over(eacs[:, c, heads], HD), ALU.mult))
                    dve.sem_inc(free_o, 1)
                    if c < TC - 1:
                        link(tt(by_head(state[:, :]), by_head(state[:, :]), over(cdec[:, c, heads], HD), ALU.mult))
                        link(tt(state[:, :], state[:, :], bank_s[:, :], ALU.add))
                    dve.sem_inc(free_s, 1)
                    dve.sem_inc(st_ready, 1)
                    bank_d, free_d = full(("ssd_out", i), 0)
                    link(tt(y_part[:, :], y_part[:, :], bank_d[:, :], ALU.add))
                    dve.sem_inc(free_d, 1)
                    link(tt(y_part[:, :], y_part[:, :], xdt[:, 2, :], ALU.add))
                else:
                    dve.sem_inc(free_o, 1)
                    link(nc.vector.tensor_copy(state[:, :], bank_s[:, :]))
                    dve.sem_inc(free_s, 1)
                    dve.sem_inc(st_ready, 1)
                    bank_d, free_d = full(("ssd_out", i), 0)
                    link(tt(y_part[:, :], bank_d[:, :], xdt[:, 2, :], ALU.add))
                    dve.sem_inc(free_d, 1)
                dve.sem_inc(ssd_read, 1)
                link(tt(z[:, c, :], z[:, c, :], y_part[:, :], ALU.mult))
                dve.sem_inc(y_ready, 1)

            def ssd_turn(i, n):
                g, c = i
                bank, free = full(("ssd_turn", i), 0)
                if n:
                    dve.wait_ge(yt_h, n)
                link(tt(y_turned[:, :, :], bank[:, :].rearrange("p (t d) -> p t d", t=4), over(pc("ssd_norm", 4 * g, 4 * g + 4), P), ALU.mult))
                dve.sem_inc(free, 1)
                dve.sem_inc(yt_t, 1)
                dve.wait_ge(yt_h, n + 1)
                if c == 0 and g:
                    dve.wait_ge(*units_over(unit_at["Y1"][g - 1] + 1))
                link(tt(yt_lo[:, :, chunk(c)], y_turned[:, :, :], yt_hi[:, :, chunk(c)], ALU.subtract))
                dve.sem_inc(yt_l, 1)

            def window(t, n):
                w = POOL_WINDOWS[t // 2]
                if t == 0:
                    j = units[unit_at["U"][3]].job0 + 1
                    for b in range(4):
                        dve.wait_ge(main_free[(j - b) % 4], (j - b) // 4 + 1)
                else:
                    dve.wait_ge(pl_lo, t)
                u = xs_tok[:, t // 4, t % 4, :]
                src, d, slot = u, 1, 0
                while d < w:
                    dst = tmp[:, 2 + slot, :]
                    nc.vector.tensor_copy(dst[:, 0:d], src[:, 0:d])
                    link(tt(dst[:, d:SEQ], src[:, d:SEQ], src[:, 0:SEQ - d], ALU.add))
                    src, d, slot = dst, 2 * d, 1 - slot
                assert 2 + 1 - slot == win_slot(t)
                link(tt(src[:, 0:16], src[:, 0:16], cc("pool_count", 16 * (t // 2), 16 * (t // 2 + 1)), ALU.mult))
                tt(src[:, 0:16], src[:, 0:16], u[:, 0:16], ALU.subtract)
                link(stt(src[:, 16:SEQ], src[:, 16:SEQ], 1.0 / w, u[:, 16:SEQ], ALU.mult, ALU.subtract))
                dve.sem_inc(win_ready, 1)
                dve.wait_ge(pl_hi, t + 1)
                tt(p_lo[:, t, :], src, p_hi[:, t, :], ALU.subtract).then_inc(pl_lo, 1)

            def att_scores(q, n):
                g = q % 2
                ks = slice(P, 2 * P) if q < 2 else slice(0, 2 * P)
                kn = ks.stop - ks.start
                for b in range(2):
                    bank, free = full(("att_scores", q), b)
                    ins = stt(prob[:, 2 * b:2 * b + 2, ks], bank[:, :].rearrange("p (j k) -> p j k", j=2)[:, :, ks],
                              float(AD) ** -0.5, each(cc("band", ks.start, ks.stop), 2), ALU.mult, ALU.add)
                    link(ins)
                    dve.sem_inc(free, 1)
                link(nc.vector.tensor_reduce(att[:, 0:4], prob[:, :, ks], AX_X, ALU.max))
                link(tt(att[:, 4:8], att[:, 0:4], pc("sinks", 4 * g, 4 * g + 4), ALU.max))
                ts(att[:, 8:12], att[:, 4:8], -1.0, None, ALU.mult)
                tt(att[:, 16:20], pc("sinks", 4 * g, 4 * g + 4), att[:, 4:8], ALU.subtract).then_inc(sm_max, 1)

            def att_out(q, n):
                i, g = q // 2, q % 2
                dve.wait_ge(sm_exp, q + 1)
                link(tt(att[:, 20:24], att[:, 12:16], att[:, 16:20], ALU.add))
                link(nc.vector.reciprocal(att[:, 28:32], att[:, 20:24]))
                bank, free = full(("att_out", q), 0)
                o = qa[:, i, :, :].rearrange("p t d -> p (t d)")[:, 2 * P * g:2 * P * (g + 1)]
                link(tt(o.rearrange("p (j d) -> p j d", j=4), bank[:, 0:2 * P].rearrange("p (j d) -> p j d", j=4),
                        over(att[:, 28:32], AD), ALU.mult))
                dve.sem_inc(free, 1)
                dve.sem_inc(at_raw, 1)
                if g:
                    dve.wait_ge(at_rs, i + 1)
                    o = qa[:, i, :, :].rearrange("p t d -> p (t d)")
                    link(ts(o, o, att[:, 27:28], None, ALU.mult))
                    dve.sem_inc(at_out, 1)

            def ml_gates(i, n):
                scan = nc.vector.tensor_tensor_scan
                nc.vector.memset(quant[:, :], 0.0)
                nc.vector.memset(cell[:, :, :], 0.0)
                link(nc.vector.memset(row_z, 0.0))
                dve.sem_inc(mg_x, 1)
                dve.wait_ge(mg_e, 1)
                link(stt(row_f, row_f, 0.0, row_e, ALU.min, ALU.subtract))
                for c in range(TC):
                    scan(row_b[:, chunk(c)], row_f[:, chunk(c)], row_z[:, chunk(c)], 0.0, ALU.add, ALU.add)
                link(scan(row_m, row_f, row_i, 0.0, ALU.add, ALU.max))
                tt(urow[0:MH, :], row_b, row_m, ALU.subtract)
                link(tt(quant[0:MH, :], row_i, row_b, ALU.subtract))
                for c in range(TC):
                    m_prev = 0.0 if c == 0 else row_m[:, P * c - 1:P * c]
                    ts(row_t[:, chunk(c)], urow[0:MH, chunk(c)], m_prev, None, ALU.add)
                    ins = ts(row_z[:, chunk(c)], quant[0:MH, chunk(c)], urow[0:MH, P * (c + 1) - 1:P * (c + 1)], None, ALU.add)
                ins.then_inc(mg_x, 1)

            def ml_columns(i, n):
                bank, free = full(("ml_columns", 0), 0)
                link(nc.vector.tensor_copy(qcol[:, :, :].rearrange("p c t -> p (c t)"), bank[:, :]))
                dve.sem_inc(free, 1)
                bank, free = full(("ml_columns", 0), 1)
                link(nc.vector.tensor_copy(decb[:, :], bank[:, 0:MH * TC]))
                dve.sem_inc(free, 1)
                nc.vector.memset(v1[:, :, :, MD:MD + 1], 1.0).then_inc(col_ready, 1)
                dve.sem_inc(ml_cell, 1)

            def flat_tmp(a, n):
                return tmp[:, :, :].rearrange("p a b -> p (a b)")[:, a:a + n]

            W = MD + 1

            def ml_scores(c, n):
                bank_s, free_s = full(("ml_scores", c), 0)
                bank_u, free_u = full(("ml_scores", c), 1)
                for hd in range(MH):
                    ins = ts(tmp[:, 0, chunk(hd)], bank_u[:, chunk(hd)], qcol[:, c, hd:hd + 1], 0.0, ALU.add, ALU.min)
                link(ins)
                dve.sem_inc(free_u, 1)
                dve.sem_inc(ml_u, 1)
                finish_heads()
                dve.wait_ge(ml_e, c + 1)
                pp = tmp[:, 0, :].rearrange("p (h t) -> p h t", h=MH)
                link(tt(pp, pp, each(tri, MH), ALU.mult))
                link(tt(tmp[:, 0, :], tmp[:, 0, :], bank_s[:, :], ALU.mult))
                dve.sem_inc(free_s, 1)
                dve.sem_inc(ml_p, 1)
                dve.wait_ge(v_ready, TC)
                vw = flat_tmp(SEQ, MH * W).rearrange("p (h d) -> p h d", h=MH)
                tt(vw, v1[:, c, :, :], over(qcol[:, c, 64:64 + MH], W), ALU.mult).then_inc(ml_vw, 1)

            def ml_out_(c, n):
                part = flat_tmp(SEQ + MH * W, 2 * W).rearrange("p (h d) -> p h d", h=2)
                tot = flat_tmp(SEQ + MH * W + 2 * W, MH * W).rearrange("p (h d) -> p h d", h=MH)
                for b in range(2):
                    bank, free = full(("ml_out", c), b)
                    bank2, free2 = full(("ml_out", c), 2 + b)
                    link(tt(part, bank2[:, 0:2 * W].rearrange("p (h d) -> p h d", h=2),
                            over(qcol[:, c, 32 + 2 * b:34 + 2 * b], W), ALU.mult))
                    dve.sem_inc(free2, 1)
                    link(tt(tot[:, 2 * b:2 * b + 2, :], part, bank[:, 0:2 * W].rearrange("p (h d) -> p h d", h=2), ALU.add))
                    dve.sem_inc(free, 1)
                dec_c = decb[:, :].rearrange("p (h c) -> p h c", h=MH)[:, :, c]
                for b in range(2):
                    full(("ml_out", c), 4 + b)
                link(tt(cell[:, :, :], cell[:, :, :], over(dec_c, W), ALU.mult))
                for b in range(2):
                    bank, free = full(("ml_out", c), 4 + b)
                    v = cell[:, 2 * b:2 * b + 2, :]
                    link(tt(v, v, bank[:, 0:2 * W].rearrange("p (h d) -> p h d", h=2), ALU.add))
                    dve.sem_inc(free, 1)
                dve.sem_inc(ml_cell, 1)
                den = tot[:, :, MD]
                link(ts(small[:, 12:16], den, -1.0, None, ALU.mult))
                link(tt(small[:, 12:16], small[:, 12:16], den, ALU.max))
                link(tt(small[:, 12:16], small[:, 12:16], qcol[:, c, 96:96 + MH], ALU.max))
                link(nc.vector.reciprocal(small[:, 16:20], small[:, 12:16]))
                hv = hm[:, c, :].rearrange("p (h d) -> p h d", h=MH)
                link(tt(hv, tot[:, :, 0:MD], over(small[:, 16:20], MD), ALU.mult))
                link(tt(tmp[:, 0, :], hm[:, c, :], hm[:, c, :], ALU.mult))
                link(nc.vector.tensor_reduce(small[:, 0:4], tmp[:, 0, :].rearrange("p (h d) -> p h d", h=MH), AX_X, ALU.add))
                dve.sem_inc(ml_sq, 1)
                unscaled.append(c)

            unscaled = []

            def finish_heads():
                while unscaled:
                    c = unscaled.pop()
                    hv = hm[:, c, :].rearrange("p (h d) -> p h d", h=MH)
                    dve.wait_ge(ml_rs, c + 1)
                    link(tt(hv, hv, over(small[:, 8:12], MD), ALU.mult))

            def join(c, n):
                dve.wait_ge(og_t, TC)
                if c == 0:
                    finish_heads()
                    for k in range(TC):
                        stt(hm[:, k, :], og[:, k, :], 1.0, hm[:, k, :], ALU.add, ALU.mult).then_inc(ml_out, 1)
                for b in (1, 0):
                    bank, free = full(("join", c), b)
                    if c >= 2:
                        dve.wait_ge(jn_lo, 2 * (c - 1) - b)
                    col = mn_half if b == 0 else pc("attn_norm")
                    v = tmp[:, 2 * (c % 2) + b, :].rearrange("p (t d) -> p t d", t=4)
                    link(tt(v, bank[:, :].rearrange("p (t d) -> p t d", t=4), over(col, P), ALU.mult))
                    dve.sem_inc(free, 1)
                    dve.sem_inc(jn_t, 1)

            def silu_stage(i, n):
                finish_silu()

            stages = {"silu": silu_stage, "k_turn": silu_stage, "norm": norm, "sumsq": sumsq, "ada_piece": ada_piece, "ada_sum": ada_sum, "dt_turn": dt_turn, "dt_gates": dt_gates, "dt_sums": dt_sums,
                      "ssd_scores": ssd_scores, "ssd_out": ssd_out, "ssd_turn": ssd_turn, "window": window,
                      "att_scores": att_scores, "att_out": att_out, "ml_gates": ml_gates, "ml_columns": ml_columns,
                      "ml_scores": ml_scores, "ml_out": ml_out_, "join": join}
            count = {}

            def run(steps):
                for name, item in steps:
                    n = count.get(name, 0)
                    count[name] = n + 1
                    if name in stages:
                        stages[name](item, n)

            dve.wait_ge(par_in, 32)
            ts(cw_half, pc("conv_w"), 0.5, None, ALU.mult)
            ts(cb_half, pc("conv_b"), 0.5, None, ALU.mult)
            ts(mw_half, pc("ml_conv_w"), 0.5, None, ALU.mult)
            ts(mb_half, pc("ml_conv_b"), 0.5, None, ALU.mult)
            ts(mn_half, pc("ml_norm"), 0.5, None, ALU.mult)
            dve.wait_ge(cs_t, 1)
            csf = cs[:, :, :].rearrange("p a k -> p (a k)")
            link(stt(csf, cst[:, :, :].rearrange("p a k -> p (a k)"), 1.0, par[:, 0:2 * KD], ALU.add, ALU.mult))
            link(ts(csf, csf, 0.5, None, ALU.mult))
            for n, s in enumerate((1, 0)):
                for k in range(KD):
                    dve.wait_ge(first_in[k], 16 * (n + 1))
                    add_piece(s, k, ada_first[:, KD * s + k, :])
                dve.sem_inc(ada_ready, 1)
                if n == 0:
                    reciprocal_root(0)
            for n, s in enumerate((1, 0)):
                ada_sum(s, n)
            for u in units:
                run(before[u.n])
                if u.last:
                    for t in range(u.n_jobs // 2):
                        evict(u, t)
                run(mid[u.n])
                if u.last:
                    for t in range(u.n_jobs // 2, u.n_jobs):
                        evict(u, t)
                run(end[u.n])
            run(last)


def pack_weights(inputs):
    units = plan_units()
    out = np.zeros((len(units), P, SLOT), np.float32)
    for u in units:
        w = np.asarray(inputs[u.weight])[0]
        w = w.reshape(-1, w.shape[-1])
        at = 0
        view = out[u.n, :, :u.kn * u.cols].reshape(P, u.kn, u.cols)
        rows = w[P * u.k0:P * (u.k0 + u.kn)].reshape(u.kn, P, -1).transpose(1, 0, 2)
        for c0, n, pad in u.segs:
            view[:, :, at:at + n] = rows[:, :, c0:c0 + n]
            at += n + pad
    return out


def columns(v):
    return np.asarray(v).reshape(-1, P).T


def pack_params(inputs):
    out = np.zeros((P, N_PARAM), np.float32)

    def put(name, value):
        at, n = PARAM_AT[name]
        out[:, at:at + n] = value

    for name, source in (("c", "c"), ("c2", "c_2"), ("b_ada", "b_ada"), ("b_ada2", "b_ada_2"), ("norm_mix", "norm_mix_w"),
                         ("norm_mlp", "norm_mlp_w"), ("norm_final", "norm_final_w"), ("conv_b", "conv_b"),
                         ("ssd_norm", "ssd_norm_w"), ("pool_scale", "pool_scale"), ("pre_mix", "pre_mix_g_2"),
                         ("post_mix", "post_mix_g_2"), ("pre_ffn", "pre_ffn_g_2"), ("post_ffn", "post_ffn_g_2"),
                         ("ml_conv_b", "ml_conv_b_2"), ("ml_norm", "ml_norm_g_2"), ("attn_norm", "attn_norm_g_2"),
                         ("ff_conv_b", "ffn_conv_b_2")):
        put(name, columns(inputs[source]))
    for name, source in (("conv_w", "conv_w"), ("ml_conv_w", "ml_conv_w_2"), ("ff_conv_w", "ffn_conv_w_2")):
        w = np.asarray(inputs[source])[0]
        put(name, w.reshape(w.shape[0], -1, P).transpose(2, 1, 0).reshape(P, -1))
    for name, source in (("dt_bias", "dt_bias"), ("a_log", "a_log"), ("d_skip", "d_skip"), ("sinks", "attn_sinks_2")):
        put(name, np.broadcast_to(np.asarray(inputs[source]).reshape(1, -1), (P, PARAM_AT[name][1])))
    at, _ = PARAM_AT["gate_b"]
    out[0:MH, at] = np.asarray(inputs["ml_i_b_2"])[0]
    out[0:MH, at + 1] = np.asarray(inputs["ml_f_b_2"])[0]
    put("eps1", NORM_EPS)
    put("eps2", RMS_EPS)
    return out


def kernel(**inputs):
    import concourse.bacc as bacc
    from concourse.bass_utils import run_bass_kernel_spmd

    nc = bacc.Bacc("TRN2", target_bir_lowering=False, num_devices=1)
    x = np.asarray(inputs["x"])[0]
    arrays = {
        "stream": pack_weights(inputs),
        "w_ada": np.ascontiguousarray(np.asarray(inputs["w_ada"])[0]),
        "w_ada2": np.ascontiguousarray(np.asarray(inputs["w_ada_2"])[0]),
        "x_in": np.ascontiguousarray(x.T.reshape(KD, P, SEQ).transpose(1, 0, 2)),
        "params": pack_params(inputs),
        "consts": constants(),
    }
    args = [nc.dram_tensor(name, a.shape, F32, kind="ExternalInput").ap() for name, a in arrays.items()]
    out = nc.dram_tensor("out", (P, KD, SEQ), F32, kind="ExternalOutput").ap()
    build(nc, *args, out)
    r = run_bass_kernel_spmd(nc, [arrays], core_ids=[0])
    y = np.asarray(r.results[0]["out"])
    return np.ascontiguousarray(y.transpose(1, 0, 2).reshape(D_MODEL, SEQ).T)[None]
```
